# Optimizing a Trainium2 kernel written in Bass

```python
import math
import jax, jax.numpy as jnp
from jax import lax
import numpy as np

D_MODEL = 1024
BATCH = 1
SEQ = 512
DEPTH = 2

EPS = 1e-6
BLOCK = 128

MLA_HEADS = 8
MLA_Q_LORA = 256
MLA_KV_LORA = 128
MLA_NOPE = 64
MLA_ROPE = 32
MLA_V = 64
ROPE_BASE = 10000.0

DIL_HEADS = 8
DIL_HEAD_DIM = 64
DIL_PATTERNS = ((128, 1), (512, 4), (2048, 16))

SWA_Q_HEADS = 16
SWA_KV_HEADS = 2
SWA_HEAD_DIM = 64
SWA_WINDOW = 128

D_FF = -(-8 * D_MODEL // (3 * 256)) * 256

N_EVEN = (DEPTH + 1) // 2
N_ODD = DEPTH // 2

MIX_IN_A = MLA_Q_LORA + MLA_KV_LORA + MLA_ROPE
MIX_IN_B = 3 * DIL_HEADS * DIL_HEAD_DIM
MIX_IN = MIX_IN_A + MIX_IN_B
MIX_OUT = MLA_HEADS * MLA_V + DIL_HEADS * DIL_HEAD_DIM
MLA_QK = MLA_NOPE + MLA_ROPE
SWA_QKV = (SWA_Q_HEADS + 2 * SWA_KV_HEADS) * SWA_HEAD_DIM
SWA_OUT = SWA_Q_HEADS * SWA_HEAD_DIM


def _rmsnorm(x, g):
    xf = x.astype(jnp.float32)
    y = xf * lax.rsqrt(jnp.mean(xf * xf, axis=-1, keepdims=True) + EPS)
    return (y * g.astype(jnp.float32)).astype(x.dtype)

def _alibi_slopes(n):
    return jnp.exp2(-8.0 * jnp.arange(1, n + 1, dtype=jnp.float32) / n)

def _rope_tables(seq, dim):
    pos = jnp.arange(seq, dtype=jnp.float32)
    inv_freq = ROPE_BASE ** (-jnp.arange(0, dim, 2, dtype=jnp.float32) / dim)
    ang = pos[:, None] * inv_freq[None, :]
    return jnp.cos(ang), jnp.sin(ang)

def _rope(x, cos, sin):
    half = x.shape[-1] // 2
    x1, x2 = x[..., :half], x[..., half:]
    c = cos.astype(x.dtype)
    s = sin.astype(x.dtype)
    return jnp.concatenate([x1 * c - x2 * s, x2 * c + x1 * s], axis=-1)

def _to_blocks(t):
    b, s, h, d = t.shape
    return t.reshape(b, s // BLOCK, BLOCK, h, d).transpose(1, 0, 2, 3, 4)

def _from_blocks(t):
    nb, b, blk, h, d = t.shape
    return t.transpose(1, 0, 2, 3, 4).reshape(b, nb * blk, h * d)

def _mla_causal_attention(q, k, v):
    S = q.shape[1]
    nb = S // BLOCK
    scale = 1.0 / math.sqrt(q.shape[-1])
    kpos = jnp.arange(S)

    def one(args):
        qi, bi = args
        s = jnp.einsum('bqhd,bshd->bhqs', qi, k).astype(jnp.float32) * scale
        qpos = bi * BLOCK + jnp.arange(BLOCK)
        s = jnp.where((kpos[None, :] <= qpos[:, None])[None, None], s, -jnp.inf)
        p = jax.nn.softmax(s, axis=-1)
        return jnp.einsum('bhqs,bshd->bqhd', p.astype(v.dtype), v)

    out = lax.map(one, (_to_blocks(q), jnp.arange(nb)))
    return _from_blocks(out)

def _dilated_attention(q, k, v, slopes):
    S = q.shape[1]
    nb = S // BLOCK
    scale = 1.0 / math.sqrt(q.shape[-1])

    def one(args):
        qi, bi = args
        qpos = bi * BLOCK + jnp.arange(BLOCK)
        outs, lses = [], []
        for window, dil in DIL_PATTERNS:
            offs = dil * jnp.arange(window // dil + 1)
            kpos = qpos[:, None] - offs[None, :]
            valid = kpos >= 0
            idx = jnp.maximum(kpos, 0)
            kg = jnp.take(k, idx, axis=1)
            vg = jnp.take(v, idx, axis=1)
            s = jnp.einsum('bqhd,bqjhd->bhqj', qi, kg).astype(jnp.float32) * scale
            s = s - slopes[:, None, None] * offs.astype(jnp.float32)[None, None, :]
            s = jnp.where(valid[None, None], s, -jnp.inf)
            lse = jax.nn.logsumexp(s, axis=-1)
            p = jnp.exp(s - lse[..., None])
            outs.append(jnp.einsum('bhqj,bqjhd->bqhd', p.astype(v.dtype), vg))
            lses.append(lse)
        w = jax.nn.softmax(jnp.stack(lses, axis=0), axis=0)
        w = w.transpose(0, 1, 3, 2)[..., None].astype(v.dtype)
        return jnp.sum(w * jnp.stack(outs, axis=0), axis=0)

    out = lax.map(one, (_to_blocks(q), jnp.arange(nb)))
    return _from_blocks(out)

def _swa_sink_attention(q, k, v, sinks, slopes):
    B_, S, Hq, dh = q.shape
    Hkv = k.shape[2]
    G = Hq // Hkv
    nb = S // BLOCK
    scale = 1.0 / math.sqrt(dh)
    qb = q.reshape(B_, nb, BLOCK, Hkv, G, dh)

    def band(t):
        cur = t.reshape(B_, nb, BLOCK, Hkv, dh)
        prev = jnp.pad(t, ((0, 0), (BLOCK, 0), (0, 0), (0, 0)))[:, :S].reshape(B_, nb, BLOCK, Hkv, dh)
        return jnp.concatenate([prev, cur], axis=2)

    kb, vb = band(k), band(v)
    qi = jnp.arange(BLOCK)
    kj = jnp.arange(2 * BLOCK)
    dist = qi[:, None] + BLOCK - kj[None, :]
    kpos = jnp.arange(nb)[:, None] * BLOCK - BLOCK + kj[None, :]
    valid = ((dist >= 0) & (dist < SWA_WINDOW))[None] & (kpos >= 0)[:, None, :]
    s = jnp.einsum('bnqkgd,bnjkd->bnkgqj', qb, kb).astype(jnp.float32) * scale
    s = s - slopes.reshape(Hkv, G)[:, :, None, None] * dist.astype(jnp.float32)
    s = jnp.where(valid[None, :, None, None], s, -jnp.inf)
    sink = jnp.broadcast_to(sinks.astype(jnp.float32).reshape(1, 1, Hkv, G, 1, 1), s.shape[:-1] + (1,))
    p = jax.nn.softmax(jnp.concatenate([s, sink], axis=-1), axis=-1)[..., :-1]
    o = jnp.einsum('bnkgqj,bnjkd->bnqkgd', p.astype(v.dtype), vb)
    return o.reshape(B_, S, Hq * dh)

def _even_mixer(h, w_in, g_q, g_kv, w_uq, w_ukv, w_out, cos, sin, dil_slopes):
    B_, S, _ = h.shape
    proj = h @ w_in
    o1 = MLA_Q_LORA
    o2 = o1 + MLA_KV_LORA
    o3 = o2 + MLA_ROPE
    nd = DIL_HEADS * DIL_HEAD_DIM
    c_q, c_kv, k_r = proj[..., :o1], proj[..., o1:o2], proj[..., o2:o3]
    qB = proj[..., o3:o3 + nd].reshape(B_, S, DIL_HEADS, DIL_HEAD_DIM)
    kB = proj[..., o3 + nd:o3 + 2 * nd].reshape(B_, S, DIL_HEADS, DIL_HEAD_DIM)
    vB = proj[..., o3 + 2 * nd:o3 + 3 * nd].reshape(B_, S, DIL_HEADS, DIL_HEAD_DIM)
    qA = (_rmsnorm(c_q, g_q) @ w_uq).reshape(B_, S, MLA_HEADS, MLA_QK)
    q_nope, q_rope = qA[..., :MLA_NOPE], qA[..., MLA_NOPE:]
    q_rope = _rope(q_rope, cos[None, :, None, :], sin[None, :, None, :])
    kv = (_rmsnorm(c_kv, g_kv) @ w_ukv).reshape(B_, S, MLA_HEADS, MLA_NOPE + MLA_V)
    k_nope, vA = kv[..., :MLA_NOPE], kv[..., MLA_NOPE:]
    k_rope = _rope(k_r, cos[None], sin[None])
    k_rope = jnp.broadcast_to(k_rope[:, :, None, :], (B_, S, MLA_HEADS, MLA_ROPE))
    oA = _mla_causal_attention(jnp.concatenate([q_nope, q_rope], axis=-1),
                               jnp.concatenate([k_nope, k_rope], axis=-1), vA)
    oB = _dilated_attention(qB, kB, vB, dil_slopes)
    return jnp.concatenate([oA, oB], axis=-1) @ w_out

def _odd_mixer(h, w_qkv, sinks, w_out, swa_slopes):
    B_, S, _ = h.shape
    qkv = h @ w_qkv
    nq = SWA_Q_HEADS * SWA_HEAD_DIM
    nk = SWA_KV_HEADS * SWA_HEAD_DIM
    q = qkv[..., :nq].reshape(B_, S, SWA_Q_HEADS, SWA_HEAD_DIM)
    k = qkv[..., nq:nq + nk].reshape(B_, S, SWA_KV_HEADS, SWA_HEAD_DIM)
    v = qkv[..., nq + nk:].reshape(B_, S, SWA_KV_HEADS, SWA_HEAD_DIM)
    return _swa_sink_attention(q, k, v, sinks, swa_slopes) @ w_out

def _swiglu(h, w_gate_up, w_down):
    gu = h @ w_gate_up
    gate, up = gu[..., :D_FF], gu[..., D_FF:]
    return (jax.nn.silu(gate) * up) @ w_down

def first_inputs(seed: int = 0) -> dict:
    key = jax.random.key(seed)
    ks = jax.random.split(key, 16)
    f32 = jnp.float32

    def w(k, shape, fan_in):
        return jax.random.normal(k, shape, f32) * (fan_in ** -0.5)

    def gain(k, shape):
        return 1.0 + 0.05 * jax.random.normal(k, shape, f32)

    return {
        "x": jax.random.normal(ks[0], (BATCH, SEQ, D_MODEL), f32),
        "attn_norm": gain(ks[1], (DEPTH, D_MODEL)),
        "ffn_norm": gain(ks[2], (DEPTH, D_MODEL)),
        "final_norm": gain(ks[3], (D_MODEL,)),
        "e_w_in": w(ks[4], (N_EVEN, D_MODEL, MIX_IN), D_MODEL),
        "e_q_norm": gain(ks[5], (N_EVEN, MLA_Q_LORA)),
        "e_kv_norm": gain(ks[6], (N_EVEN, MLA_KV_LORA)),
        "e_w_uq": w(ks[7], (N_EVEN, MLA_Q_LORA, MLA_HEADS * MLA_QK), MLA_Q_LORA),
        "e_w_ukv": w(ks[8], (N_EVEN, MLA_KV_LORA, MLA_HEADS * (MLA_NOPE + MLA_V)), MLA_KV_LORA),
        "e_w_out": w(ks[9], (N_EVEN, MIX_OUT, D_MODEL), MIX_OUT),
        "o_w_qkv": w(ks[10], (N_ODD, D_MODEL, SWA_QKV), D_MODEL),
        "o_sinks": jax.random.normal(ks[11], (N_ODD, SWA_Q_HEADS), f32),
        "o_w_out": w(ks[12], (N_ODD, SWA_OUT, D_MODEL), SWA_OUT),
        "f_w_gate_up": w(ks[13], (DEPTH, D_MODEL, 2 * D_FF), D_MODEL),
        "f_w_down": w(ks[14], (DEPTH, D_FF, D_MODEL), D_FF),
    }

def first_block(x, attn_norm, ffn_norm, final_norm, e_w_in, e_q_norm, e_kv_norm, e_w_uq,
              e_w_ukv, e_w_out, o_w_qkv, o_sinks, o_w_out, f_w_gate_up, f_w_down):
    S = x.shape[1]
    cos, sin = _rope_tables(S, MLA_ROPE)
    dil_slopes = _alibi_slopes(DIL_HEADS)
    swa_slopes = _alibi_slopes(SWA_Q_HEADS)
    h = x
    for layer in range(DEPTH):
        i = layer // 2
        hn = _rmsnorm(h, attn_norm[layer])
        if layer % 2 == 0:
            mix = _even_mixer(hn, e_w_in[i], e_q_norm[i], e_kv_norm[i], e_w_uq[i],
                              e_w_ukv[i], e_w_out[i], cos, sin, dil_slopes)
        else:
            mix = _odd_mixer(hn, o_w_qkv[i], o_sinks[i], o_w_out[i], swa_slopes)
        h = h + mix
        h = h + _swiglu(_rmsnorm(h, ffn_norm[layer]), f_w_gate_up[layer], f_w_down[layer])
    return _rmsnorm(h, final_norm)


N_A = DEPTH // 2
N_B = DEPTH - N_A

GLA_HEADS = 4
GLA_DK = (D_MODEL // 2) // GLA_HEADS
GLA_DV = D_MODEL // GLA_HEADS
GLA_GATE_RANK = 16
GLA_TAU = 16.0
GLA_CHUNK = 64
GLA_COLS = (GLA_HEADS * GLA_DK, GLA_HEADS * GLA_DK, GLA_HEADS * GLA_DV, GLA_HEADS * GLA_DV, GLA_GATE_RANK)
GLA_SPLITS = list(np.cumsum(GLA_COLS)[:-1].tolist())
GLA_IN = int(sum(GLA_COLS))

DIFF_HEADS = 8
DIFF_DH = 64
DIFF_VD = 2 * DIFF_DH
Q_BLOCK = 128

MLP_HIDDEN = 4 * D_MODEL
NORM_EPS = 1e-6


def rms_norm(x, g):
    xf = x.astype(jnp.float32)
    y = xf * lax.rsqrt(jnp.mean(xf * xf, axis=-1, keepdims=True) + NORM_EPS)
    return (y * g.astype(jnp.float32)).astype(x.dtype)

def sqrelu_mlp(xn, w1, w2):
    return jnp.square(jax.nn.relu(xn @ w1)) @ w2

def gla_chunked(q, k, v, log_a):
    B, S, H, DK = q.shape
    DV = v.shape[-1]
    C = GLA_CHUNK
    n = S // C

    def chunks(t):
        return t.astype(jnp.float32).reshape(B, n, C, H, t.shape[-1]).transpose(1, 0, 3, 2, 4)

    qc = chunks(q) * (DK ** -0.5)
    kc = chunks(k)
    vc = chunks(v)
    bc = jnp.cumsum(chunks(log_a), axis=-2)
    causal = jnp.tril(jnp.ones((C, C), bool))

    def step(state, inp):
        qi, ki, vi, bi = inp
        diff = bi[:, :, :, None, :] - bi[:, :, None, :, :]
        decay = jnp.exp(jnp.where(causal[:, :, None], diff, -jnp.inf))
        attn = jnp.einsum('bhid,bhjd,bhijd->bhij', qi, ki, decay)
        o = (jnp.einsum('bhij,bhjv->bhiv', attn, vi)
             + jnp.einsum('bhid,bhdv->bhiv', qi * jnp.exp(bi), state))
        b_last = bi[:, :, -1:, :]
        state = (jnp.exp(b_last[:, :, 0, :, None]) * state
                 + jnp.einsum('bhjd,bhjv->bhdv', ki * jnp.exp(b_last - bi), vi))
        return state, o

    _, o = lax.scan(step, jnp.zeros((B, H, DK, DV), jnp.float32), (qc, kc, vc, bc))
    return o.transpose(1, 0, 3, 2, 4).reshape(B, S, H, DV)

def gla_mixer(xn, w_in, w_gate_up, b_gate, head_gain, w_out):
    B, S, _ = xn.shape
    proj = xn @ w_in
    q, k, v, g, z = jnp.split(proj, GLA_SPLITS, axis=-1)
    log_a = jax.nn.log_sigmoid((z @ w_gate_up + b_gate).astype(jnp.float32)) / GLA_TAU
    hk = lambda t: t.reshape(B, S, GLA_HEADS, GLA_DK)
    o = gla_chunked(hk(q), hk(k), v.reshape(B, S, GLA_HEADS, GLA_DV), hk(log_a)).astype(xn.dtype)
    o = rms_norm(o, head_gain) * jax.nn.silu(g.reshape(B, S, GLA_HEADS, GLA_DV))
    return o.reshape(B, S, GLA_HEADS * GLA_DV) @ w_out

def shared_kv(h, kv_norm, w_kv, k_norm):
    B, S, _ = h.shape
    kv = rms_norm(h, kv_norm) @ w_kv
    k, v = jnp.split(kv, [DIFF_HEADS * 2 * DIFF_DH], axis=-1)
    k = rms_norm(k.reshape(B, S, DIFF_HEADS, 2, DIFF_DH), k_norm).transpose(0, 2, 3, 1, 4)
    v = v.reshape(B, S, DIFF_HEADS, DIFF_VD).transpose(0, 2, 1, 3)
    return k, v

def diff_mixer(xn, k, v, w_q, q_gain, lam_params, head_gain, w_out, lambda_init):
    B, S, _ = xn.shape
    q = rms_norm((xn @ w_q).reshape(B, S, DIFF_HEADS, 2, DIFF_DH), q_gain) * (DIFF_DH ** -0.5)
    lp = lam_params.astype(jnp.float32)
    lam = jnp.exp(jnp.sum(lp[0] * lp[1])) - jnp.exp(jnp.sum(lp[2] * lp[3])) + lambda_init
    nq = S // Q_BLOCK
    qb = q.transpose(0, 2, 3, 1, 4).reshape(B, DIFF_HEADS, 2, nq, Q_BLOCK, DIFF_DH).transpose(3, 0, 1, 2, 4, 5)
    kpos = jnp.arange(S)

    def attend(args):
        q_blk, bi = args
        s = jnp.einsum('bhcqd,bhckd->bhcqk', q_blk, k).astype(jnp.float32)
        qpos = bi * Q_BLOCK + jnp.arange(Q_BLOCK)
        s = jnp.where(kpos[None, :] <= qpos[:, None], s, -jnp.inf)
        p = jax.nn.softmax(s, axis=-1)
        a = p[:, :, 0] - lam * p[:, :, 1]
        return jnp.einsum('bhqk,bhkv->bhqv', a.astype(v.dtype), v)

    o = lax.map(attend, (qb, jnp.arange(nq)))
    o = o.transpose(1, 0, 3, 2, 4).reshape(B, S, DIFF_HEADS, DIFF_VD)
    o = rms_norm(o, head_gain) * (1.0 - lambda_init)
    return o.reshape(B, S, DIFF_HEADS * DIFF_VD) @ w_out

def second_inputs(seed: int = 0) -> dict:
    key = jax.random.key(seed)
    ks = jax.random.split(key, 24)
    f32 = jnp.float32
    nrm = lambda k, shape, fan_in: jax.random.normal(k, shape, f32) * (fan_in ** -0.5)
    gain = lambda k, shape: 1.0 + 0.02 * jax.random.normal(k, shape, f32)
    D = D_MODEL
    return {
        "x": jax.random.normal(ks[0], (BATCH, SEQ, D), f32),
        "a_norm": gain(ks[1], (N_A, D)),
        "a_w_in": nrm(ks[2], (N_A, D, GLA_IN), D),
        "a_w_gate_up": nrm(ks[3], (N_A, GLA_GATE_RANK, GLA_HEADS * GLA_DK), GLA_GATE_RANK),
        "a_b_gate": 0.1 * jax.random.normal(ks[4], (N_A, GLA_HEADS * GLA_DK), f32),
        "a_head_norm": gain(ks[5], (N_A, GLA_DV)),
        "a_w_out": nrm(ks[6], (N_A, GLA_HEADS * GLA_DV, D), GLA_HEADS * GLA_DV),
        "kv_norm": gain(ks[7], (D,)),
        "w_kv": nrm(ks[8], (D, DIFF_HEADS * (2 * DIFF_DH + DIFF_VD)), D),
        "k_norm": gain(ks[9], (DIFF_DH,)),
        "b_norm": gain(ks[10], (N_B, D)),
        "b_w_q": nrm(ks[11], (N_B, D, DIFF_HEADS * 2 * DIFF_DH), D),
        "b_q_norm": gain(ks[12], (N_B, DIFF_DH)),
        "b_lambda": 0.1 * jax.random.normal(ks[13], (N_B, 4, DIFF_DH), f32),
        "b_head_norm": gain(ks[14], (N_B, DIFF_VD)),
        "b_w_out": nrm(ks[15], (N_B, DIFF_HEADS * DIFF_VD, D), DIFF_HEADS * DIFF_VD),
        "mlp_norm": gain(ks[16], (DEPTH, D)),
        "mlp_w1": nrm(ks[17], (DEPTH, D, MLP_HIDDEN), D),
        "mlp_w2": nrm(ks[18], (DEPTH, MLP_HIDDEN, D), MLP_HIDDEN),
    }

def second_block(x, a_norm, a_w_in, a_w_gate_up, a_b_gate, a_head_norm, a_w_out,
              kv_norm, w_kv, k_norm, b_norm, b_w_q, b_q_norm, b_lambda, b_head_norm, b_w_out,
              mlp_norm, mlp_w1, mlp_w2):
    h = x
    k_sh, v_sh = None, None
    for layer in range(DEPTH):
        if layer < N_A:
            i = layer
            h = h + gla_mixer(rms_norm(h, a_norm[i]), a_w_in[i], a_w_gate_up[i], a_b_gate[i],
                              a_head_norm[i], a_w_out[i])
        else:
            if layer == N_A:
                k_sh, v_sh = shared_kv(h, kv_norm, w_kv, k_norm)
            j = layer - N_A
            lambda_init = 0.8 - 0.6 * math.exp(-0.3 * layer)
            h = h + diff_mixer(rms_norm(h, b_norm[j]), k_sh, v_sh, b_w_q[j], b_q_norm[j],
                               b_lambda[j], b_head_norm[j], b_w_out[j], lambda_init)
        h = h + sqrelu_mlp(rms_norm(h, mlp_norm[layer]), mlp_w1[layer], mlp_w2[layer])
    return h


def setup_inputs(seed=0):
    out = dict(first_inputs(seed))
    for name, value in second_inputs(seed + 1).items():
        if name != "x":
            out[name + "_2"] = value
    return out


def reference(
    x, attn_norm, ffn_norm, final_norm, e_w_in, e_q_norm, e_kv_norm, e_w_uq, e_w_ukv, e_w_out,
    o_w_qkv, o_sinks, o_w_out, f_w_gate_up, f_w_down, a_norm_2, a_w_in_2, a_w_gate_up_2,
    a_b_gate_2, a_head_norm_2, a_w_out_2, kv_norm_2, w_kv_2, k_norm_2, b_norm_2, b_w_q_2,
    b_q_norm_2, b_lambda_2, b_head_norm_2, b_w_out_2, mlp_norm_2, mlp_w1_2, mlp_w2_2,
):
    x = first_block(
        x, attn_norm, ffn_norm, final_norm, e_w_in, e_q_norm, e_kv_norm, e_w_uq, e_w_ukv,
        e_w_out, o_w_qkv, o_sinks, o_w_out, f_w_gate_up, f_w_down,
    )
    return second_block(
        x, a_norm_2, a_w_in_2, a_w_gate_up_2, a_b_gate_2, a_head_norm_2, a_w_out_2, kv_norm_2,
        w_kv_2, k_norm_2, b_norm_2, b_w_q_2, b_q_norm_2, b_lambda_2, b_head_norm_2, b_w_out_2,
        mlp_norm_2, mlp_w1_2, mlp_w2_2,
    )


_drawn_inputs = setup_inputs


def setup_inputs(seed=0):
    import zlib

    import numpy as np

    out = dict(_drawn_inputs(seed))
    spreads = {}
    factors = {'e_q_norm': 5.362,
     'e_kv_norm': 3.152,
     'a_head_norm_2': 5.027,
     'kv_norm_2': 6.968,
     'k_norm_2': 8.0,
     'b_norm_2': 8.0,
     'b_q_norm_2': 8.0,
     'b_head_norm_2': 7.574}
    for name, (base, spread) in spreads.items():
        noise = np.random.default_rng([zlib.crc32(name.encode()), seed]).standard_normal(out[name].shape)
        drawn = base * np.exp(spread * noise) if base else spread * noise
        out[name] = __import__('jax').numpy.asarray(drawn.astype(out[name].dtype))
    for name, factor in factors.items():
        out[name] = (out[name] * factor).astype(out[name].dtype)
    return out
```

```python
from contextlib import ExitStack

import numpy as np

import concourse.bass as bass
from concourse import mybir

F32 = mybir.dt.float32
F32R = mybir.dt.float32r
U32 = mybir.dt.uint32
ACT = mybir.ActivationFunctionType
ALU = mybir.AluOpType

P = 128
TOK = 512
TB = TOK // P
D = 1024
KD = D // P
EPS = 1e-6
FF = 2816
HALF_FF = FF // 2
KF = HALF_FF // P
HID = 4096
HALF_HID = HID // 2
KH = HALF_HID // P
MASKED = -1e30
LAMBDA_INIT = 0.8 - 0.6 * float(np.exp(-0.3))
GLA_TAU = 16.0
SLOT = KD * 256
LEVELS = (64, 32, 16, 8, 4, 2, 1)

GAINS = {}
_at = 0
for _name, _n in (("attn0", 8), ("attn1", 8), ("ffn0", 8), ("ffn1", 8), ("final", 8), ("e_q", 2),
                  ("e_kv", 1), ("a", 8), ("a_head", 2), ("kv", 8), ("k", 1), ("b", 8), ("q", 1),
                  ("b_head", 1), ("mlp0", 8), ("mlp1", 8), ("b_gate", 4), ("sinks", 16)):
    GAINS[_name] = _at
    _at += _n
NGAINS = _at


class Stage:

    def __init__(self, base, iters, body, tail=()):
        self.base, self.iters, self.body, self.tail = base, iters, body, tail
        self.step = len(body)
        self.count = iters * len(body) + len(tail)
        assert iters == 1 or self.step % 2 == 0


def same(base, array, elems, n, first=0):
    if n == 1:
        return Stage(base, 1, [(array, elems, first, 0)])
    tail = [(array, elems, first + n - 1, 0)] if n % 2 else []
    return Stage(base, n // 2, [(array, elems, first, 2), (array, elems, first + 1, 2)], tail)


def turns(eng, iters, body):
    body(0)
    if iters > 1:
        with eng.Fori(1, iters) as i:
            body(i)


def each_chunk(eng, st, fn):
    def body(i):
        for u, entry in enumerate(st.body):
            fn(entry, i, st.base + st.step * i + u, (st.base + u) % 2,
               (st.base + u) // 2 + (st.step // 2) * i + 1 if st.iters > 1 else (st.base + u) // 2 + 1,
               st.step * i + u)
    turns(eng, st.iters, body)
    for u, entry in enumerate(st.tail):
        c = st.base + st.iters * st.step + u
        fn(entry, 0, c, c % 2, c // 2 + 1, c - st.base)


class Mark:

    def __init__(self, sem, base):
        self.sem, self.base = sem, base


def wait_for(eng, mark, value):
    if isinstance(mark, Mark):
        eng.wait_ge(mark.sem, value + mark.base)
    else:
        eng.wait_ge(mark, value)


def wait_past(eng, mark, value):
    if not isinstance(value, int) or value > 0:
        wait_for(eng, mark, value)


def build(nc, dram):
    with ExitStack() as ctx:
        _build(nc, dram, ctx)


def _build(nc, dram, ctx):
    chunks = 0
    ORDER = []

    def stage(make, *args):
        nonlocal chunks
        st = make(chunks, *args)
        ORDER.append(st)
        chunks += st.count
        return st

    W = dram
    st_ein = stage(same, W["w_e_in"], KD * 256, 2)
    st_mla = stage(Stage, 4, [(W["w_e_uq"], 512, 0, 1), (W["w_e_ukv"], 256, 0, 1)])
    st_dil = stage(Stage, 4, [(W["w_e_qk"], KD * 256, 0, 1), (W["w_e_v"], KD * P, 0, 1)])
    st_eout = stage(same, W["w_e_out"], KD * 256, 4)
    st_ffn = []
    for layer in range(2):
        if layer == 1:
            st_okv = stage(same, W["w_o_kv"], KD * 256, 1)
            st_swa = stage(same, W["w_o_q"], KD * P, 8)
            st_oout = stage(same, W["w_o_out"], KD * 256, 4)
        for half in range(2):
            up = stage(same, W["w_f_gu"], KD * 256, KF, (2 * layer + half) * KF)
            down = stage(same, W["w_f_dn"], KF * P, KD, (2 * layer + half) * KD)
            st_ffn.append((up, down))
    st_z = stage(same, W["w_a_z"], KD * P, 1)
    st_gla = stage(Stage, 4, [(W["w_a_qk"], KD * 256, 0, 1), (W["w_a_v"], KD * 256, 0, 1),
                              (W["w_a_g"], KD * P, 0, 2), (W["w_a_g"], KD * P, 1, 2)])
    st_aout = stage(same, W["w_a_out"], KD * 256, 4)
    st_mlp = []
    for layer in range(2):
        if layer == 1:
            st_diff = stage(Stage, 8, [(W["w_b_qk"], KD * 256, 0, 1), (W["w_b_v"], KD * P, 0, 1)])
            st_bout = stage(same, W["w_b_out"], KD * 256, 4)
        for half in range(2):
            up = stage(same, W["w_m_up"], KD * 256, KH // 2, (2 * layer + half) * KH // 2)
            down = stage(same, W["w_m_dn"], KH * P, KD, (2 * layer + half) * KD)
            st_mlp.append((up, down))

    def sb(name, shape, dt=F32):
        return ctx.enter_context(nc.sbuf_tensor(name, shape, dt))

    def sem(name):
        return ctx.enter_context(nc.semaphore(name))

    h = sb("h", [P, KD, TOK])
    xh = sb("xh", [P, KD, TOK], F32R)
    xl = sb("xl", [P, KD, TOK], F32R)
    raw = [sb(f"raw{i}", [P, SLOT]) for i in range(2)]
    wh = [sb(f"wh{i}", [P, SLOT], F32R) for i in range(2)]
    wl = [sb(f"wl{i}", [P, SLOT], F32R) for i in range(2)]
    sq = sb("sq", [P, 4, TOK])
    rstd = sb("rstd", [P, TOK])
    xf = sb("xf", [P, 2, TOK])
    gains = sb("gains", [P, NGAINS])
    ident = sb("ident", [P, P])
    ones = sb("ones", [P, P])
    blockones = sb("blockones", [P, P])
    eps = sb("eps", [P, 1])
    small = sb("small", [P, 64])

    arena_base = (nc.sbuf_base + 63) // 64 * 64

    def area(name, specs, start=arena_base):
        at, out = start, []
        for n, shape, dt in specs:
            size = int(np.prod(shape[1:])) * 4
            out.append(nc.alloc_sbuf_tensor_at(f"{name}_{n}", list(shape), dt, offset=at))
            at += (size + 63) // 64 * 64
        assert at <= nc.sbuf_usable_end, (name, at, nc.sbuf_usable_end)
        return out, at

    (oh, ol), arena_rest = area("mix", [("oh", (P, KD, TOK), F32R), ("ol", (P, KD, TOK), F32R)])
    (e_cqh, e_cql, e_ckh, e_ckl, e_q0, e_q1, e_k0, e_k1, e_v0, e_v1, e_p, e_t0, e_t1, e_causal, e_ropeq), _ = area("mla", [
         ("cqh", (P, 2, TOK), F32R), ("cql", (P, 2, TOK), F32R),
         ("ckh", (P, 1, TOK), F32R), ("ckl", (P, 1, TOK), F32R),
         ("q0", (P, 2, TOK), F32), ("q1", (P, 2, TOK), F32),
         ("k0", (P, 2, TOK), F32), ("k1", (P, 2, TOK), F32),
         ("v0", (P, TB, P), F32), ("v1", (P, TB, P), F32),
         ("p", (P, 4, TOK), F32), ("t0", (P, TB, TOK), F32), ("t1", (P, TB, TOK), F32),
         ("causal", (P, TOK), F32), ("ropeq", (P, TOK), F32)], arena_rest)
    (d_q0, d_q1, d_k0, d_k1, d_v0, d_v1, d_p, d_t0, d_t1, d_b0, d_b1), _ = area("dil", [
        ("q0", (P, TOK), F32), ("q1", (P, TOK), F32), ("k0", (P, TOK), F32), ("k1", (P, TOK), F32),
        ("v0", (P, TB, P), F32), ("v1", (P, TB, P), F32),
        ("p", (P, 4, TOK), F32), ("t0", (P, TB, TOK), F32), ("t1", (P, TB, TOK), F32),
        ("b0", (P, 2, TOK), F32), ("b1", (P, 2, TOK), F32)], arena_rest)
    (s_q0, s_q1, s_k, s_v, s_p, s_t0, s_t1, s_b0, s_b1, s_neg0, s_neg1, s_es), _ = area("swa", [
        ("q0", (P, TOK), F32), ("q1", (P, TOK), F32), ("k", (P, TOK), F32), ("v", (P, TB, P), F32),
        ("p", (P, 4, TOK), F32), ("t0", (P, TB, TOK), F32), ("t1", (P, TB, TOK), F32),
        ("b0", (P, 2, 256), F32), ("b1", (P, 2, 256), F32), ("neg0", (P, 2), F32),
        ("neg1", (P, 2), F32), ("es", (P, 8), F32)], arena_rest)
    (hidh, hidl), _ = area("ffn", [("hidh", (P, KH, TOK), F32R), ("hidl", (P, KH, TOK), F32R)])
    (g_b, g_z, g_wg, g_q, g_k, g_v, g_g, g_tmp, g_e, g_ks0, g_ks1, g_qs0, g_qs1, g_at, g_qe, g_kt,
     g_ktt, g_s, g_masks, g_reset, g_y, g_cum), _ = area("gla", [
         ("b", (P, 4, TOK), F32), ("z", (16, TOK), F32), ("wg", (16, TOK), F32),
         ("q", (P, TOK), F32), ("k", (P, TOK), F32), ("v", (P, TB, 256), F32),
         ("g", (P, 2, TOK), F32), ("tmp", (P, TOK), F32), ("e", (P, TOK), F32),
         ("ks0", (P, TOK), F32), ("ks1", (P, TOK), F32), ("qs0", (P, TOK), F32),
         ("qs1", (P, TOK), F32), ("at", (P, TOK), F32), ("qe", (P, TOK), F32),
         ("kt", (P, TOK), F32), ("ktt", (P, TOK), F32), ("s", (P, 256), F32),
         ("masks", (P, 8, P), U32), ("reset", (P, TOK), F32), ("y", (P, 2, TOK), F32),
         ("cum", (P, TOK), F32)], arena_rest)
    (f_kh, f_kl, f_o, f_q0, f_q1, f_k0, f_k1, f_v0, f_v1, f_p, f_t, f_causal, f_raw, f_lam), _ = area("diff", [
        ("kh", (P, KD, TOK), F32R), ("kl", (P, KD, TOK), F32R), ("o", (P, KD, TOK), F32),
        ("q0", (P, TOK), F32), ("q1", (P, TOK), F32), ("k0", (P, TOK), F32), ("k1", (P, TOK), F32),
        ("v0", (P, TB, P), F32), ("v1", (P, TB, P), F32), ("p", (P, 8, TOK), F32),
        ("t", (P, TB, TOK), F32), ("causal", (P, TOK), F32), ("raw", (P, 2, TOK), F32),
        ("lam", (P, 260), F32)])

    rsum, rinv, nmax, lamr = small[:, 0:8], small[:, 8:16], small[:, 16:24], small[:, 24:28]
    lam = small[:, 32:40]
    kc_tab, ks_tab = xf[:, 0, :], xf[:, 1, :]

    ps = ctx.enter_context(nc.psum_tensor("ps", [P, 8, TOK], F32))
    A0, A1, T_BANK, O_BANK = 0, 1, 6, 7
    S_BANKS = 2

    w_loaded = [sem("w_loaded0"), sem("w_loaded1")]
    w_rounded = sem("w_rounded")
    w_split = sem("w_split")
    w_used = sem("w_used")
    x_loaded = sem("x_loaded")
    const_loaded = sem("const_loaded")
    consts_made = sem("consts_made")
    out_stored = sem("out_stored")

    def sems(tag, names):
        return {n: sem(f"{tag}_{n}") for n in names.split()}

    block = ctx.enter_context(nc.Block())

    def stand_alone(ins):
        return ins.wait_op(consts_made, 2, "sem-ge")

    def mm3(pe, out, sh, sl, mh, ml, start, stop):
        pe.matmul(out, sh, mh, start=start, stop=False)
        pe.matmul(out, sh, ml, start=False, stop=False)
        return pe.matmul(out, sl, mh, start=False, stop=stop)

    def chunk_w(slot, kt, cols):
        n = kt * cols
        return (wh[slot][:, 0:n].rearrange("p (k n) -> p k n", k=kt),
                wl[slot][:, 0:n].rearrange("p (k n) -> p k n", k=kt))

    norm_sems = sems("norm", "squared summed logged rstd scaled rounded split")
    resid_sems = sems("resid", "added")
    up_sems = sems("up", "acted made rounded split")
    counted = {}

    def marks(group, adds):
        out = {}
        for name, n in adds.items():
            key = (id(group), name)
            out[name] = Mark(group[name], counted.get(key, 0))
            counted[key] = counted.get(key, 0) + n
        return out

    class Norm:
        def __init__(self, nt, src, outs):
            n = nt * max(1, len(outs))
            self.s = marks(norm_sems, dict(squared=nt, summed=nt, logged=1, rstd=1, scaled=n,
                                           rounded=nt * len(outs), split=nt * len(outs)))
            self.nt, self.src = nt, src
            self.outs, self.bank = outs, T_BANK

    def norm_act(act, N, ready):
        s = N.s
        for sm, v in ready:
            wait_for(act, sm, v)
        for t in range(N.nt):
            if t >= 4:
                wait_for(act, s["summed"], t - 3)
            act.activation(sq[:, t % 4, :], N.src(t), ACT.Square).then_inc(s["squared"].sem, 1)
        wait_for(act, s["summed"], N.nt)
        act.activation(rstd[:, :], ps[:, N.bank, :], ACT.Ln, bias=eps[:, 0:1],
                       scale=1.0 / (N.nt * P)).then_inc(s["logged"].sem, 1)
        wait_for(act, s["logged"], 1)
        act.activation(rstd[:, :], rstd[:, :], ACT.Exp, scale=-0.5).then_inc(s["rstd"].sem, 1)
        m = 0
        for high, _, _ in N.outs:
            for t in range(N.nt):
                m += 1
                wait_for(act, s["scaled"], m)
                act.activation(high[:, t, :], xf[:, (m - 1) % 2, :], ACT.Copy).then_inc(s["rounded"].sem, 1)

    def norm_dve(dve, N, ready=()):
        s = N.s
        for sm, v in ready:
            wait_for(dve, sm, v)
        wait_for(dve, s["rstd"], 1)
        if s["split"].base:
            wait_for(dve, s["split"], 0)
        todo = [(hi, lo, g, t) for hi, lo, g in N.outs for t in range(N.nt)]

        def scale(m):
            _, _, g, t = todo[m]
            if m >= 2:
                wait_for(dve, s["split"], m - 1)
            dve.scalar_tensor_tensor(out=xf[:, m % 2, :], in0=N.src(t), scalar=gains[:, g + t:g + t + 1],
                                     in1=rstd[:, :], op0=ALU.mult, op1=ALU.mult).then_inc(s["scaled"].sem, 1)

        scale(0)
        for m, (hi, lo, g, t) in enumerate(todo):
            if m + 1 < len(todo):
                scale(m + 1)
            wait_for(dve, s["rounded"], m + 1)
            dve.tensor_tensor(lo[:, t, :], xf[:, m % 2, :], hi[:, t, :].bitcast(F32),
                              ALU.subtract).then_inc(s["split"].sem, 1)

    def norm_pe(pe, N):
        s = N.s
        for t in range(N.nt):
            wait_for(pe, s["squared"], t + 1)
            pe.matmul(ps[:, N.bank, :], ones[:, :], sq[:, t % 4, :], start=(t == 0),
                      stop=(t == N.nt - 1)).then_inc(s["summed"].sem, 1)

    class Resid:
        def __init__(self, st, kt, nt, xs, ready, before=0, prev=None):
            self.st, self.kt, self.nt, self.xs, self.ready = st, kt, nt, xs, ready
            self.added = marks(resid_sems, dict(added=st.count))["added"]
            self.before, self.prev, self.read, self.per = before, prev, self.added, 1

    def banks_read(pe, X, n):
        if isinstance(n, int) and n < 2:
            if X.prev:
                wait_for(pe, X.prev.read, X.prev.per * (X.prev.st.count + n - 1))
        else:
            wait_for(pe, X.read, X.per * (n - 1))

    def resid_pe(pe, R):
        def one(entry, i, c, slot, uses, n):
            w_h, w_l = chunk_w(slot, R.kt, R.nt * P)
            pe.wait_ge(w_split, c + 1)
            banks_read(pe, R, n)
            par = slot
            for k in range(R.kt):
                if isinstance(n, int) and n == 0:
                    wait_for(pe, R.ready, max(1, k + 1 - R.before))
                for j in range(R.nt):
                    last = mm3(pe, ps[:, 2 * par + j, :], w_h[:, k, j * P:(j + 1) * P],
                               w_l[:, k, j * P:(j + 1) * P], R.xs[0][:, k, :], R.xs[1][:, k, :],
                               k == 0, k == R.kt - 1)
            last.then_inc(w_used, 1)
        each_chunk(pe, R.st, one)

    def resid_dve(dve, R):
        def one(entry, i, c, slot, uses, n):
            par = slot
            dve.wait_ge(w_used, c + 1)
            to = h[:, bass.ds(n * R.nt, R.nt), :] if not isinstance(n, int) else h[:, n * R.nt:(n + 1) * R.nt, :]
            dve.tensor_tensor(to, to, ps[:, 2 * par:2 * par + R.nt, :], ALU.add).then_inc(R.added.sem, 1)
        each_chunk(dve, R.st, one)

    class Up:
        def __init__(self, st, ready, swiglu, prev=None):
            self.st, self.ready, self.swiglu, self.prev = st, ready, swiglu, prev
            n = st.count * (1 if swiglu else 2)
            self.s = marks(up_sems, dict(acted=n, made=n, rounded=n, split=n))
            self.read, self.per = (self.s["made"], 1) if swiglu else (self.s["acted"], 2)

    def at_tile(buf, n):
        return buf[:, n, :] if isinstance(n, int) else buf[:, bass.ds(n, 1), :].rearrange("p a t -> p (a t)")

    def up_pe(pe, U):
        def one(entry, i, c, slot, uses, n):
            w_h, w_l = chunk_w(slot, KD, 256)
            par = slot
            pe.wait_ge(w_split, c + 1)
            banks_read(pe, U, n)
            for k in range(KD):
                if isinstance(n, int) and n == 0:
                    wait_for(pe, U.ready, k + 1)
                for j in range(2):
                    last = mm3(pe, ps[:, 2 * par + j, :], w_h[:, k, j * P:(j + 1) * P],
                               w_l[:, k, j * P:(j + 1) * P], xh[:, k, :], xl[:, k, :], k == 0, k == KD - 1)
            last.then_inc(w_used, 1)
        each_chunk(pe, U.st, one)

    def up_act(act, U):
        s = U.s

        def one(entry, i, c, slot, uses, n):
            par = slot
            act.wait_ge(w_used, c + 1)
            if U.swiglu:
                wait_past(act, s["made"], n - 1)
                act.activation(sq[:, par, :], ps[:, 2 * par, :], ACT.Silu).then_inc(s["acted"].sem, 1)
                wait_for(act, s["made"], n + 1)
                act.activation(at_tile(hidh, n), sq[:, 2 + par, :], ACT.Copy).then_inc(s["rounded"].sem, 1)
            else:
                for j in range(2):
                    wait_past(act, s["made"], 2 * n + j - 1)
                    act.activation(sq[:, j, :], ps[:, 2 * par + j, :], ACT.Relu).then_inc(s["acted"].sem, 1)
                for j in range(2):
                    wait_for(act, s["made"], 2 * n + j + 1)
                    act.activation(at_tile(hidh, 2 * n + j), sq[:, 2 + j, :], ACT.Copy).then_inc(s["rounded"].sem, 1)
        each_chunk(act, U.st, one)

    def up_dve(dve, U):
        s = U.s

        def one(entry, i, c, slot, uses, n):
            par = slot
            if U.swiglu:
                wait_for(dve, s["acted"], n + 1)
                wait_past(dve, s["split"], n - 1)
                dve.tensor_tensor(sq[:, 2 + par, :], sq[:, par, :], ps[:, 2 * par + 1, :],
                                  ALU.mult).then_inc(s["made"].sem, 1)
                wait_for(dve, s["rounded"], n + 1)
                dve.tensor_tensor(at_tile(hidl, n), sq[:, 2 + par, :], at_tile(hidh, n).bitcast(F32),
                                  ALU.subtract).then_inc(s["split"].sem, 1)
            else:
                for j in range(2):
                    wait_for(dve, s["acted"], 2 * n + j + 1)
                    wait_past(dve, s["split"], 2 * n + j - 1)
                    dve.tensor_tensor(sq[:, 2 + j, :], sq[:, j, :], sq[:, j, :], ALU.mult).then_inc(s["made"].sem, 1)
                for j in range(2):
                    wait_for(dve, s["rounded"], 2 * n + j + 1)
                    dve.tensor_tensor(at_tile(hidl, 2 * n + j), sq[:, 2 + j, :],
                                      at_tile(hidh, 2 * n + j).bitcast(F32), ALU.subtract).then_inc(s["split"].sem, 1)
        each_chunk(dve, U.st, one)

    hsrc = lambda t: h[:, t, :]


    lat = sems("lat", "taken roped")



    lraw = e_t0
    k_rot = e_t1

    def latents_pe(pe):
        for n in range(2):
            c = st_ein.base + n
            w_h, w_l = chunk_w(c % 2, KD, 256)
            pe.wait_ge(w_split, c + 1)
            for k in range(KD):
                if n == 0:
                    wait_for(pe, n_attn0.s["split"], k + 1)
                for bank, col in ((0, 0), (1, P)) if n == 0 else ((2, 0), (3, 64), (4, P)):
                    last = mm3(pe, ps[:, bank, :], w_h[:, k, col:col + P], w_l[:, k, col:col + P],
                               xh[:, k, :], xl[:, k, :], k == 0, k == KD - 1)
            last.then_inc(w_used, 1)

    def latents_act(act):
        act.wait_ge(w_used, st_ein.base + 1)
        for t in range(2):
            act.activation(lraw[:, t, :], ps[:, t, :], ACT.Copy).then_inc(lat["taken"], 1)
        act.wait_ge(w_used, st_ein.base + 2)
        act.activation(lraw[:, 2, :], ps[:, 2, :], ACT.Copy).then_inc(lat["taken"], 1)
        wait_for(act, n_attn0.s["split"], KD)
        act.dma_start(kc_tab, dram["rope_k"][0]).then_inc(rope_loaded, 16)
        act.dma_start(ks_tab, dram["rope_k"][1]).then_inc(rope_loaded, 16)
        act.wait_ge(lat["roped"], 3)
        for kbuf in (e_k0, e_k1):
            for hh in range(2):
                act.activation(kbuf[64:P, hh, :], k_rot[64:P, 2, :], ACT.Copy).then_inc(key_placed, 1)

    def latents_dve(dve):
        dve.wait_ge(w_used, st_ein.base + 2)
        dve.wait_ge(rope_loaded, 32)
        for t, tab in enumerate((kc_tab, ks_tab)):
            dve.tensor_tensor(k_rot[64:P, t, :], ps[64:P, 3 + t, :], tab[64:P, :],
                              ALU.mult).then_inc(lat["roped"], 1)
        dve.wait_ge(lat["roped"], 2)
        dve.tensor_tensor(k_rot[64:P, 2, :], k_rot[64:P, 0, :], k_rot[64:P, 1, :],
                          ALU.add).then_inc(lat["roped"], 1)

    rope_loaded = sem("rope_loaded")
    key_placed = sem("key_placed")

    ATT_ALL = ("q_staged k_staged v_staged scored masked exped inverted normed turned pt_copied pv_done "
           "o_rounded o_taken")
    ATT_MORE = {"mla": "", "dil": " tab_loaded0 tab_loaded1", "swa": " tab_loaded0 tab_loaded1 es",
                "diff": " raw_staged squared logged rooted"}

    class Att:
        pass

    def attention(tag, kind, st, pairs, scale, q, k, v, p, pt, tab, first_out):
        A = Att()
        A.kind, A.st, A.pairs, A.scale, A.first_out = kind, st, pairs, scale, first_out
        A.q, A.k, A.v, A.p, A.pt, A.tab = q, k, v, p, pt, tab
        A.s = sems(tag, ATT_ALL + ATT_MORE[kind])
        return A

    CAUSAL = [(0, (i + 1) * P) for i in range(TB)]
    BAND = [(max(i - 1, 0) * P, (i + 1) * P) for i in range(TB)]

    def span(A, i):
        return BAND[i] if A.kind == "swa" else CAUSAL[i]

    def heads_q(A, st, hh, i):
        if A.kind == "mla":
            return A.q[st][:, hh, i * P:(i + 1) * P]
        return A.q[st][64 * hh:64 * hh + 64, i * P:(i + 1) * P]

    def heads_k(A, st, hh, i):
        a, b = span(A, i)
        if A.kind == "mla":
            return A.k[st][:, hh, a:b]
        return A.k[st][64 * hh:64 * hh + 64, a:b]

    def table(A, st, hh, i):
        a, b = span(A, i)
        if A.kind in ("mla", "diff"):
            return A.tab[st][:, TOK - (b - a):TOK]
        full = 256 if A.kind == "swa" else TOK
        return A.tab[st][:, hh, full - (b - a):full]

    def attention_steps(eng, A, project, step):
        n = A.pairs
        project(0, 0, 0, 0)
        project(0, 0, 0, 1)

        def body(i):
            for u in range(2):
                step(2 * i + u, u, i, (2 * i + u + 1, 1 - u, i + u))
        turns(eng, n // 2 - 1, body)
        i = n // 2 - 1
        step(n - 2, 0, i, (n - 1, 1, i))
        step(n - 1, 1, i, None)

    def att_pe(pe, A, ready):
        s, kind = A.s, A.kind
        for sm, v in ready:
            wait_for(pe, sm, v)

        def proj(p, st, turn, part):
            if kind == "swa":
                if part == 1:
                    return
                c, slot = A.st.base + p, (A.st.base + st) % 2
                w_h, w_l = chunk_w(slot, KD, P)
                pe.wait_ge(w_split, c + 1)
                wait_past(pe, s["q_staged"], p)
                for k in range(KD):
                    last = mm3(pe, ps[:, A0, :], w_h[:, k, :], w_l[:, k, :], xh[:, k, :], xl[:, k, :],
                               k == 0, k == KD - 1)
                last.then_inc(w_used, 1)
                return
            c, slot = A.st.base + 2 * p + part, (A.st.base + part) % 2
            pe.wait_ge(w_split, c + 1)
            if kind == "mla" and part == 0:
                w_h, w_l = chunk_w(slot, 2, 256)
                wait_past(pe, s["v_staged"], p)
                wait_past(pe, s["k_staged"], 2 * p)
                for k in range(2):
                    for hh in range(2):
                        last = mm3(pe, ps[:, A0 + hh, :], w_h[:, k, hh * P:(hh + 1) * P],
                                   w_l[:, k, hh * P:(hh + 1) * P], e_cqh[:, k, :], e_cql[:, k, :],
                                   k == 0, k == 1)
                last.then_inc(w_used, 1)
            elif kind == "mla":
                w_h, w_l = chunk_w(slot, 1, 256)
                for hh in range(2):
                    pe.wait_ge(s["q_staged"], 2 * p + hh + 1)
                    last = mm3(pe, ps[:, A0 + hh, :], w_h[:, 0, hh * P:(hh + 1) * P],
                               w_l[:, 0, hh * P:(hh + 1) * P], e_ckh[:, 0, :], e_ckl[:, 0, :], True, True)
                    last.then_inc(keys_made, 1)
                pe.wait_ge(s["k_staged"], 2 * p + 1)
                for t in range(TB):
                    vh = w_h[:, 0, :].rearrange("p (a b) -> p a b", a=2)[:, :, 64:P]
                    vl = w_l[:, 0, :].rearrange("p (a b) -> p a b", a=2)[:, :, 64:P]
                    last = mm3(pe, ps[:, A0, t * P:(t + 1) * P], e_ckh[:, 0, t * P:(t + 1) * P],
                               e_ckl[:, 0, t * P:(t + 1) * P], vh, vl, True, True)
                last.then_inc(w_used, 1)
            elif part == 0:
                w_h, w_l = chunk_w(slot, KD, 256)
                if kind == "diff":
                    wait_past(pe, s["logged"], 2 * p)
                    kx = (f_kh, f_kl)
                else:
                    wait_past(pe, s["v_staged"], p)
                    wait_past(pe, s["k_staged"], p)
                    kx = (xh, xl)
                for k in range(KD):
                    for j, (a, b) in enumerate(((xh, xl), kx)):
                        last = mm3(pe, ps[:, A0 + j, :], w_h[:, k, j * P:(j + 1) * P],
                                   w_l[:, k, j * P:(j + 1) * P], a[:, k, :], b[:, k, :], k == 0, k == KD - 1)
                last.then_inc(w_used, 1)
            else:
                w_h, w_l = chunk_w(slot, KD, P)
                a, b = (f_kh, f_kl) if kind == "diff" else (xh, xl)
                if kind == "diff":
                    pe.wait_ge(s["raw_staged"], 2 * p + 1)
                else:
                    pe.wait_ge(s["q_staged"], p + 1)
                for t in range(TB):
                    for k in range(KD):
                        last = mm3(pe, ps[:, A0, t * P:(t + 1) * P], a[:, k, t * P:(t + 1) * P],
                                   b[:, k, t * P:(t + 1) * P], w_h[:, k, :], w_l[:, k, :], k == 0, k == KD - 1)
                last.then_inc(w_used, 1)
                if kind == "diff":
                    pe.wait_ge(s["squared"], 2 * p + 1)
                    pe.wait_ge(s["raw_staged"], 2 * p + 2)
                    pe.matmul(ps[:, A1, :], blockones[:, :], sq[:, 0, :], start=True, stop=True)\
                      .then_inc(sums_made, 1)
                    pe.wait_ge(s["squared"], 2 * p + 2)
                    pe.wait_ge(s["v_staged"], p + 1)
                    pe.matmul(ps[:, A0, :], blockones[:, :], sq[:, 1, :], start=True, stop=True)\
                      .then_inc(sums_made, 1)

        def scores(p, st, hh):
            if hh == 0:
                per = 2 if kind in ("mla", "diff") else 1
                pe.wait_ge(s["q_staged"], per * (p + 1) if kind == "mla" else p + 1)
                if kind != "swa":
                    pe.wait_ge(s["k_staged"], 2 * (p + 1) if kind == "mla" else p + 1)
                    pe.wait_ge(s["v_staged"], p + 1)
            for i in range(TB):
                a, b = span(A, i)
                u = 8 * p + 4 * hh + i
                wait_past(pe, s["masked"], u - 3)
                pe.matmul(ps[:, S_BANKS + i, 0:b - a], heads_q(A, st, hh, i), heads_k(A, st, hh, i),
                          start=True, stop=True).then_inc(s["scored"], 1)

        def turn_p(p, hh, units):
            for i in range(TB):
                a, b = span(A, i)
                u = units * p + (4 * hh if units == 8 else 0) + i
                pe.wait_ge(s["normed"], u + 1)
                wait_past(pe, s["pt_copied"], u)
                for j in range((b - a) // P):
                    last = pe.transpose(ps[:, T_BANK, j * P:(j + 1) * P],
                                        A.p[:, i, j * P:(j + 1) * P], ident[:, :])
                last.then_inc(s["turned"], 1)

        def pv(p, st, hh, units):
            pe.wait_ge(s["pt_copied"], units * p + (4 * hh + 4 if units == 8 else 4))
            if hh == 0:
                wait_past(pe, s["o_taken"], p)
            pt = A.pt[hh]
            vals = A.v[st][:, :, :]
            o = ps[:, O_BANK, :] if kind == "diff" else ps[64 * hh:64 * hh + 64, O_BANK, :]
            cols = slice(0, P) if kind == "diff" else slice(64 * hh, 64 * hh + 64)
            if kind == "swa":
                for i in range(TB):
                    a, b = span(A, i)
                    n = (b - a) // P
                    for j in range(n):
                        last = pe.matmul(o[:, i * P:(i + 1) * P], vals[:, a // P + j, cols],
                                         pt[:, j, i * P:(i + 1) * P], start=(j == 0), stop=(j == n - 1))
            else:
                for j in range(TB):
                    last = pe.matmul(o[:, j * P:TOK], vals[:, j, cols], pt[:, j, j * P:TOK],
                                     start=(j == 0), stop=(j == TB - 1))
            last.then_inc(s["pv_done"], 1)

        def step(p, st, turn, nx):
            scores(p, st, 0)
            if nx:
                proj(*nx, 0)
            if kind == "diff":
                scores(p, st, 1)
                if nx:
                    proj(*nx, 1)
                turn_p(p, 0, 4)
                pv(p, st, 0, 4)
                return
            turn_p(p, 0, 8)
            scores(p, st, 1)
            pv(p, st, 0, 8)
            if nx:
                proj(*nx, 1)
            turn_p(p, 1, 8)
            pv(p, st, 1, 8)

        attention_steps(pe, A, proj, step)

    keys_made = sem("mla_keys_made")
    sums_made = sem("diff_sums_made")

    def att_act(act, A, ready=()):
        s, kind = A.s, A.kind
        for sm, v in ready:
            wait_for(act, sm, v)

        def proj(p, st, turn, part):
            if part == 0 and kind in ("dil", "swa"):
                wait_past(act, s["masked"], 8 * (p - 1))
                src = dram["tab_dil"] if kind == "dil" else dram["tab_swa"]
                act.dma_start(A.tab[st][:, :, :], src[p].rearrange("p (a b) -> p a b", a=2))\
                   .then_inc(s[f"tab_loaded{st}"], 16)
            if kind == "swa":
                if part == 0:
                    act.wait_ge(w_used, A.st.base + p + 1)
                    act.activation(A.q[st][:, :], ps[:, A0, :], ACT.Copy).then_inc(s["q_staged"], 1)
                return
            c = A.st.base + 2 * p + part
            if kind == "mla":
                if part == 1:
                    for hh in range(2):
                        act.wait_ge(keys_made, 2 * p + hh + 1)
                        act.activation(A.k[st][0:64, hh, :], ps[0:64, A0 + hh, :], ACT.Copy)\
                           .then_inc(s["k_staged"], 1)
                    act.wait_ge(w_used, c + 1)
                    act.activation(A.v[st][:, :, :], ps[:, A0, :].rearrange("p (a b) -> p a b", a=TB),
                                   ACT.Copy).then_inc(s["v_staged"], 1)
            elif kind == "dil":
                act.wait_ge(w_used, c + 1)
                if part == 0:
                    act.activation(A.q[st][:, :], ps[:, A0, :], ACT.Copy).then_inc(s["q_staged"], 1)
                else:
                    act.activation(A.v[st][:, :, :], ps[:, A0, :].rearrange("p (a b) -> p a b", a=TB),
                                   ACT.Copy).then_inc(s["v_staged"], 1)
            else:
                if part == 0:
                    for j in range(2):
                        act.wait_ge(s["raw_staged"], 2 * p + j + 1)
                        act.activation(sq[:, j, :], f_raw[:, j, :], ACT.Square).then_inc(s["squared"], 1)
                else:
                    act.wait_ge(w_used, c + 1)
                    act.activation(A.v[st][:, :, :], ps[:, A0, :].rearrange("p (a b) -> p a b", a=TB),
                                   ACT.Copy).then_inc(s["v_staged"], 1)
                    for j in range(2):
                        act.wait_ge(sums_made, 2 * p + j + 1)
                        wait_past(act, s["k_staged" if j else "q_staged"], p)
                        act.activation(sq[:, 2 + j, :], ps[:, A1 - j, :], ACT.Ln, bias=eps[:, 0:1],
                                       scale=1.0 / 64).then_inc(s["logged"], 1)
                        act.wait_ge(s["logged"], 2 * p + j + 1)
                        act.activation(sq[:, 2 + j, :], sq[:, 2 + j, :], ACT.Exp, scale=-0.5)\
                           .then_inc(s["rooted"], 1)

        def exps(p, hh):
            for i in range(TB):
                a, b = span(A, i)
                u = 8 * p + 4 * hh + i
                row = 4 * hh + i
                slot = (4 * hh if kind == "diff" else 0) + i
                act.wait_ge(s["masked"], u + 1)
                act.activation(A.p[:, slot, 0:b - a], A.p[:, slot, 0:b - a], ACT.Exp, scale=-1.0,
                               bias=nmax[:, row:row + 1], accum_out=rsum[:, row:row + 1])\
                   .then_inc(s["exped"], 1)
            if kind == "swa":
                act.wait_ge(s["es"], 2 * (2 * p + hh) + 1)
                act.activation(s_es[:, 4 * hh:4 * hh + 4], s_es[:, 4 * hh:4 * hh + 4], ACT.Exp)\
                   .then_inc(s["exped"], 1)

        def copy_pt(p, hh, units):
            for i in range(TB):
                a, b = span(A, i)
                n = (b - a) // P
                u = units * p + (4 * hh if units == 8 else 0) + i
                act.wait_ge(s["turned"], u + 1)
                wait_past(act, s["pv_done"], (2 * p + hh - 1) if units == 8 else p)
                act.activation(A.pt[hh][:, 0:n, i * P:(i + 1) * P],
                               ps[:, T_BANK, 0:n * P].rearrange("p (a b) -> p a b", a=n), ACT.Copy)\
                   .then_inc(s["pt_copied"], 1)

        def step(p, st, turn, nx):
            if kind == "diff":
                exps(p, 0)
                if nx:
                    proj(*nx, 0)
                exps(p, 1)
                if nx:
                    proj(*nx, 1)
                copy_pt(p, 0, 4)
                act.wait_ge(s["pv_done"], p + 1)
                act.activation(at_tile(f_o, p), ps[:, O_BANK, :], ACT.Copy).then_inc(s["o_taken"], 1)
                return
            exps(p, 0)
            if nx:
                proj(*nx, 0)
            copy_pt(p, 0, 8)
            exps(p, 1)
            if nx:
                proj(*nx, 1)
            copy_pt(p, 1, 8)
            act.wait_ge(s["pv_done"], 2 * p + 2)
            act.activation(at_tile(oh, A.first_out + p), ps[:, O_BANK, :], ACT.Copy)\
               .then_inc(s["o_rounded"], 1)

        attention_steps(act, A, proj, step)

    def att_dve(dve, A, ready=()):
        s, kind = A.s, A.kind
        for sm, v in ready:
            wait_for(dve, sm, v)

        def proj(p, st, turn, part):
            if kind == "swa":
                if part == 0:
                    wait_past(dve, s["masked"], 8 * (p - 1))
                    g = GAINS["sinks"] + 2 * p
                    src = gains[:, g:g + 2] if isinstance(p, int) else gains[:, bass.ds(g, 2)]
                    dve.tensor_scalar(A.neg[st][:, :], src, -1.0, None, ALU.mult).then_inc(sinks_ready, 1)
                return
            c = A.st.base + 2 * p + part
            if kind == "mla" and part == 0:
                dve.wait_ge(w_used, c + 1)
                for hh in range(2):
                    dve.tensor_tensor(A.q[st][:, hh, :], ps[:, A0 + hh, :], e_ropeq[:, :], ALU.mult)\
                       .then_inc(s["q_staged"], 1)
            elif kind == "dil" and part == 0:
                dve.wait_ge(w_used, c + 1)
                dve.tensor_copy(A.k[st][:, :], ps[:, A1, :]).then_inc(s["k_staged"], 1)
            elif kind == "diff":
                if part == 0:
                    dve.wait_ge(w_used, c + 1)
                    for j in range(2):
                        wait_past(dve, s["k_staged" if j else "q_staged"], p)
                        wait_past(dve, s["squared"], 2 * p)
                        dve.tensor_copy(f_raw[:, j, :], ps[:, A0 + j, :]).then_inc(s["raw_staged"], 1)
                else:
                    for j, (to, g, nm) in enumerate(((A.q[st], "q", "q_staged"), (A.k[st], "k", "k_staged"))):
                        dve.wait_ge(s["rooted"], 2 * p + j + 1)
                        dve.scalar_tensor_tensor(out=to[:, :], in0=f_raw[:, j, :],
                                                 scalar=gains[:, GAINS[g]:GAINS[g] + 1],
                                                 in1=sq[:, 2 + j, :], op0=ALU.mult, op1=ALU.mult)\
                           .then_inc(s[nm], 1)

        def mask(p, st, turn, hh):
            for i in range(TB):
                a, b = span(A, i)
                u = 8 * p + 4 * hh + i
                row = 4 * hh + i
                slot = (4 * hh if kind == "diff" else 0) + i
                dve.wait_ge(s["scored"], u + 1)
                if kind in ("dil", "swa") and hh == 0 and i == 0:
                    dve.wait_ge(s[f"tab_loaded{st}"], 16 * (turn + 1))
                    if kind == "swa":
                        dve.wait_ge(sinks_ready, p + 1)
                if kind == "diff":
                    wait_past(dve, s["turned"], 4 * (p - 1) + i + 1)
                    wait_past(dve, s["normed"], 4 * p)
                else:
                    wait_past(dve, s["turned"], u - 3)
                if u_is_late(p, hh):
                    dve.wait_ge(s["exped"], exped_before(A, p, hh))
                start = A.neg[st][:, hh:hh + 1] if kind == "swa" else 3e38
                stand_alone(dve.tensor_tensor_reduce(
                    A.p[:, slot, 0:b - a], ps[:, S_BANKS + i, 0:b - a], table(A, st, hh, i), -A.scale,
                    start, ALU.add, ALU.min, nmax[:, row:row + 1])).then_inc(s["masked"], 1)
            if kind == "swa":
                dve.wait_ge(s["masked"], 8 * p + 4 * hh + 4)
                dve.tensor_scalar(s_es[:, 4 * hh:4 * hh + 4], nmax[:, 4 * hh:4 * hh + 4],
                                  A.neg[st][:, hh:hh + 1], None, ALU.subtract).then_inc(s["es"], 1)

        def u_is_late(p, hh):
            return not (isinstance(p, int) and p == 0)

        def exped_before(A, p, hh):
            per = 10 if A.kind == "swa" else 8
            return per * p + (per // 2) * hh - per // 2

        def norm(p, hh):
            per = 10 if kind == "swa" else 8
            dve.wait_ge(s["exped"], per * p + (per // 2) * (hh + 1))
            r = slice(4 * hh, 4 * hh + 4)
            if kind == "swa":
                dve.tensor_tensor(rsum[:, r], rsum[:, r], s_es[:, r], ALU.add).then_inc(s["es"], 1)
                dve.wait_ge(s["es"], 2 * (2 * p + hh) + 2)
            dve.reciprocal(rinv[:, r], rsum[:, r]).then_inc(s["inverted"], 1)
            dve.wait_ge(s["inverted"], 2 * p + hh + 1)
            for i in range(TB):
                a, b = span(A, i)
                dve.tensor_scalar(A.p[:, i, 0:b - a], A.p[:, i, 0:b - a], rinv[:, 4 * hh + i:4 * hh + i + 1],
                                  None, ALU.mult).then_inc(s["normed"], 1)

        def norm_diff(p):
            dve.wait_ge(s["exped"], 8 * p + 8)
            dve.reciprocal(rinv[:, 0:8], rsum[:, 0:8]).then_inc(s["inverted"], 1)
            dve.wait_ge(s["inverted"], 2 * p + 1)
            dve.tensor_scalar(lamr, rinv[:, 4:8], lam[:, 7:8], None, ALU.mult).then_inc(s["inverted"], 1)
            for i in range(TB):
                a, b = span(A, i)
                dve.tensor_scalar(A.p[:, i, 0:b - a], A.p[:, i, 0:b - a], rinv[:, i:i + 1], None,
                                  ALU.mult).then_inc(p_scaled, 1)
            dve.wait_ge(s["inverted"], 2 * p + 2)
            for i in range(TB):
                a, b = span(A, i)
                dve.wait_ge(p_scaled, 4 * p + i + 1)
                dve.scalar_tensor_tensor(out=A.p[:, i, 0:b - a], in0=A.p[:, 4 + i, 0:b - a],
                                         scalar=lamr[:, i:i + 1], in1=A.p[:, i, 0:b - a],
                                         op0=ALU.mult, op1=ALU.add).then_inc(s["normed"], 1)

        def step(p, st, turn, nx):
            mask(p, st, turn, 0)
            if kind == "diff":
                if nx:
                    proj(*nx, 0)
                mask(p, st, turn, 1)
                norm_diff(p)
                if nx:
                    proj(*nx, 1)
                return
            norm(p, 0)
            if nx:
                proj(*nx, 0)
            mask(p, st, turn, 1)
            norm(p, 1)
            if nx:
                proj(*nx, 1)
            dve.wait_ge(s["o_rounded"], p + 1)
            o = A.first_out + p
            dve.tensor_tensor(at_tile(ol, o), ps[:, O_BANK, :], at_tile(oh, o).bitcast(F32),
                              ALU.subtract).then_inc(s["o_taken"], 1)

        attention_steps(dve, A, proj, step)

    sinks_ready = sem("swa_sinks_ready")
    p_scaled = sem("diff_p_scaled")

    a_mla = attention("mla", "mla", st_mla, 4, 96.0 ** -0.5, (e_q0, e_q1), (e_k0, e_k1), (e_v0, e_v1),
                      e_p, (e_t0, e_t1), (e_causal, e_causal), 0)
    a_dil = attention("dil", "dil", st_dil, 4, 0.125, (d_q0, d_q1), (d_k0, d_k1), (d_v0, d_v1),
                      d_p, (d_t0, d_t1), (d_b0, d_b1), 4)
    a_swa = attention("swa", "swa", st_swa, 8, 0.125, (s_q0, s_q1), (s_k, s_k), (s_v, s_v),
                      s_p, (s_t0, s_t1), (s_b0, s_b1), 0)
    a_swa.neg = (s_neg0, s_neg1)
    kv_taken = sem("swa_kv_taken")
    kv_keys = sem("swa_kv_keys")




    def swa_kv_pe(pe):
        c = st_okv.base
        w_h, w_l = chunk_w(c % 2, KD, 256)
        pe.wait_ge(w_split, c + 1)
        for k in range(KD):
            wait_for(pe, n_attn1.s["split"], k + 1)
            last = mm3(pe, ps[:, A1, :], w_h[:, k, 0:P], w_l[:, k, 0:P], xh[:, k, :], xl[:, k, :],
                       k == 0, k == KD - 1)
        last.then_inc(kv_keys, 1)
        for t in range(TB):
            for k in range(KD):
                last = mm3(pe, ps[:, O_BANK, t * P:(t + 1) * P], xh[:, k, t * P:(t + 1) * P],
                           xl[:, k, t * P:(t + 1) * P], w_h[:, k, P:2 * P], w_l[:, k, P:2 * P],
                           k == 0, k == KD - 1)
        last.then_inc(w_used, 1)

    def swa_kv_act(act):
        act.wait_ge(kv_keys, 1)
        act.activation(s_k[:, :], ps[:, A1, :], ACT.Copy).then_inc(kv_taken, 1)
        act.wait_ge(w_used, st_okv.base + 1)
        act.activation(s_v[:, :, :], ps[:, O_BANK, :].rearrange("p (a b) -> p a b", a=TB), ACT.Copy)\
           .then_inc(kv_taken, 1)

    def final_dve(dve):
        wait_for(dve, n_fin.s["rstd"], 1)
        for t in range(KD):
            g = GAINS["final"] + t
            dve.scalar_tensor_tensor(out=h[:, t, :], in0=h[:, t, :], scalar=gains[:, g:g + 1],
                                     in1=rstd[:, :], op0=ALU.mult, op1=ALU.mult)\
               .then_inc(n_fin.s["scaled"].sem, 1)

    G = sems("gla", "tables z_taken pre_made biased absed exped1 logged lowered combined scanned "
             "q_taken k_taken v0_made v_taken g_taken cum_taken diff e ks qs products merged zeroed "
             "eb qe dlast elast kt_made kt_turned ktt_taken upd_made state out_made squared summed "
             "hlogged hrstd hy hy2 rounded split")

    def bview(x, s_):
        return x.rearrange("p (n b) -> p n b", b=2 * s_)

    def gla_gate_pe(pe):
        c = st_z.base
        w_h, w_l = chunk_w(c % 2, KD, P)
        pe.wait_ge(w_split, c + 1)
        for k in range(KD):
            wait_for(pe, n_a.s["split"], k + 1)
            last = mm3(pe, ps[:, 0, :], w_h[:, k, :], w_l[:, k, :], xh[:, k, :], xl[:, k, :],
                       k == 0, k == KD - 1)
        last.then_inc(w_used, 1)
        pe.wait_ge(G["z_taken"], 1)
        pe.wait_ge(G["tables"], 48)
        for hd in range(4):
            pe.matmul(ps[:, 4 + hd, :], g_wg[:, hd * P:(hd + 1) * P], g_z[:, :], start=True, stop=True)\
              .then_inc(G["pre_made"], 1)

    def gla_gate_act(act):
        wait_for(act, n_a.s["rstd"], 1)
        act.dma_start(g_wg[:, :], dram["a_gate_up"]).then_inc(G["tables"], 16)
        act.dma_start(g_masks[:, :, :], dram["level_masks"].rearrange("p (a b) -> p a b", a=8))\
           .then_inc(G["tables"], 16)
        act.dma_start(g_reset[:, :], dram["scan_reset"]).then_inc(G["tables"], 16)
        act.wait_ge(w_used, st_z.base + 1)
        act.activation(g_z[:, :], ps[0:16, 0, :], ACT.Copy).then_inc(G["z_taken"], 1)
        for hd in range(4):
            act.wait_ge(G["pre_made"], hd + 1)
            g = GAINS["b_gate"] + hd
            act.activation(sq[:, hd, :], ps[:, 4 + hd, :], ACT.Identity, bias=gains[:, g:g + 1])\
               .then_inc(G["biased"], 1)
        for hd in range(4):
            act.wait_ge(G["biased"], hd + 1)
            wait_past(act, G["combined"], hd)
            act.activation(g_tmp[:, :], sq[:, hd, :], ACT.Abs).then_inc(G["absed"], 1)
            act.wait_ge(G["absed"], hd + 1)
            act.activation(g_tmp[:, :], g_tmp[:, :], ACT.Exp, scale=-1.0).then_inc(G["exped1"], 1)
            act.wait_ge(G["exped1"], hd + 1)
            act.activation(g_tmp[:, :], g_tmp[:, :], ACT.Ln, bias=1.0).then_inc(G["logged"], 1)

    def gla_gate_dve(dve):
        dve.memset(g_at[:, :], 0.0).then_inc(G["zeroed"], 1)
        for buf in (g_ks0, g_ks1, g_qs0, g_qs1):
            dve.memset(buf[:, :], 0.0).then_inc(G["zeroed"], 1)
        dve.wait_ge(G["tables"], 48)
        for hd in range(4):
            dve.wait_ge(G["logged"], hd + 1)
            dve.scalar_tensor_tensor(out=sq[:, hd, :], in0=sq[:, hd, :], scalar=0.0, in1=g_tmp[:, :],
                                     op0=ALU.min, op1=ALU.subtract).then_inc(G["combined"], 1)
            dve.wait_ge(G["combined"], hd + 1)
            dve.tensor_tensor_scan(g_b[:, hd, :], g_reset[:, :], sq[:, hd, :], 0.0, ALU.mult, ALU.add)\
               .then_inc(G["scanned"], 1)

    NL = len(LEVELS) + 1
    KS, QS = (g_ks0, g_ks1), (g_qs0, g_qs1)

    def gla_pe(pe):
        def body(hd):
            c = st_gla.base + 4 * hd
            sl = [(st_gla.base + u) % 2 for u in range(4)]
            w_h, w_l = chunk_w(sl[0], KD, 256)
            pe.wait_ge(w_split, c + 1)
            wait_past(pe, G["g_taken"], 2 * hd)
            for k in range(KD):
                for j in range(2):
                    last = mm3(pe, ps[:, j, :], w_h[:, k, j * P:(j + 1) * P], w_l[:, k, j * P:(j + 1) * P],
                               xh[:, k, :], xl[:, k, :], k == 0, k == KD - 1)
            last.then_inc(w_used, 1)
            w_h, w_l = chunk_w(sl[1], KD, 256)
            pe.wait_ge(w_split, c + 2)
            for t in range(TB):
                if t % 2 == 0:
                    pe.wait_ge(G["k_taken" if t else "q_taken"], hd + 1)
                for k in range(KD):
                    last = mm3(pe, ps[:, t // 2, (t % 2) * 256:(t % 2) * 256 + 256],
                               xh[:, k, t * P:(t + 1) * P], xl[:, k, t * P:(t + 1) * P],
                               w_h[:, k, :], w_l[:, k, :], k == 0, k == KD - 1)
                if t == 1:
                    last.then_inc(G["v0_made"], 1)
            last.then_inc(w_used, 1)
            for j in range(2):
                w_h, w_l = chunk_w(sl[2 + j], KD, P)
                pe.wait_ge(w_split, c + 3 + j)
                pe.wait_ge(G["v_taken"], 2 * hd + j + 1)
                for k in range(KD):
                    last = mm3(pe, ps[:, j, :], w_h[:, k, :], w_l[:, k, :], xh[:, k, :], xl[:, k, :],
                               k == 0, k == KD - 1)
                last.then_inc(w_used, 1)
            for lv in range(NL):
                n = NL * hd + lv
                kk, qq = (KS[lv % 2], QS[lv % 2]) if lv < NL - 1 else (g_k, g_q)
                if lv < NL - 1:
                    pe.wait_ge(G["ks"], (NL - 1) * hd + lv + 1)
                    pe.wait_ge(G["qs"], (NL - 1) * hd + lv + 1)
                wait_past(pe, G["merged"], n - 1)
                for t in range(TB):
                    last = pe.matmul(ps[:, 2 + lv % 2, t * P:(t + 1) * P], kk[:, t * P:(t + 1) * P],
                                     qq[:, t * P:(t + 1) * P], start=True, stop=True)
                last.then_inc(G["products"], 1)
            pe.wait_ge(G["kt_made"], hd + 1)
            wait_past(pe, G["hlogged"], hd)
            for t in range(TB):
                last = pe.transpose(ps[:, 4, t * P:(t + 1) * P], g_kt[:, t * P:(t + 1) * P], ident[:, :])
            last.then_inc(G["kt_turned"], 1)
            pe.wait_ge(G["ktt_taken"], hd + 1)
            pe.wait_ge(G["merged"], NL * (hd + 1))
            pe.wait_ge(G["qe"], hd + 1)
            wait_past(pe, G["hy"], 2 * hd)
            for t in range(TB):
                if t > 0:
                    pe.wait_ge(G["state"], 3 * hd + t)
                for dv in range(2):
                    o = ps[:, 6 + dv, t * P:(t + 1) * P]
                    last = pe.matmul(o, g_v[:, t, dv * P:(dv + 1) * P], g_at[:, t * P:(t + 1) * P],
                                     start=True, stop=(t == 0))
                    if t > 0:
                        last = pe.matmul(o, g_s[:, dv * P:(dv + 1) * P], g_qe[:, t * P:(t + 1) * P],
                                         start=False, stop=True)
                last.then_inc(G["out_made"], 1)
                if t < TB - 1:
                    pe.matmul(ps[:, 5, 0:256], g_ktt[:, t * P:(t + 1) * P], g_v[:, t, :],
                              start=True, stop=True).then_inc(G["upd_made"], 1)
            for dv in range(2):
                pe.wait_ge(G["squared"], 2 * hd + dv + 1)
                pe.matmul(ps[:, 4, :], ones[:, :], g_y[:, dv, :], start=(dv == 0), stop=(dv == 1))\
                  .then_inc(G["summed"], 1)
        turns(pe, 4, body)

    def gla_act(act):
        def body(hd):
            c = st_gla.base + 4 * hd
            act.wait_ge(w_used, c + 1)
            wait_past(act, G["products"], NL * hd)
            wait_past(act, G["qe"], hd)
            act.activation(g_q[:, :], ps[:, 0, :], ACT.Copy, scale=float(P) ** -0.5).then_inc(G["q_taken"], 1)
            for j in range(2):
                if j == 0:
                    act.wait_ge(G["v0_made"], hd + 1)
                else:
                    act.wait_ge(w_used, c + 2)
                wait_past(act, G["out_made"], 4 * hd)
                act.activation(g_v[:, 2 * j:2 * j + 2, :],
                               ps[:, j, :].rearrange("p (a b) -> p a b", a=2), ACT.Copy)\
                   .then_inc(G["v_taken"], 1)
            for j in range(2):
                act.wait_ge(w_used, c + 3 + j)
                wait_past(act, G["hy2"], 2 * hd)
                act.activation(g_g[:, j, :], ps[:, j, :], ACT.Silu).then_inc(G["g_taken"], 1)
            for lv, s_ in enumerate(LEVELS):
                n = (NL - 1) * hd + lv
                act.wait_ge(G["diff"], n + 1)
                wait_past(act, G["qs"], n)
                wait_past(act, G["ks"], n)
                d, e = bview(g_tmp[:, :], s_), bview(g_e[:, :], s_)
                act.activation(e[:, :, 0:s_], d[:, :, 0:s_], ACT.Exp, scale=-1.0 / GLA_TAU).then_inc(G["e"], 1)
                act.activation(e[:, :, s_:2 * s_], d[:, :, s_:2 * s_], ACT.Exp, scale=1.0 / GLA_TAU)\
                   .then_inc(G["e"], 1)
            wait_past(act, G["state"], 3 * hd)
            act.wait_ge(G["cum_taken"], hd + 1)
            act.wait_ge(G["qs"], (NL - 1) * (hd + 1))
            act.activation(g_e[:, :], g_cum[:, :], ACT.Exp, scale=1.0 / GLA_TAU).then_inc(G["eb"], 1)
            act.wait_ge(G["dlast"], hd + 1)
            act.activation(g_tmp[:, :], g_tmp[:, :], ACT.Exp, scale=1.0 / GLA_TAU).then_inc(G["elast"], 1)
            act.wait_ge(G["kt_turned"], hd + 1)
            wait_past(act, G["upd_made"], 3 * hd)
            act.activation(g_ktt[:, :], ps[:, 4, :], ACT.Copy).then_inc(G["ktt_taken"], 1)
            act.wait_ge(G["out_made"], 4 * hd + 4)
            wait_past(act, G["split"], 2 * hd)
            for dv in range(2):
                act.activation(g_y[:, dv, :], ps[:, 6 + dv, :], ACT.Square).then_inc(G["squared"], 1)
            act.wait_ge(G["summed"], 2 * hd + 2)
            act.activation(rstd[:, :], ps[:, 4, :], ACT.Ln, bias=eps[:, 0:1], scale=1.0 / 256)\
               .then_inc(G["hlogged"], 1)
            act.wait_ge(G["hlogged"], hd + 1)
            act.activation(rstd[:, :], rstd[:, :], ACT.Exp, scale=-0.5).then_inc(G["hrstd"], 1)
            for dv in range(2):
                act.wait_ge(G["hy2"], 2 * hd + dv + 1)
                act.activation(at_tile(oh, 2 * hd + dv), g_y[:, dv, :], ACT.Copy).then_inc(G["rounded"], 1)
        turns(act, 4, body)

    def gla_dve(dve):
        def body(hd):
            c = st_gla.base + 4 * hd
            dve.wait_ge(w_used, c + 1)
            wait_past(dve, G["kt_made"], hd)
            wait_past(dve, G["products"], NL * hd)
            dve.tensor_copy(g_k[:, :], ps[:, 1, :]).then_inc(G["k_taken"], 1)
            if isinstance(hd, int):
                dve.wait_ge(G["scanned"], 4)
                dve.wait_ge(G["zeroed"], 5)
            wait_past(dve, G["state"], 3 * hd)
            dve.tensor_copy(g_cum[:, :], at_tile(g_b, hd)).then_inc(G["cum_taken"], 1)
            dve.wait_ge(G["cum_taken"], hd + 1)
            dve.wait_ge(G["q_taken"], hd + 1)
            dve.wait_ge(G["k_taken"], hd + 1)
            wait_past(dve, G["out_made"], 4 * hd)

            def merge(lv):
                n = NL * hd + lv
                dve.wait_ge(G["products"], n + 1)
                wait_past(dve, G["merged"], n)
                stand_alone(dve.copy_predicated(
                    g_at[:, :].rearrange("p (a b) -> p a b", a=TB),
                    g_masks[:, lv:lv + 1, :].broadcast_to([P, TB, P]),
                    ps[:, 2 + lv % 2, :].rearrange("p (a b) -> p a b", a=TB)))\
                   .then_inc(G["merged"], 1)

            for lv, s_ in enumerate(LEVELS):
                n = (NL - 1) * hd + lv
                b = bview(g_cum[:, :], s_)
                ref = b[:, :, s_ - 1:s_].broadcast_to([P, TOK // (2 * s_), 2 * s_])
                wait_past(dve, G["e"], 2 * n)
                dve.tensor_tensor(bview(g_tmp[:, :], s_), b, ref, ALU.subtract).then_inc(G["diff"], 1)
                if lv > 0:
                    merge(lv - 1)
                dve.wait_ge(G["e"], 2 * n + 2)
                if lv >= 2:
                    dve.wait_ge(G["products"], NL * hd + lv - 1)
                e = bview(g_e[:, :], s_)
                dve.tensor_tensor(bview(KS[lv % 2][:, :], s_)[:, :, 0:s_], bview(g_k[:, :], s_)[:, :, 0:s_],
                                  e[:, :, 0:s_], ALU.mult).then_inc(G["ks"], 1)
                dve.tensor_tensor(bview(QS[lv % 2][:, :], s_)[:, :, s_:2 * s_],
                                  bview(g_q[:, :], s_)[:, :, s_:2 * s_], e[:, :, s_:2 * s_],
                                  ALU.mult).then_inc(G["qs"], 1)
            b4 = g_cum[:, :].rearrange("p (a b) -> p a b", a=TB)
            last4 = b4[:, :, P - 1:P].broadcast_to([P, TB, P])
            dve.wait_ge(G["e"], 2 * (NL - 1) * (hd + 1))
            dve.tensor_tensor(g_tmp[:, :].rearrange("p (a b) -> p a b", a=TB), last4, b4, ALU.subtract)\
               .then_inc(G["dlast"], 1)
            merge(NL - 2)
            dve.wait_ge(G["eb"], hd + 1)
            dve.tensor_tensor(g_qe[:, :], g_q[:, :], g_e[:, :], ALU.mult).then_inc(G["qe"], 1)
            merge(NL - 1)
            dve.wait_ge(G["elast"], hd + 1)
            dve.tensor_tensor(g_kt[:, :], g_k[:, :], g_tmp[:, :], ALU.mult).then_inc(G["kt_made"], 1)
            for t in range(TB - 1):
                dve.wait_ge(G["upd_made"], 3 * hd + t + 1)
                if t == 0:
                    dve.tensor_copy(g_s[:, :], ps[:, 5, 0:256]).then_inc(G["state"], 1)
                else:
                    dve.wait_ge(G["out_made"], 4 * hd + t + 1)
                    dve.wait_ge(G["state"], 3 * hd + t)
                    dve.scalar_tensor_tensor(out=g_s[:, :], in0=g_s[:, :],
                                             scalar=g_e[:, t * P + P - 1:t * P + P], in1=ps[:, 5, 0:256],
                                             op0=ALU.mult, op1=ALU.add).then_inc(G["state"], 1)
            dve.wait_ge(G["hrstd"], hd + 1)
            dve.wait_ge(G["g_taken"], 2 * hd + 2)
            for dv in range(2):
                g = GAINS["a_head"] + dv
                dve.scalar_tensor_tensor(out=g_y[:, dv, :], in0=ps[:, 6 + dv, :], scalar=gains[:, g:g + 1],
                                         in1=rstd[:, :], op0=ALU.mult, op1=ALU.mult).then_inc(G["hy"], 1)
            for dv in range(2):
                dve.wait_ge(G["hy"], 2 * hd + dv + 1)
                dve.tensor_tensor(g_y[:, dv, :], g_y[:, dv, :], g_g[:, dv, :], ALU.mult).then_inc(G["hy2"], 1)
            for dv in range(2):
                dve.wait_ge(G["rounded"], 2 * hd + dv + 1)
                to = at_tile(oh, 2 * hd + dv)
                dve.tensor_tensor(at_tile(ol, 2 * hd + dv), g_y[:, dv, :], to.bitcast(F32), ALU.subtract)\
                   .then_inc(G["split"], 1)
        turns(dve, 4, body)

    a_diff = attention("diff", "diff", st_diff, 8, 0.125, (f_q0, f_q1), (f_k0, f_k1), (f_v0, f_v1),
                       f_p, (f_t, f_t), (f_causal, f_causal), 0)

    L = sems("lam", "loaded dots exped made")
    H = sems("hn", "squared summed logged rooted scaled rounded split")

    def lambda_act(act):
        wait_for(act, n_b.s["rstd"], 1)
        act.dma_start(f_lam[:, 0:256], dram["lambda_rows"]).then_inc(L["loaded"], 16)
        act.dma_start(f_causal[:, :], dram["tab_causal"]).then_inc(L["loaded"], 16)
        act.wait_ge(L["dots"], 2)
        act.activation(lam[:, 2:4], lam[:, 0:2], ACT.Exp).then_inc(L["exped"], 1)

    def lambda_dve(dve):
        dve.wait_ge(L["loaded"], 32)
        for j in range(2):
            dve.tensor_tensor_reduce(f_raw[:, j, 0:64], f_lam[:, 128 * j:128 * j + 64],
                                     f_lam[:, 128 * j + 64:128 * j + 128], 1.0, 0.0, ALU.mult, ALU.add,
                                     lam[:, j:j + 1]).then_inc(L["dots"], 1)
        dve.wait_ge(L["exped"], 1)
        dve.tensor_tensor(lam[:, 4:5], lam[:, 3:4], lam[:, 2:3], ALU.subtract).then_inc(L["made"], 1)
        dve.wait_ge(L["made"], 1)
        dve.tensor_scalar(lam[:, 7:8], lam[:, 4:5], -LAMBDA_INIT, None, ALU.add).then_inc(L["made"], 1)
        dve.tensor_scalar(lam[:, 5:6], gains[:, GAINS["b_head"]:GAINS["b_head"] + 1], 1.0 - LAMBDA_INIT,
                          None, ALU.mult).then_inc(L["made"], 1)
        dve.wait_ge(L["made"], 3)

    def headnorm_act(act):
        def square(t):
            wait_past(act, H["summed"], t - 1)
            act.activation(sq[:, t % 2, :], f_o[:, t, :], ACT.Square).then_inc(H["squared"], 1)

        act.wait_ge(a_diff.s["o_taken"], 8)
        square(0)
        for t in range(8):
            if t < 7:
                square(t + 1)
            act.wait_ge(H["summed"], t + 1)
            wait_past(act, H["scaled"], t - 1)
            act.activation(sq[:, 2 + t % 2, :], ps[:, t % 4, :], ACT.Ln, bias=eps[:, 0:1], scale=1.0 / P)\
               .then_inc(H["logged"], 1)
            act.wait_ge(H["logged"], t + 1)
            act.activation(sq[:, 2 + t % 2, :], sq[:, 2 + t % 2, :], ACT.Exp, scale=-0.5)\
               .then_inc(H["rooted"], 1)
            act.wait_ge(H["scaled"], t + 1)
            act.activation(xh[:, t, :], xf[:, t % 2, :], ACT.Copy).then_inc(H["rounded"], 1)

    def headnorm_pe(pe):
        for t in range(8):
            pe.wait_ge(H["squared"], t + 1)
            wait_past(pe, H["logged"], t - 3)
            pe.matmul(ps[:, t % 4, :], ones[:, :], sq[:, t % 2, :], start=True, stop=True)\
              .then_inc(H["summed"], 1)

    def headnorm_dve(dve):
        for t in range(8):
            dve.wait_ge(H["rooted"], t + 1)
            wait_past(dve, H["split"], t - 1)
            dve.scalar_tensor_tensor(out=xf[:, t % 2, :], in0=f_o[:, t, :], scalar=lam[:, 5:6],
                                     in1=sq[:, 2 + t % 2, :], op0=ALU.mult, op1=ALU.mult)\
               .then_inc(H["scaled"], 1)
            dve.wait_ge(H["rounded"], t + 1)
            dve.tensor_tensor(xl[:, t, :], xf[:, t % 2, :], xh[:, t, :].bitcast(F32), ALU.subtract)\
               .then_inc(H["split"], 1)



    def norm_of(*outs):
        return Norm(KD, hsrc, [(hi, lo, GAINS[g]) for hi, lo, g in outs])

    def halves(stages, ready, swiglu, kt):
        ups, downs = [], []
        for up, down in stages:
            ups.append(Up(up, ready, swiglu, prev=downs[-1] if downs else None))
            downs.append(Resid(down, kt, 1, (hidh, hidl), ups[-1].s["split"], prev=ups[-1]))
        return ups, downs

    n_ffn, n_mlp, u_ffn, r_ffn, u_mlp, r_mlp = [], [], [], [], [], []

    def add_ffn(layer):
        n_ffn.append(norm_of((xh, xl, f"ffn{layer}")))
        ups, downs = halves(st_ffn[2 * layer:2 * layer + 2], n_ffn[-1].s["split"], True, KF)
        u_ffn.extend(ups)
        r_ffn.extend(downs)

    def add_mlp(layer):
        n_mlp.append(norm_of((xh, xl, f"mlp{layer}")))
        ups, downs = halves(st_mlp[2 * layer:2 * layer + 2], n_mlp[-1].s["split"], False, KH)
        u_mlp.extend(ups)
        r_mlp.extend(downs)

    n_attn0 = norm_of((xh, xl, "attn0"))
    n_cq = Norm(2, lambda t: lraw[:, t, :], [(e_cqh, e_cql, GAINS["e_q"])])
    n_ck = Norm(1, lambda t: lraw[:, 2 + t, :], [(e_ckh, e_ckl, GAINS["e_kv"])])
    r_eout = Resid(st_eout, KD, 2, (oh, ol), a_dil.s["o_taken"], before=4)
    add_ffn(0)
    n_attn1 = norm_of((xh, xl, "attn1"))
    r_oout = Resid(st_oout, KD, 2, (oh, ol), a_swa.s["o_taken"])
    add_ffn(1)
    n_fin = Norm(KD, hsrc, [])
    n_a = norm_of((xh, xl, "a"))
    r_aout = Resid(st_aout, KD, 2, (oh, ol), G["split"])
    add_mlp(0)
    n_b = norm_of((xh, xl, "b"), (f_kh, f_kl, "kv"))
    r_bout = Resid(st_bout, KD, 2, (xh, xl), H["split"])
    add_mlp(1)

    CONSTS = 6

    @block.sync
    def _(sp):
        sp.dma_start(h[:, :, :], dram["x_t"].rearrange("p (a b) -> p a b", a=KD)).then_inc(x_loaded, 16)
        sp.dma_start(gains[:, :], dram["gains"]).then_inc(const_loaded, 16)
        sp.dma_start(ident[:, :], dram["ident"]).then_inc(const_loaded, 16)
        sp.dma_start(blockones[:, :], dram["blockones"]).then_inc(const_loaded, 16)
        sp.dma_start(e_causal[:, :], dram["tab_causal"]).then_inc(const_loaded, 16)
        sp.dma_start(e_ropeq[:, :], dram["rope_q"]).then_inc(const_loaded, 16)

        def load(entry, i, c, slot, uses, n):
            array, elems, first, step = entry
            wait_past(sp, w_split, c - 1)
            sp.dma_start(raw[slot][:, 0:elems], array[first + step * i]).then_inc(w_loaded[slot], 16)
        for st in ORDER:
            each_chunk(sp, st, load)
        wait_for(sp, r_mlp[3].added, KD)
        sp.dma_start(dram["out_t"].rearrange("p (a b) -> p a b", a=KD), h[:, :, :]).then_inc(out_stored, 16)
        sp.wait_ge(out_stored, 16)

    @block.gpsimd
    def _(pool):
        def split(entry, i, c, slot, uses, n):
            elems = entry[1]
            pool.wait_ge(w_loaded[slot], 16 * uses)
            wait_past(pool, w_used, c - 1)
            stand_alone(pool.tensor_scalar(wh[slot][:, 0:elems], raw[slot][:, 0:elems], 1.0, 1.0,
                                           ALU.mult, ALU.mult))\
                .then_inc(w_rounded, 1)
            pool.wait_ge(w_rounded, c + 1)
            pool.tensor_tensor(wl[slot][:, 0:elems], raw[slot][:, 0:elems],
                               wh[slot][:, 0:elems].bitcast(F32), ALU.subtract).then_inc(w_split, 1)
        for st in ORDER:
            each_chunk(pool, st, split)

    @block.tensor
    def _(pe):
        pe.wait_ge(consts_made, 2)
        pe.wait_ge(const_loaded, 80)
        norm_pe(pe, n_attn0)
        latents_pe(pe)
        norm_pe(pe, n_cq)
        norm_pe(pe, n_ck)
        att_pe(pe, a_mla, [(n_cq.s["split"], 2), (n_ck.s["split"], 1), (key_placed, 4)])
        att_pe(pe, a_dil, [])
        resid_pe(pe, r_eout)
        for layer in range(2):
            if layer == 1:
                norm_pe(pe, n_attn1)
                swa_kv_pe(pe)
                att_pe(pe, a_swa, [(kv_taken, 2)])
                resid_pe(pe, r_oout)
            norm_pe(pe, n_ffn[layer])
            for half in range(2):
                up_pe(pe, u_ffn[2 * layer + half])
                resid_pe(pe, r_ffn[2 * layer + half])
        norm_pe(pe, n_fin)
        norm_pe(pe, n_a)
        gla_gate_pe(pe)
        gla_pe(pe)
        resid_pe(pe, r_aout)
        for layer in range(2):
            if layer == 1:
                norm_pe(pe, n_b)
                att_pe(pe, a_diff, [(n_b.s["split"], 2 * KD)])
                headnorm_pe(pe)
                resid_pe(pe, r_bout)
            norm_pe(pe, n_mlp[layer])
            for half in range(2):
                up_pe(pe, u_mlp[2 * layer + half])
                resid_pe(pe, r_mlp[2 * layer + half])

    @block.scalar
    def _(act):
        act.wait_ge(consts_made, 2)
        act.wait_ge(const_loaded, 80)
        norm_act(act, n_attn0, [(x_loaded, 16)])
        latents_act(act)
        norm_act(act, n_cq, [(lat["taken"], 3)])
        norm_act(act, n_ck, [])
        att_act(act, a_mla)
        att_act(act, a_dil)
        for layer in range(2):
            if layer == 1:
                norm_act(act, n_attn1, [(r_ffn[1].added, KD)])
                swa_kv_act(act)
                att_act(act, a_swa)
            norm_act(act, n_ffn[layer], [((r_eout, r_oout)[layer].added, 4)])
            for half in range(2):
                up_act(act, u_ffn[2 * layer + half])
        norm_act(act, n_fin, [(r_ffn[3].added, KD)])
        norm_act(act, n_a, [(n_fin.s["scaled"], KD)])
        gla_gate_act(act)
        gla_act(act)
        for layer in range(2):
            if layer == 1:
                norm_act(act, n_b, [(r_mlp[1].added, KD)])
                lambda_act(act)
                att_act(act, a_diff)
                headnorm_act(act)
            norm_act(act, n_mlp[layer], [((r_aout, r_bout)[layer].added, 4)])
            for half in range(2):
                up_act(act, u_mlp[2 * layer + half])

    @block.vector
    def _(dve):
        dve.memset(ones[:, :], 1.0).then_inc(consts_made, 1)
        dve.memset(eps[:, :], EPS).then_inc(consts_made, 1)
        dve.wait_ge(const_loaded, 80)
        norm_dve(dve, n_attn0)
        latents_dve(dve)
        norm_dve(dve, n_cq)
        norm_dve(dve, n_ck)
        att_dve(dve, a_mla)
        att_dve(dve, a_dil)
        resid_dve(dve, r_eout)
        for layer in range(2):
            if layer == 1:
                norm_dve(dve, n_attn1)
                att_dve(dve, a_swa)
                resid_dve(dve, r_oout)
            norm_dve(dve, n_ffn[layer])
            for half in range(2):
                up_dve(dve, u_ffn[2 * layer + half])
                resid_dve(dve, r_ffn[2 * layer + half])
        final_dve(dve)
        norm_dve(dve, n_a)
        gla_gate_dve(dve)
        gla_dve(dve)
        resid_dve(dve, r_aout)
        for layer in range(2):
            if layer == 1:
                norm_dve(dve, n_b)
                lambda_dve(dve)
                att_dve(dve, a_diff)
                headnorm_dve(dve)
                resid_dve(dve, r_bout)
            norm_dve(dve, n_mlp[layer])
            for half in range(2):
                up_dve(dve, u_mlp[2 * layer + half])
                resid_dve(dve, r_mlp[2 * layer + half])


def panels(w, column_lists):
    out = []
    for cols in column_lists:
        part = w[:, cols]
        out.append(part.reshape(part.shape[0] // P, P, -1).transpose(1, 0, 2).reshape(P, -1))
    return np.ascontiguousarray(np.stack(out))


def shape_constants():
    f = np.float32
    pos = np.arange(TOK, dtype=f)
    inv = f(10000.0) ** (-np.arange(0, 32, 2, dtype=f) / f(32))
    ang = (pos[:, None] * inv[None, :]).astype(f)
    cos, sin = np.cos(ang).T.astype(f), np.sin(ang).T.astype(f)
    c32, s32 = np.concatenate([cos, cos]), np.concatenate([-sin, sin])
    rope_q = np.concatenate([np.ones((64, TOK), f), c32, s32])
    pad = np.zeros((64, TOK), f)
    rope_k = np.stack([np.concatenate([pad, c32, c32]), np.concatenate([pad, s32, s32])])
    q = np.arange(P)[:, None]
    off = q + TOK - P - np.arange(TOK)[None, :]
    causal = np.where(off >= 0, 0.0, MASKED).astype(f)
    count = (off <= 128).astype(int) + (off % 4 == 0) + (off % 16 == 0)
    logs = np.where((off >= 0) & (count > 0), np.log(np.maximum(count, 1)), 0.0)
    valid = (off >= 0) & (count > 0)
    dil = []
    for hd in range(8):
        slope = 2.0 ** (-(hd + 1))
        dil.append(np.where(valid, (logs - slope * off) * 8.0, MASKED))
    dil = np.stack(dil).reshape(4, 2, P, TOK).transpose(0, 2, 1, 3).reshape(4, P, 2 * TOK).astype(f)
    dist = q + P - np.arange(2 * P)[None, :]
    ok = (dist >= 0) & (dist < 128)
    swa = []
    for pair in range(8):
        for hd in (pair, pair + 8):
            swa.append(np.where(ok, -(2.0 ** (-8.0 * (hd + 1) / 16)) * dist * 8.0, MASKED))
    swa = np.stack(swa).reshape(8, 2, P, 2 * P).transpose(0, 2, 1, 3).reshape(8, P, 4 * P).astype(f)
    j, i = np.arange(P)[:, None], np.arange(P)[None, :]
    masks = [(j // (2 * s) == i // (2 * s)) & (j % (2 * s) < s) & (i % (2 * s) >= s) for s in LEVELS]
    masks.append(j == i)
    masks = np.stack(masks, 1).reshape(P, -1).astype(np.uint32)
    reset = np.ones((P, TOK), f)
    reset[:, ::P] = 0.0
    blocks = np.zeros((P, P), f)
    blocks[:64, :64] = 1.0
    blocks[64:, 64:] = 1.0
    return {"rope_q": rope_q, "rope_k": rope_k, "tab_causal": causal, "tab_dil": dil, "tab_swa": swa,
            "level_masks": masks, "scan_reset": reset, "ident": np.eye(P, dtype=f), "blockones": blocks}


def lay_out(v):
    a = {k: np.asarray(x) for k, x in v.items()}
    r = np.arange
    arrays = dict(shape_constants())
    arrays["x_t"] = np.ascontiguousarray(a["x"][0].T.reshape(KD, P, TOK).transpose(1, 0, 2).reshape(P, -1))

    w = a["e_w_in"][0]
    kr = r(384, 416)
    krs = np.concatenate([r(400, 416), r(384, 400)])
    arrays["w_e_in"] = panels(w, [r(256), np.concatenate([r(256, 384), kr, kr, krs, krs])])
    cols = []
    for pr in range(4):
        for hd in (2 * pr, 2 * pr + 1):
            b = hd * 96
            cols.append(np.concatenate([r(b, b + 96), r(b + 80, b + 96), r(b + 64, b + 80)]))
    arrays["w_e_uq"] = panels(a["e_w_uq"][0], [np.concatenate(cols[2 * i:2 * i + 2]) for i in range(4)])
    arrays["w_e_ukv"] = panels(a["e_w_ukv"][0], [r(256 * i, 256 * i + 256) for i in range(4)])
    q0, k0, v0 = 416, 416 + 512, 416 + 1024
    arrays["w_e_qk"] = panels(w, [np.concatenate([r(q0 + P * i, q0 + P * i + P), r(k0 + P * i, k0 + P * i + P)])
                                  for i in range(4)])
    arrays["w_e_v"] = panels(w, [r(v0 + P * i, v0 + P * i + P) for i in range(4)])

    def wide(m):
        return panels(m, [r(256 * i, 256 * i + 256) for i in range(m.shape[1] // 256)])
    arrays["w_e_out"] = wide(a["e_w_out"][0])
    gu, dn = [], []
    for layer in range(2):
        for half in range(2):
            s = half * HALF_FF
            gu.append(panels(a["f_w_gate_up"][layer],
                             [np.concatenate([r(s + P * i, s + P * i + P), r(FF + s + P * i, FF + s + P * i + P)])
                              for i in range(KF)]))
            dn.append(panels(a["f_w_down"][layer][s:s + HALF_FF], [r(P * i, P * i + P) for i in range(KD)]))
    arrays["w_f_gu"], arrays["w_f_dn"] = np.concatenate(gu), np.concatenate(dn)
    wo = a["o_w_qkv"][0]
    arrays["w_o_kv"] = panels(wo, [r(1024, 1280)])
    pair_cols = [np.concatenate([r(64 * i, 64 * i + 64), r(64 * (i + 8), 64 * (i + 8) + 64)]) for i in range(8)]
    arrays["w_o_q"] = panels(wo, pair_cols)
    arrays["w_o_out"] = wide(a["o_w_out"][0][np.concatenate(pair_cols)])
    wa = a["a_w_in_2"][0]
    z = np.zeros((D, P), np.float32)
    z[:, 0:16] = wa[:, 3072:3088]
    arrays["w_a_z"] = panels(z, [r(P)])
    arrays["w_a_qk"] = panels(wa, [np.concatenate([r(P * i, P * i + P), r(512 + P * i, 512 + P * i + P)])
                                   for i in range(4)])
    arrays["w_a_v"] = panels(wa, [r(1024 + 256 * i, 1280 + 256 * i) for i in range(4)])
    arrays["w_a_g"] = panels(wa, [r(2048 + P * i, 2048 + P * i + P) for i in range(8)])
    arrays["a_gate_up"] = np.ascontiguousarray(a["a_w_gate_up_2"][0])
    arrays["w_a_out"] = wide(a["a_w_out_2"][0])
    up, dn = [], []
    for layer in range(2):
        for half in range(2):
            s = half * HALF_HID
            up.append(wide(a["mlp_w1_2"][layer][:, s:s + HALF_HID]))
            dn.append(panels(a["mlp_w2_2"][layer][s:s + HALF_HID], [r(P * i, P * i + P) for i in range(KD)]))
    arrays["w_m_up"], arrays["w_m_dn"] = np.concatenate(up), np.concatenate(dn)
    both = np.concatenate([a["b_w_q_2"][0], a["w_kv_2"]], axis=1)
    arrays["w_b_qk"] = panels(both, [np.concatenate([r(P * i, P * i + P), r(1024 + P * i, 1024 + P * i + P)])
                                     for i in range(8)])
    arrays["w_b_v"] = panels(both, [r(2048 + P * i, 2048 + P * i + P) for i in range(8)])
    arrays["w_b_out"] = wide(a["b_w_out_2"][0])

    def tiles(vec):
        return vec.reshape(-1, P).T

    def twice(vec):
        return np.concatenate([vec, vec])[:, None]
    sinks = a["o_sinks"][0][np.stack([r(8), r(8) + 8], 1).reshape(-1)]
    parts = {
        "attn0": tiles(a["attn_norm"][0]), "attn1": tiles(a["attn_norm"][1]),
        "ffn0": tiles(a["ffn_norm"][0]), "ffn1": tiles(a["ffn_norm"][1]), "final": tiles(a["final_norm"]),
        "e_q": tiles(a["e_q_norm"][0]), "e_kv": tiles(a["e_kv_norm"][0]), "a": tiles(a["a_norm_2"][0]),
        "a_head": tiles(a["a_head_norm_2"][0]), "kv": tiles(a["kv_norm_2"]), "k": twice(a["k_norm_2"]),
        "b": tiles(a["b_norm_2"][0]), "q": twice(a["b_q_norm_2"][0]), "b_head": tiles(a["b_head_norm_2"][0]),
        "mlp0": tiles(a["mlp_norm_2"][0]), "mlp1": tiles(a["mlp_norm_2"][1]), "b_gate": tiles(a["a_b_gate_2"][0]),
        "sinks": np.broadcast_to(sinks[None, :], (P, 16)),
    }
    arrays["gains"] = np.ascontiguousarray(np.concatenate([parts[n] for n in GAINS], axis=1))
    arrays["lambda_rows"] = np.ascontiguousarray(np.broadcast_to(a["b_lambda_2"][0].reshape(1, -1), (P, 256)))
    return arrays


def kernel(**inputs):
    import concourse.bacc as bacc
    from concourse.bass_utils import run_bass_kernel_spmd

    arrays = lay_out(inputs)
    nc = bacc.Bacc("TRN2", target_bir_lowering=False, num_devices=1)
    dram = {n: nc.dram_tensor("in_" + n, list(x.shape), mybir.dt.from_np(x.dtype), kind="ExternalInput").ap()
            for n, x in arrays.items()}
    dram["out_t"] = nc.dram_tensor("out_t", [P, KD * TOK], F32, kind="ExternalOutput").ap()
    build(nc, dram)
    got = run_bass_kernel_spmd(nc, [{"in_" + n: x for n, x in arrays.items()}], core_ids=[0]).results[0]["out_t"]
    return np.ascontiguousarray(got.reshape(P, KD, TOK).transpose(1, 0, 2).reshape(D, TOK).T)[None]
```

```python
from contextlib import ExitStack

import numpy as np

import concourse.bass as bass
from concourse import mybir

F32 = mybir.dt.float32
F32R = mybir.dt.float32r
U32 = mybir.dt.uint32
ACT = mybir.ActivationFunctionType
ALU = mybir.AluOpType

P = 128
TOK = 512
TB = TOK // P
D = 1024
KD = D // P
EPS = 1e-6
FF = 2816
HALF_FF = FF // 2
KF = HALF_FF // P
HID = 4096
HALF_HID = HID // 2
KH = HALF_HID // P
MASKED = -1e30
LAMBDA_INIT = 0.8 - 0.6 * float(np.exp(-0.3))
GLA_TAU = 16.0
SLOT = KD * 256
LEVELS = (64, 32, 16, 8, 4, 2, 1)

GAINS = {}
_at = 0
for _name, _n in (("attn0", 8), ("attn1", 8), ("ffn0", 8), ("ffn1", 8), ("final", 8), ("e_q", 2),
                  ("e_kv", 1), ("a", 8), ("a_head", 2), ("kv", 8), ("k", 1), ("b", 8), ("q", 1),
                  ("b_head", 1), ("mlp0", 8), ("mlp1", 8), ("b_gate", 4), ("sinks", 16)):
    GAINS[_name] = _at
    _at += _n
NGAINS = _at


class Stage:

    def __init__(self, base, iters, body, tail=()):
        self.base, self.iters, self.body, self.tail = base, iters, body, tail
        self.step = len(body)
        self.count = iters * len(body) + len(tail)
        assert iters == 1 or self.step % 2 == 0


def same(base, array, elems, n, first=0):
    if n == 1:
        return Stage(base, 1, [(array, elems, first, 0)])
    tail = [(array, elems, first + n - 1, 0)] if n % 2 else []
    return Stage(base, n // 2, [(array, elems, first, 2), (array, elems, first + 1, 2)], tail)


def turns(eng, iters, body):
    body(0)
    if iters > 1:
        with eng.Fori(1, iters) as i:
            body(i)


def each_chunk(eng, st, fn):
    def body(i):
        for u, entry in enumerate(st.body):
            fn(entry, i, st.base + st.step * i + u, (st.base + u) % 2,
               (st.base + u) // 2 + (st.step // 2) * i + 1 if st.iters > 1 else (st.base + u) // 2 + 1,
               st.step * i + u)
    turns(eng, st.iters, body)
    for u, entry in enumerate(st.tail):
        c = st.base + st.iters * st.step + u
        fn(entry, 0, c, c % 2, c // 2 + 1, c - st.base)


class Mark:

    def __init__(self, sem, base):
        self.sem, self.base = sem, base


def wait_for(eng, mark, value):
    if isinstance(mark, Mark):
        eng.wait_ge(mark.sem, value + mark.base)
    else:
        eng.wait_ge(mark, value)


def wait_past(eng, mark, value):
    if not isinstance(value, int) or value > 0:
        wait_for(eng, mark, value)


def build(nc, dram):
    with ExitStack() as ctx:
        _build(nc, dram, ctx)


def _build(nc, dram, ctx):
    chunks = 0
    ORDER = []

    def stage(make, *args):
        nonlocal chunks
        st = make(chunks, *args)
        ORDER.append(st)
        chunks += st.count
        return st

    W = dram
    st_ein = stage(same, W["w_e_in"], KD * 256, 2)
    st_mla = stage(Stage, 4, [(W["w_e_uq"], 512, 0, 1), (W["w_e_ukv"], 256, 0, 1)])
    st_dil = stage(Stage, 4, [(W["w_e_qk"], KD * 256, 0, 1), (W["w_e_v"], KD * P, 0, 1)])
    st_eout = stage(same, W["w_e_out"], KD * 256, 4)
    st_ffn = []
    for layer in range(2):
        if layer == 1:
            st_okv = stage(same, W["w_o_kv"], KD * 256, 1)
            st_swa = stage(same, W["w_o_q"], KD * P, 8)
            st_oout = stage(same, W["w_o_out"], KD * 256, 4)
        for half in range(2):
            up = stage(same, W["w_f_gu"], KD * 256, KF, (2 * layer + half) * KF)
            down = stage(same, W["w_f_dn"], KF * P, KD, (2 * layer + half) * KD)
            st_ffn.append((up, down))
    st_z = stage(same, W["w_a_z"], KD * P, 1)
    st_gla = stage(Stage, 4, [(W["w_a_qk"], KD * 256, 0, 1), (W["w_a_v"], KD * 256, 0, 1),
                              (W["w_a_g"], KD * P, 0, 2), (W["w_a_g"], KD * P, 1, 2)])
    st_aout = stage(same, W["w_a_out"], KD * 256, 4)
    st_mlp = []
    for layer in range(2):
        if layer == 1:
            st_diff = stage(Stage, 8, [(W["w_b_qk"], KD * 256, 0, 1), (W["w_b_v"], KD * P, 0, 1)])
            st_bout = stage(same, W["w_b_out"], KD * 256, 4)
        for half in range(2):
            up = stage(same, W["w_m_up"], KD * 256, KH // 2, (2 * layer + half) * KH // 2)
            down = stage(same, W["w_m_dn"], KH * P, KD, (2 * layer + half) * KD)
            st_mlp.append((up, down))

    def sb(name, shape, dt=F32):
        return ctx.enter_context(nc.sbuf_tensor(name, shape, dt))

    def sem(name):
        return ctx.enter_context(nc.semaphore(name))

    h = sb("h", [P, KD, TOK])
    xh = sb("xh", [P, KD, TOK], F32R)
    xl = sb("xl", [P, KD, TOK], F32R)
    raw = [sb(f"raw{i}", [P, SLOT]) for i in range(2)]
    wh = [sb(f"wh{i}", [P, SLOT], F32R) for i in range(2)]
    wl = [sb(f"wl{i}", [P, SLOT], F32R) for i in range(2)]
    sq = sb("sq", [P, 4, TOK])
    rstd = sb("rstd", [P, TOK])
    xf = sb("xf", [P, 2, TOK])
    gains = sb("gains", [P, NGAINS])
    ident = sb("ident", [P, P])
    ones = sb("ones", [P, P])
    blockones = sb("blockones", [P, P])
    eps = sb("eps", [P, 1])
    small = sb("small", [P, 64])

    arena_base = (nc.sbuf_base + 63) // 64 * 64

    def area(name, specs, start=arena_base):
        at, out = start, []
        for n, shape, dt in specs:
            size = int(np.prod(shape[1:])) * 4
            out.append(nc.alloc_sbuf_tensor_at(f"{name}_{n}", list(shape), dt, offset=at))
            at += (size + 63) // 64 * 64
        assert at <= nc.sbuf_usable_end, (name, at, nc.sbuf_usable_end)
        return out, at

    (oh, ol), arena_rest = area("mix", [("oh", (P, KD, TOK), F32R), ("ol", (P, KD, TOK), F32R)])
    (e_cqh, e_cql, e_ckh, e_ckl, e_q0, e_q1, e_k0, e_k1, e_v0, e_v1, e_p, e_t0, e_causal, e_ropeq), _ = area("mla", [
         ("cqh", (P, 2, TOK), F32R), ("cql", (P, 2, TOK), F32R),
         ("ckh", (P, 1, TOK), F32R), ("ckl", (P, 1, TOK), F32R),
         ("q0", (P, 2, TOK), F32), ("q1", (P, 2, TOK), F32),
         ("k0", (P, 2, TOK), F32), ("k1", (P, 2, TOK), F32),
         ("v0", (P, TB, P), F32), ("v1", (P, TB, P), F32),
         ("p", (P, 8, TOK), F32), ("t0", (P, TB, TOK), F32),
         ("causal", (P, TOK), F32), ("ropeq", (P, TOK), F32)], arena_rest)
    (d_q0, d_q1, d_k0, d_k1, d_v0, d_v1, d_p, d_t0, d_b0, d_b1), _ = area("dil", [
        ("q0", (P, TOK), F32), ("q1", (P, TOK), F32), ("k0", (P, TOK), F32), ("k1", (P, TOK), F32),
        ("v0", (P, TB, P), F32), ("v1", (P, TB, P), F32),
        ("p", (P, 8, TOK), F32), ("t0", (P, TB, TOK), F32),
        ("b0", (P, 2, TOK), F32), ("b1", (P, 2, TOK), F32)], arena_rest)
    (s_q0, s_q1, s_k, s_v, s_p, s_t0, s_b0, s_b1, s_neg0, s_neg1, s_es), _ = area("swa", [
        ("q0", (P, TOK), F32), ("q1", (P, TOK), F32), ("k", (P, TOK), F32), ("v", (P, TB, P), F32),
        ("p", (P, 8, TOK), F32), ("t0", (P, TB, TOK), F32),
        ("b0", (P, 2, 256), F32), ("b1", (P, 2, 256), F32), ("neg0", (P, 2), F32),
        ("neg1", (P, 2), F32), ("es", (P, 8), F32)], arena_rest)
    (hidh, hidl), _ = area("ffn", [("hidh", (P, KH, TOK), F32R), ("hidl", (P, KH, TOK), F32R)])
    (g_b, g_z, g_wg, g_q, g_k, g_v, g_g, g_tmp, g_e, g_ks0, g_ks1, g_qs0, g_qs1, g_at, g_qe, g_kt,
     g_ktt, g_s, g_masks, g_reset, g_y, g_cum), _ = area("gla", [
         ("b", (P, 4, TOK), F32), ("z", (16, TOK), F32), ("wg", (16, TOK), F32),
         ("q", (P, TOK), F32), ("k", (P, TOK), F32), ("v", (P, TB, 256), F32),
         ("g", (P, 2, TOK), F32), ("tmp", (P, TOK), F32), ("e", (P, TOK), F32),
         ("ks0", (P, TOK), F32), ("ks1", (P, TOK), F32), ("qs0", (P, TOK), F32),
         ("qs1", (P, TOK), F32), ("at", (P, TOK), F32), ("qe", (P, TOK), F32),
         ("kt", (P, TOK), F32), ("ktt", (P, TOK), F32), ("s", (P, 256), F32),
         ("masks", (P, 8, P), U32), ("reset", (P, TOK), F32), ("y", (P, 2, TOK), F32),
         ("cum", (P, TOK), F32)], arena_rest)
    (f_kh, f_kl, f_o, f_q0, f_q1, f_k0, f_k1, f_v0, f_v1, f_p, f_t, f_causal, f_raw, f_lam), _ = area("diff", [
        ("kh", (P, KD, TOK), F32R), ("kl", (P, KD, TOK), F32R), ("o", (P, KD, TOK), F32),
        ("q0", (P, TOK), F32), ("q1", (P, TOK), F32), ("k0", (P, TOK), F32), ("k1", (P, TOK), F32),
        ("v0", (P, TB, P), F32), ("v1", (P, TB, P), F32), ("p", (P, 8, TOK), F32),
        ("t", (P, TB, TOK), F32), ("causal", (P, TOK), F32), ("raw", (P, 2, TOK), F32),
        ("lam", (P, 260), F32)])

    rsum, rinv, nmax, lamr = small[:, 0:8], small[:, 8:16], small[:, 16:24], small[:, 24:28]
    lam = small[:, 32:40]
    kc_tab, ks_tab = xf[:, 0, :], xf[:, 1, :]

    ps = ctx.enter_context(nc.psum_tensor("ps", [P, 8, TOK], F32))
    A0, A1, T_BANK, O_BANK = 0, 1, 5, 7
    S_BANK = ((2, 3, 4, 2), (3, 4, 2, 3))

    w_loaded = [sem("w_loaded0"), sem("w_loaded1")]
    w_rounded = sem("w_rounded")
    w_split = sem("w_split")
    w_used = sem("w_used")
    x_loaded = sem("x_loaded")
    const_loaded = sem("const_loaded")
    consts_made = sem("consts_made")
    out_stored = sem("out_stored")

    def sems(tag, names):
        return {n: sem(f"{tag}_{n}") for n in names.split()}

    block = ctx.enter_context(nc.Block())

    def log_exp(act):
        act.preload_act_table_set("natural_log_exp_and_others")

    def stand_alone(ins):
        return ins.wait_op(consts_made, 2, "sem-ge")

    def mm3(pe, out, sh, sl, mh, ml, start, stop):
        pe.matmul(out, sh, mh, start=start, stop=False)
        pe.matmul(out, sh, ml, start=False, stop=False)
        return pe.matmul(out, sl, mh, start=False, stop=stop)

    def chunk_w(slot, kt, cols):
        n = kt * cols
        return (wh[slot][:, 0:n].rearrange("p (k n) -> p k n", k=kt),
                wl[slot][:, 0:n].rearrange("p (k n) -> p k n", k=kt))

    norm_sems = sems("norm", "squared summed logged rstd scaled rounded split")
    resid_sems = sems("resid", "added")
    up_sems = sems("up", "acted made rounded split")
    counted = {}

    def marks(group, adds):
        out = {}
        for name, n in adds.items():
            key = (id(group), name)
            out[name] = Mark(group[name], counted.get(key, 0))
            counted[key] = counted.get(key, 0) + n
        return out

    class Norm:
        def __init__(self, nt, src, outs):
            n = nt * max(1, len(outs))
            self.s = marks(norm_sems, dict(squared=nt, summed=nt, logged=1, rstd=1, scaled=n,
                                           rounded=nt * len(outs), split=nt * len(outs)))
            self.nt, self.src = nt, src
            self.outs, self.bank = outs, T_BANK

    def norm_act(act, N, ready):
        s = N.s
        for sm, v in ready:
            wait_for(act, sm, v)
        for t in range(N.nt):
            if t >= 4:
                wait_for(act, s["summed"], t - 3)
            act.activation(sq[:, t % 4, :], N.src(t), ACT.Square).then_inc(s["squared"].sem, 1)
        wait_for(act, s["summed"], N.nt)
        act.activation(rstd[:, :], ps[:, N.bank, :], ACT.Ln, bias=eps[:, 0:1],
                       scale=1.0 / (N.nt * P)).then_inc(s["logged"].sem, 1)
        wait_for(act, s["logged"], 1)
        act.activation(rstd[:, :], rstd[:, :], ACT.Exp, scale=-0.5).then_inc(s["rstd"].sem, 1)
        m = 0
        for high, _, _ in N.outs:
            for t in range(N.nt):
                m += 1
                wait_for(act, s["scaled"], m)
                act.activation(high[:, t, :], xf[:, (m - 1) % 2, :], ACT.Copy).then_inc(s["rounded"].sem, 1)

    def norm_dve(dve, N, ready=()):
        s = N.s
        for sm, v in ready:
            wait_for(dve, sm, v)
        wait_for(dve, s["rstd"], 1)
        if s["split"].base:
            wait_for(dve, s["split"], 0)
        todo = [(hi, lo, g, t) for hi, lo, g in N.outs for t in range(N.nt)]

        def scale(m):
            _, _, g, t = todo[m]
            if m >= 2:
                wait_for(dve, s["split"], m - 1)
            dve.scalar_tensor_tensor(out=xf[:, m % 2, :], in0=N.src(t), scalar=gains[:, g + t:g + t + 1],
                                     in1=rstd[:, :], op0=ALU.mult, op1=ALU.mult).then_inc(s["scaled"].sem, 1)

        scale(0)
        for m, (hi, lo, g, t) in enumerate(todo):
            if m + 1 < len(todo):
                scale(m + 1)
            wait_for(dve, s["rounded"], m + 1)
            dve.tensor_tensor(lo[:, t, :], xf[:, m % 2, :], hi[:, t, :].bitcast(F32),
                              ALU.subtract).then_inc(s["split"].sem, 1)

    def norm_pe(pe, N):
        s = N.s
        for t in range(N.nt):
            wait_for(pe, s["squared"], t + 1)
            pe.matmul(ps[:, N.bank, :], ones[:, :], sq[:, t % 4, :], start=(t == 0),
                      stop=(t == N.nt - 1)).then_inc(s["summed"].sem, 1)

    class Resid:
        def __init__(self, st, kt, nt, xs, ready, before=0, prev=None):
            self.st, self.kt, self.nt, self.xs, self.ready = st, kt, nt, xs, ready
            self.added = marks(resid_sems, dict(added=st.count))["added"]
            self.before, self.prev, self.read, self.per = before, prev, self.added, 1

    def banks_read(pe, X, n):
        if isinstance(n, int) and n < 2:
            if X.prev:
                wait_for(pe, X.prev.read, X.prev.per * (X.prev.st.count + n - 1))
        else:
            wait_for(pe, X.read, X.per * (n - 1))

    def resid_pe(pe, R):
        def one(entry, i, c, slot, uses, n):
            w_h, w_l = chunk_w(slot, R.kt, R.nt * P)
            pe.wait_ge(w_split, c + 1)
            banks_read(pe, R, n)
            par = slot
            for k in range(R.kt):
                if isinstance(n, int) and n == 0:
                    wait_for(pe, R.ready, max(1, k + 1 - R.before))
                for j in range(R.nt):
                    last = mm3(pe, ps[:, 2 * par + j, :], w_h[:, k, j * P:(j + 1) * P],
                               w_l[:, k, j * P:(j + 1) * P], R.xs[0][:, k, :], R.xs[1][:, k, :],
                               k == 0, k == R.kt - 1)
            last.then_inc(w_used, 1)
        each_chunk(pe, R.st, one)

    def resid_dve(dve, R):
        def one(entry, i, c, slot, uses, n):
            par = slot
            dve.wait_ge(w_used, c + 1)
            to = h[:, bass.ds(n * R.nt, R.nt), :] if not isinstance(n, int) else h[:, n * R.nt:(n + 1) * R.nt, :]
            dve.tensor_tensor(to, to, ps[:, 2 * par:2 * par + R.nt, :], ALU.add).then_inc(R.added.sem, 1)
        each_chunk(dve, R.st, one)

    class Up:
        def __init__(self, st, ready, swiglu, prev=None):
            self.st, self.ready, self.swiglu, self.prev = st, ready, swiglu, prev
            n = st.count * (1 if swiglu else 2)
            self.s = marks(up_sems, dict(acted=n, made=n, rounded=n, split=n))
            self.read, self.per = (self.s["made"], 1) if swiglu else (self.s["acted"], 2)

    def at_tile(buf, n):
        return buf[:, n, :] if isinstance(n, int) else buf[:, bass.ds(n, 1), :].rearrange("p a t -> p (a t)")

    def up_pe(pe, U):
        def one(entry, i, c, slot, uses, n):
            w_h, w_l = chunk_w(slot, KD, 256)
            par = slot
            pe.wait_ge(w_split, c + 1)
            banks_read(pe, U, n)
            for k in range(KD):
                if isinstance(n, int) and n == 0:
                    wait_for(pe, U.ready, k + 1)
                for j in range(2):
                    last = mm3(pe, ps[:, 2 * par + j, :], w_h[:, k, j * P:(j + 1) * P],
                               w_l[:, k, j * P:(j + 1) * P], xh[:, k, :], xl[:, k, :], k == 0, k == KD - 1)
            last.then_inc(w_used, 1)
        each_chunk(pe, U.st, one)

    def up_act(act, U):
        s = U.s

        def one(entry, i, c, slot, uses, n):
            par = slot
            act.wait_ge(w_used, c + 1)
            if U.swiglu:
                wait_past(act, s["made"], n - 1)
                act.activation(sq[:, par, :], ps[:, 2 * par, :], ACT.Silu).then_inc(s["acted"].sem, 1)
                wait_for(act, s["made"], n + 1)
                act.activation(at_tile(hidh, n), sq[:, 2 + par, :], ACT.Copy).then_inc(s["rounded"].sem, 1)
            else:
                for j in range(2):
                    wait_past(act, s["made"], 2 * n + j - 1)
                    act.activation(sq[:, j, :], ps[:, 2 * par + j, :], ACT.Relu).then_inc(s["acted"].sem, 1)
                for j in range(2):
                    wait_for(act, s["made"], 2 * n + j + 1)
                    act.activation(at_tile(hidh, 2 * n + j), sq[:, 2 + j, :], ACT.Copy).then_inc(s["rounded"].sem, 1)
        each_chunk(act, U.st, one)

    def up_dve(dve, U):
        s = U.s

        def one(entry, i, c, slot, uses, n):
            par = slot
            if U.swiglu:
                wait_for(dve, s["acted"], n + 1)
                wait_past(dve, s["split"], n - 1)
                dve.tensor_tensor(sq[:, 2 + par, :], sq[:, par, :], ps[:, 2 * par + 1, :],
                                  ALU.mult).then_inc(s["made"].sem, 1)
                wait_for(dve, s["rounded"], n + 1)
                dve.tensor_tensor(at_tile(hidl, n), sq[:, 2 + par, :], at_tile(hidh, n).bitcast(F32),
                                  ALU.subtract).then_inc(s["split"].sem, 1)
            else:
                for j in range(2):
                    wait_for(dve, s["acted"], 2 * n + j + 1)
                    wait_past(dve, s["split"], 2 * n + j - 1)
                    dve.tensor_tensor(sq[:, 2 + j, :], sq[:, j, :], sq[:, j, :], ALU.mult).then_inc(s["made"].sem, 1)
                for j in range(2):
                    wait_for(dve, s["rounded"], 2 * n + j + 1)
                    dve.tensor_tensor(at_tile(hidl, 2 * n + j), sq[:, 2 + j, :],
                                      at_tile(hidh, 2 * n + j).bitcast(F32), ALU.subtract).then_inc(s["split"].sem, 1)
        each_chunk(dve, U.st, one)

    hsrc = lambda t: h[:, t, :]


    lat = sems("lat", "taken roped")



    lraw = e_t0
    k_rot = e_p

    def latents_pe(pe):
        for n in range(2):
            c = st_ein.base + n
            w_h, w_l = chunk_w(c % 2, KD, 256)
            pe.wait_ge(w_split, c + 1)
            for k in range(KD):
                if n == 0:
                    wait_for(pe, n_attn0.s["split"], k + 1)
                for bank, col in ((0, 0), (1, P)) if n == 0 else ((2, 0), (3, 64), (4, P)):
                    last = mm3(pe, ps[:, bank, :], w_h[:, k, col:col + P], w_l[:, k, col:col + P],
                               xh[:, k, :], xl[:, k, :], k == 0, k == KD - 1)
            last.then_inc(w_used, 1)

    def latents_act(act):
        act.wait_ge(w_used, st_ein.base + 1)
        for t in range(2):
            act.activation(lraw[:, t, :], ps[:, t, :], ACT.Copy).then_inc(lat["taken"], 1)
        act.wait_ge(w_used, st_ein.base + 2)
        act.activation(lraw[:, 2, :], ps[:, 2, :], ACT.Copy).then_inc(lat["taken"], 1)
        wait_for(act, n_attn0.s["split"], KD)
        act.dma_start(kc_tab, dram["rope_k"][0]).then_inc(rope_loaded, 16)
        act.dma_start(ks_tab, dram["rope_k"][1]).then_inc(rope_loaded, 16)
        act.wait_ge(lat["roped"], 3)
        for kbuf in (e_k0, e_k1):
            for hh in range(2):
                act.activation(kbuf[64:P, hh, :], k_rot[64:P, 2, :], ACT.Copy).then_inc(key_placed, 1)

    def latents_dve(dve):
        dve.wait_ge(w_used, st_ein.base + 2)
        dve.wait_ge(rope_loaded, 32)
        for t, tab in enumerate((kc_tab, ks_tab)):
            dve.tensor_tensor(k_rot[64:P, t, :], ps[64:P, 3 + t, :], tab[64:P, :],
                              ALU.mult).then_inc(lat["roped"], 1)
        dve.wait_ge(lat["roped"], 2)
        dve.tensor_tensor(k_rot[64:P, 2, :], k_rot[64:P, 0, :], k_rot[64:P, 1, :],
                          ALU.add).then_inc(lat["roped"], 1)

    rope_loaded = sem("rope_loaded")
    key_placed = sem("key_placed")

    ATT_ALL = ("q_made q_staged k_staged v_staged scored masked exped inverted normed turned pt_copied pv_done "
           "o_rounded o_taken")
    ATT_MORE = {"mla": "", "dil": " tab_loaded0 tab_loaded1", "swa": " tab_loaded0 tab_loaded1 es",
                "diff": " raw_staged squared logged rooted"}

    class Att:
        pass

    def attention(tag, kind, st, pairs, scale, q, k, v, p, pt, tab, first_out):
        A = Att()
        A.kind, A.st, A.pairs, A.scale, A.first_out = kind, st, pairs, scale, first_out
        A.q, A.k, A.v, A.p, A.pt, A.tab = q, k, v, p, pt, tab
        A.s = sems(tag, ATT_ALL + ATT_MORE[kind])
        return A

    CAUSAL = [(0, (i + 1) * P) for i in range(TB)]
    BAND = [(max(i - 1, 0) * P, (i + 1) * P) for i in range(TB)]

    def span(A, i):
        return BAND[i] if A.kind == "swa" else CAUSAL[i]

    def heads_q(A, st, hh, i):
        if A.kind == "mla":
            return A.q[st][:, hh, i * P:(i + 1) * P]
        return A.q[st][64 * hh:64 * hh + 64, i * P:(i + 1) * P]

    def heads_k(A, st, hh, i):
        a, b = span(A, i)
        if A.kind == "mla":
            return A.k[st][:, hh, a:b]
        return A.k[st][64 * hh:64 * hh + 64, a:b]

    def table(A, st, hh, i):
        a, b = span(A, i)
        if A.kind in ("mla", "diff"):
            return A.tab[st][:, TOK - (b - a):TOK]
        full = 256 if A.kind == "swa" else TOK
        return A.tab[st][:, hh, full - (b - a):full]

    def attention_steps(eng, A, project, step, tail):
        n = A.pairs
        project(0, 0, 0)

        def body(i):
            for u in range(2):
                prev = None if isinstance(i, int) and i == 0 and u == 0 else (2 * i + u - 1, 1 - u)
                step(2 * i + u, u, i, (2 * i + u + 1, 1 - u, i + u), prev)
        turns(eng, n // 2 - 1, body)
        i = n // 2 - 1
        step(n - 2, 0, i, (n - 1, 1, i), (n - 3, 1))
        step(n - 1, 1, i, None, (n - 2, 0))
        tail(n - 1, 1)

    def att_pe(pe, A, ready):
        s, kind = A.s, A.kind
        for sm, v in ready:
            wait_for(pe, sm, v)

        def tile(bank, w_h, w_l, col, x, ks, n=KD):
            for k in ks:
                last = mm3(pe, ps[:, bank, :], w_h[:, k, col:col + P], w_l[:, k, col:col + P],
                           x[0][:, k, :], x[1][:, k, :], k == 0, k == n - 1)
            return last

        def pieces(p, st, turn):
            if kind == "swa":
                c = A.st.base + p
                w_h, w_l = chunk_w((A.st.base + st) % 2, KD, P)

                def quarter(n):
                    if n == 0:
                        pe.wait_ge(w_split, c + 1)
                        wait_past(pe, s["q_staged"], p)
                    last = tile(A0, w_h, w_l, 0, (xh, xl), (2 * n, 2 * n + 1))
                    if n == 3:
                        last.then_inc(w_used, 1)
                return [lambda n=n: quarter(n) for n in range(4)]

            c = A.st.base + 2 * p
            slots = (A.st.base % 2, (A.st.base + 1) % 2)
            if kind == "mla":
                def queries():
                    w_h, w_l = chunk_w(slots[0], 2, 256)
                    pe.wait_ge(w_split, c + 1)
                    wait_past(pe, s["v_staged"], p)
                    wait_past(pe, s["k_staged"], 2 * p)
                    for hh in range(2):
                        last = tile(A0 + hh, w_h, w_l, hh * P, (e_cqh, e_cql), range(2), 2)
                    last.then_inc(w_used, 1)

                def keys():
                    w_h, w_l = chunk_w(slots[1], 1, 256)
                    pe.wait_ge(w_split, c + 2)
                    for hh in range(2):
                        pe.wait_ge(s["q_staged"], 2 * p + hh + 1)
                        tile(A0 + hh, w_h, w_l, hh * P, (e_ckh, e_ckl), range(1), 1)\
                            .then_inc(keys_made, 1)

                def values():
                    w_h, w_l = chunk_w(slots[1], 1, 256)
                    vh = w_h[:, 0, :].rearrange("p (a b) -> p a b", a=2)[:, :, 64:P]
                    vl = w_l[:, 0, :].rearrange("p (a b) -> p a b", a=2)[:, :, 64:P]
                    pe.wait_ge(s["k_staged"], 2 * p + 1)
                    for t in range(TB):
                        last = mm3(pe, ps[:, A0, t * P:(t + 1) * P], e_ckh[:, 0, t * P:(t + 1) * P],
                                   e_ckl[:, 0, t * P:(t + 1) * P], vh, vl, True, True)
                    last.then_inc(w_used, 1)
                return [queries, keys, values]

            kx = (f_kh, f_kl) if kind == "diff" else (xh, xl)

            def half(which, n):
                w_h, w_l = chunk_w(slots[0], KD, 256)
                if n == 0 and which == 0:
                    pe.wait_ge(w_split, c + 1)
                    wait_past(pe, s["v_staged"], p)
                elif n == 0 and kind == "diff":
                    wait_past(pe, s["logged"], 2 * p)
                elif n == 0:
                    wait_past(pe, s["k_staged"], p)
                last = tile(A0 + which, w_h, w_l, which * P, kx if which else (xh, xl),
                            range(4 * n, 4 * n + 4))
                if n == 1:
                    last.then_inc(w_used if which else s["q_made"], 1)

            def sums(which):
                pe.wait_ge(s["squared"], 2 * p + which + 1)
                pe.wait_ge(s["raw_staged"], 2 * p + 2 - which)
                pe.matmul(ps[:, A1 - which, :], blockones[:, :], sq[:, which, :], start=True, stop=True)\
                  .then_inc(sums_made, 1)

            def value(t):
                w_h, w_l = chunk_w(slots[1], KD, P)
                if t == 0:
                    pe.wait_ge(w_split, c + 2)
                    if kind == "diff":
                        pe.wait_ge(s["logged"], 2 * p + 2)
                    else:
                        pe.wait_ge(s["q_staged"], p + 1)
                for k in range(KD):
                    last = mm3(pe, ps[:, A0, t * P:(t + 1) * P], kx[0][:, k, t * P:(t + 1) * P],
                               kx[1][:, k, t * P:(t + 1) * P], w_h[:, k, :], w_l[:, k, :],
                               k == 0, k == KD - 1)
                if t == TB - 1:
                    last.then_inc(w_used, 1)

            qk = [lambda a=a, n=n: half(a, n) for a in range(2) for n in range(2)]
            vs = [lambda t=t: value(t) for t in range(TB)]
            if kind == "diff":
                return qk + [lambda: sums(0), lambda: sums(1)] + vs
            return qk + vs

        def scores(p, st, hh):
            if hh == 0:
                per = 2 if kind in ("mla", "diff") else 1
                pe.wait_ge(s["q_staged"], per * (p + 1) if kind == "mla" else p + 1)
                if kind != "swa":
                    pe.wait_ge(s["k_staged"], 2 * (p + 1) if kind == "mla" else p + 1)
                    pe.wait_ge(s["v_staged"], p + 1)
            for i in range(TB):
                a, b = span(A, i)
                u = 8 * p + 4 * hh + i
                wait_past(pe, s["masked"], u - 1 if hh == 0 and i < 2 else u - 2)
                pe.matmul(ps[:, S_BANK[hh][i], 0:b - a], heads_q(A, st, hh, i), heads_k(A, st, hh, i),
                          start=True, stop=True).then_inc(s["scored"], 1)

        def turn_p(p, hh, units, blocks):
            for i in blocks:
                a, b = span(A, i)
                u = units * p + (4 * hh if units == 8 else 0) + i
                pe.wait_ge(s["normed"], u + 1)
                wait_past(pe, s["pt_copied"], u - 1)
                for j in range((b - a) // P):
                    last = pe.transpose(ps[:, T_BANK + i % 2, j * P:(j + 1) * P],
                                        A.p[:, 4 * hh + i, j * P:(j + 1) * P], ident[:, :])
                last.then_inc(s["turned"], 1)

        def pv(p, st, hh, units):
            pe.wait_ge(s["pt_copied"], units * p + (4 * hh + 4 if units == 8 else 4))
            if hh == 0:
                wait_past(pe, s["o_taken"], p)
            pt = A.pt
            vals = A.v[st][:, :, :]
            o = ps[:, O_BANK, :] if kind == "diff" else ps[64 * hh:64 * hh + 64, O_BANK, :]
            cols = slice(0, P) if kind == "diff" else slice(64 * hh, 64 * hh + 64)
            if kind == "swa":
                for i in range(TB):
                    a, b = span(A, i)
                    n = (b - a) // P
                    for j in range(n):
                        last = pe.matmul(o[:, i * P:(i + 1) * P], vals[:, a // P + j, cols],
                                         pt[:, j, i * P:(i + 1) * P], start=(j == 0), stop=(j == n - 1))
            else:
                for j in range(TB):
                    last = pe.matmul(o[:, j * P:TOK], vals[:, j, cols], pt[:, j, j * P:TOK],
                                     start=(j == 0), stop=(j == TB - 1))
            last.then_inc(s["pv_done"], 1)

        SHARE = {"mla": (1, 0, 1, 0, 1, 0, 0, 0), "dil": (1, 1, 1, 1, 1, 1, 1, 1),
                 "swa": (1, 1, 0, 1, 0, 1, 0, 0), "diff": (1, 3, 1, 2, 3)}

        def step(p, st, turn, nx, prev):
            todo = pieces(*nx) if nx else []
            share = iter(SHARE[kind])

            def some():
                for _ in range(next(share)):
                    if todo:
                        todo.pop(0)()

            scores(p, st, 0)
            some()
            if kind == "diff":
                scores(p, st, 1)
                some()
                turn_p(p, 0, 4, (0, 1))
                some()
                turn_p(p, 0, 4, (2, 3))
                some()
                pv(p, st, 0, 4)
                some()
            else:
                if prev:
                    tail(*prev)
                some()
                scores(p, st, 1)
                some()
                turn_p(p, 0, 8, (0, 1))
                some()
                turn_p(p, 0, 8, (2, 3))
                some()
                pv(p, st, 0, 8)
                some()
                turn_p(p, 1, 8, (0, 1))
                some()
                turn_p(p, 1, 8, (2, 3))
                some()
            assert not todo

        def tail(p, st):
            if kind != "diff":
                pv(p, st, 1, 8)

        def project(p, st, turn):
            for piece in pieces(p, st, turn):
                piece()

        attention_steps(pe, A, project, step, tail)

    keys_made = sem("mla_keys_made")
    sums_made = sem("diff_sums_made")

    def att_act(act, A, ready=()):
        s, kind = A.s, A.kind
        for sm, v in ready:
            wait_for(act, sm, v)

        def load_table(p, st):
            wait_past(act, s["masked"], 8 * (p - 1))
            src = dram["tab_dil"] if kind == "dil" else dram["tab_swa"]
            act.dma_start(A.tab[st][:, :, :], src[p].rearrange("p (a b) -> p a b", a=2))\
               .then_inc(s[f"tab_loaded{st}"], 16)

        def queries(p, st):
            if kind == "swa":
                act.wait_ge(w_used, A.st.base + p + 1)
            else:
                act.wait_ge(s["q_made"], p + 1)
            act.activation(A.q[st][:, :], ps[:, A0, :], ACT.Copy).then_inc(s["q_staged"], 1)

        def keys(p, st):
            for hh in range(2):
                act.wait_ge(keys_made, 2 * p + hh + 1)
                act.activation(A.k[st][0:64, hh, :], ps[0:64, A0 + hh, :], ACT.Copy)\
                   .then_inc(s["k_staged"], 1)

        def values(p, st):
            act.wait_ge(w_used, A.st.base + 2 * p + 2)
            act.activation(A.v[st][:, :, :], ps[:, A0, :].rearrange("p (a b) -> p a b", a=TB),
                           ACT.Copy).then_inc(s["v_staged"], 1)

        def squares(p):
            for j in range(2):
                act.wait_ge(s["raw_staged"], 2 * p + j + 1)
                act.activation(sq[:, j, :], f_raw[:, j, :], ACT.Square).then_inc(s["squared"], 1)

        def root(p, j):
            act.wait_ge(sums_made, 2 * p + j + 1)
            wait_past(act, s["k_staged" if j else "q_staged"], p)
            act.activation(sq[:, 2 + j, :], ps[:, A1 - j, :], ACT.Ln, bias=eps[:, 0:1],
                           scale=1.0 / 64).then_inc(s["logged"], 1)
            act.wait_ge(s["logged"], 2 * p + j + 1)
            act.activation(sq[:, 2 + j, :], sq[:, 2 + j, :], ACT.Exp, scale=-0.5).then_inc(s["rooted"], 1)

        def project(p, st, turn):
            if kind in ("dil", "swa"):
                load_table(p, st)
                queries(p, st)
            if kind == "mla":
                keys(p, st)
            if kind == "diff":
                squares(p)
                root(p, 0)
                root(p, 1)
            if kind != "swa":
                values(p, st)

        def exps(p, hh):
            for i in range(TB):
                a, b = span(A, i)
                u = 8 * p + 4 * hh + i
                row = 4 * hh + i
                slot = 4 * hh + i
                act.wait_ge(s["masked"], u + 1)
                act.activation(A.p[:, slot, 0:b - a], A.p[:, slot, 0:b - a], ACT.Exp, scale=-1.0,
                               bias=nmax[:, row:row + 1], accum_out=rsum[:, row:row + 1])\
                   .then_inc(s["exped"], 1)
            if kind == "swa":
                act.wait_ge(s["es"], 2 * (2 * p + hh) + 1)
                act.activation(s_es[:, 4 * hh:4 * hh + 4], s_es[:, 4 * hh:4 * hh + 4], ACT.Exp)\
                   .then_inc(s["exped"], 1)

        def copy_pt(p, hh, units, blocks=range(TB)):
            for i in blocks:
                a, b = span(A, i)
                n = (b - a) // P
                u = units * p + (4 * hh if units == 8 else 0) + i
                act.wait_ge(s["turned"], u + 1)
                wait_past(act, s["pv_done"], (2 * p + hh) if units == 8 else p)
                act.activation(A.pt[:, 0:n, i * P:(i + 1) * P],
                               ps[:, T_BANK + i % 2, 0:n * P].rearrange("p (a b) -> p a b", a=n),
                               ACT.Copy).then_inc(s["pt_copied"], 1)

        def tail(p, st):
            if kind != "diff":
                act.wait_ge(s["pv_done"], 2 * p + 2)
                act.activation(at_tile(oh, A.first_out + p), ps[:, O_BANK, :], ACT.Copy)\
                   .then_inc(s["o_rounded"], 1)

        def step(p, st, turn, nx, prev):
            if nx and kind in ("dil", "swa"):
                load_table(nx[0], nx[1])
            exps(p, 0)
            if kind == "diff":
                exps(p, 1)
                if nx:
                    squares(nx[0])
                copy_pt(p, 0, 4, (0, 1))
                if nx:
                    root(nx[0], 0)
                copy_pt(p, 0, 4, (2, 3))
                if nx:
                    root(nx[0], 1)
                act.wait_ge(s["pv_done"], p + 1)
                act.activation(at_tile(f_o, p), ps[:, O_BANK, :], ACT.Copy).then_inc(s["o_taken"], 1)
                if nx:
                    values(nx[0], nx[1])
                return
            if prev:
                tail(*prev)
            if nx and kind == "dil":
                queries(nx[0], nx[1])
            exps(p, 1)
            if nx and kind == "mla":
                keys(nx[0], nx[1])
            copy_pt(p, 0, 8)
            if nx and kind == "mla":
                values(nx[0], nx[1])
            if nx and kind == "swa":
                queries(nx[0], nx[1])
            copy_pt(p, 1, 8)
            if nx and kind == "dil":
                values(nx[0], nx[1])

        attention_steps(act, A, project, step, tail)

    def att_dve(dve, A, ready=()):
        s, kind = A.s, A.kind
        for sm, v in ready:
            wait_for(dve, sm, v)

        def neg_sinks(p, st):
            wait_past(dve, s["masked"], 8 * (p - 1))
            g = GAINS["sinks"] + 2 * p
            src = gains[:, g:g + 2] if isinstance(p, int) else gains[:, bass.ds(g, 2)]
            dve.tensor_scalar(A.neg[st][:, :], src, -1.0, None, ALU.mult).then_inc(sinks_ready, 1)

        def rotate(p, st):
            dve.wait_ge(w_used, A.st.base + 2 * p + 1)
            for hh in range(2):
                dve.tensor_tensor(A.q[st][:, hh, :], ps[:, A0 + hh, :], e_ropeq[:, :], ALU.mult)\
                   .then_inc(s["q_staged"], 1)

        def keys(p, st):
            dve.wait_ge(w_used, A.st.base + 2 * p + 1)
            dve.tensor_copy(A.k[st][:, :], ps[:, A1, :]).then_inc(s["k_staged"], 1)

        def raw_qk(p):
            for j in range(2):
                if j == 0:
                    dve.wait_ge(s["q_made"], p + 1)
                else:
                    dve.wait_ge(w_used, A.st.base + 2 * p + 1)
                wait_past(dve, s["k_staged" if j else "q_staged"], p)
                wait_past(dve, s["squared"], 2 * p)
                dve.tensor_copy(f_raw[:, j, :], ps[:, A0 + j, :]).then_inc(s["raw_staged"], 1)

        def normed_qk(p, st):
            for j, (to, g, nm) in enumerate(((A.q[st], "q", "q_staged"), (A.k[st], "k", "k_staged"))):
                dve.wait_ge(s["rooted"], 2 * p + j + 1)
                dve.scalar_tensor_tensor(out=to[:, :], in0=f_raw[:, j, :],
                                         scalar=gains[:, GAINS[g]:GAINS[g] + 1],
                                         in1=sq[:, 2 + j, :], op0=ALU.mult, op1=ALU.mult)\
                   .then_inc(s[nm], 1)

        def project(p, st, turn):
            if kind == "swa":
                neg_sinks(p, st)
            elif kind == "mla":
                rotate(p, st)
            elif kind == "dil":
                keys(p, st)
            else:
                raw_qk(p)
                normed_qk(p, st)

        def mask(p, st, turn, hh):
            for i in range(TB):
                a, b = span(A, i)
                u = 8 * p + 4 * hh + i
                row = 4 * hh + i
                slot = 4 * hh + i
                dve.wait_ge(s["scored"], u + 1)
                if kind in ("dil", "swa") and hh == 0 and i == 0:
                    dve.wait_ge(s[f"tab_loaded{st}"], 16 * (turn + 1))
                    if kind == "swa":
                        dve.wait_ge(sinks_ready, p + 1)
                if kind == "diff":
                    wait_past(dve, s["turned"], 4 * (p - 1) + i + 1)
                    wait_past(dve, s["normed"], 4 * p)
                else:
                    wait_past(dve, s["turned"], u - 7)
                if u_is_late(p, hh):
                    dve.wait_ge(s["exped"], exped_before(A, p, hh))
                start = A.neg[st][:, hh:hh + 1] if kind == "swa" else 3e38
                stand_alone(dve.tensor_tensor_reduce(
                    A.p[:, slot, 0:b - a], ps[:, S_BANK[hh][i], 0:b - a], table(A, st, hh, i), -A.scale,
                    start, ALU.add, ALU.min, nmax[:, row:row + 1])).then_inc(s["masked"], 1)
            if kind == "swa":
                dve.wait_ge(s["masked"], 8 * p + 4 * hh + 4)
                dve.tensor_scalar(s_es[:, 4 * hh:4 * hh + 4], nmax[:, 4 * hh:4 * hh + 4],
                                  A.neg[st][:, hh:hh + 1], None, ALU.subtract).then_inc(s["es"], 1)

        def u_is_late(p, hh):
            return not (isinstance(p, int) and p == 0)

        def exped_before(A, p, hh):
            per = 10 if A.kind == "swa" else 8
            return per * p + (per // 2) * hh - per // 2

        def norm(p, hh):
            per = 10 if kind == "swa" else 8
            dve.wait_ge(s["exped"], per * p + (per // 2) * (hh + 1))
            r = slice(4 * hh, 4 * hh + 4)
            if kind == "swa":
                dve.tensor_tensor(rsum[:, r], rsum[:, r], s_es[:, r], ALU.add).then_inc(s["es"], 1)
                dve.wait_ge(s["es"], 2 * (2 * p + hh) + 2)
            dve.reciprocal(rinv[:, r], rsum[:, r]).then_inc(s["inverted"], 1)
            dve.wait_ge(s["inverted"], 2 * p + hh + 1)
            for i in range(TB):
                a, b = span(A, i)
                dve.tensor_scalar(A.p[:, 4 * hh + i, 0:b - a], A.p[:, 4 * hh + i, 0:b - a],
                                  rinv[:, 4 * hh + i:4 * hh + i + 1],
                                  None, ALU.mult).then_inc(s["normed"], 1)

        def norm_diff(p):
            dve.wait_ge(s["exped"], 8 * p + 8)
            dve.reciprocal(rinv[:, 0:8], rsum[:, 0:8]).then_inc(s["inverted"], 1)
            dve.wait_ge(s["inverted"], 2 * p + 1)
            dve.tensor_scalar(lamr, rinv[:, 4:8], lam[:, 7:8], None, ALU.mult).then_inc(s["inverted"], 1)
            for i in range(TB):
                a, b = span(A, i)
                dve.tensor_scalar(A.p[:, i, 0:b - a], A.p[:, i, 0:b - a], rinv[:, i:i + 1], None,
                                  ALU.mult).then_inc(p_scaled, 1)
            dve.wait_ge(s["inverted"], 2 * p + 2)
            for i in range(TB):
                a, b = span(A, i)
                dve.wait_ge(p_scaled, 4 * p + i + 1)
                dve.scalar_tensor_tensor(out=A.p[:, i, 0:b - a], in0=A.p[:, 4 + i, 0:b - a],
                                         scalar=lamr[:, i:i + 1], in1=A.p[:, i, 0:b - a],
                                         op0=ALU.mult, op1=ALU.add).then_inc(s["normed"], 1)

        def tail(p, st):
            if kind != "diff":
                dve.wait_ge(s["o_rounded"], p + 1)
                o = A.first_out + p
                dve.tensor_tensor(at_tile(ol, o), ps[:, O_BANK, :], at_tile(oh, o).bitcast(F32),
                                  ALU.subtract).then_inc(s["o_taken"], 1)

        def step(p, st, turn, nx, prev):
            mask(p, st, turn, 0)
            if kind == "diff":
                mask(p, st, turn, 1)
                norm_diff(p)
                if nx:
                    raw_qk(nx[0])
                    normed_qk(nx[0], nx[1])
                return
            norm(p, 0)
            if prev:
                tail(*prev)
            if nx and kind == "mla":
                rotate(nx[0], nx[1])
            mask(p, st, turn, 1)
            norm(p, 1)
            if nx and kind == "dil":
                keys(nx[0], nx[1])
            if nx and kind == "swa":
                neg_sinks(nx[0], nx[1])

        attention_steps(dve, A, project, step, tail)

    sinks_ready = sem("swa_sinks_ready")
    p_scaled = sem("diff_p_scaled")

    a_mla = attention("mla", "mla", st_mla, 4, 96.0 ** -0.5, (e_q0, e_q1), (e_k0, e_k1), (e_v0, e_v1),
                      e_p, e_t0, (e_causal, e_causal), 0)
    a_dil = attention("dil", "dil", st_dil, 4, 0.125, (d_q0, d_q1), (d_k0, d_k1), (d_v0, d_v1),
                      d_p, d_t0, (d_b0, d_b1), 4)
    a_swa = attention("swa", "swa", st_swa, 8, 0.125, (s_q0, s_q1), (s_k, s_k), (s_v, s_v),
                      s_p, s_t0, (s_b0, s_b1), 0)
    a_swa.neg = (s_neg0, s_neg1)
    kv_taken = sem("swa_kv_taken")
    kv_keys = sem("swa_kv_keys")




    def swa_kv_pe(pe):
        c = st_okv.base
        w_h, w_l = chunk_w(c % 2, KD, 256)
        pe.wait_ge(w_split, c + 1)
        for k in range(KD):
            wait_for(pe, n_attn1.s["split"], k + 1)
            last = mm3(pe, ps[:, A1, :], w_h[:, k, 0:P], w_l[:, k, 0:P], xh[:, k, :], xl[:, k, :],
                       k == 0, k == KD - 1)
        last.then_inc(kv_keys, 1)
        for t in range(TB):
            for k in range(KD):
                last = mm3(pe, ps[:, O_BANK, t * P:(t + 1) * P], xh[:, k, t * P:(t + 1) * P],
                           xl[:, k, t * P:(t + 1) * P], w_h[:, k, P:2 * P], w_l[:, k, P:2 * P],
                           k == 0, k == KD - 1)
        last.then_inc(w_used, 1)

    def swa_kv_act(act):
        act.wait_ge(kv_keys, 1)
        act.activation(s_k[:, :], ps[:, A1, :], ACT.Copy).then_inc(kv_taken, 1)
        act.wait_ge(w_used, st_okv.base + 1)
        act.activation(s_v[:, :, :], ps[:, O_BANK, :].rearrange("p (a b) -> p a b", a=TB), ACT.Copy)\
           .then_inc(kv_taken, 1)

    def final_dve(dve):
        wait_for(dve, n_fin.s["rstd"], 1)
        for t in range(KD):
            g = GAINS["final"] + t
            dve.scalar_tensor_tensor(out=h[:, t, :], in0=h[:, t, :], scalar=gains[:, g:g + 1],
                                     in1=rstd[:, :], op0=ALU.mult, op1=ALU.mult)\
               .then_inc(n_fin.s["scaled"].sem, 1)

    G = sems("gla", "tables z_taken pre_made biased absed exped1 logged lowered combined scanned "
             "q_taken k_taken v0_made v_taken g_taken cum_taken diff e ks qs products merged zeroed "
             "eb qe dlast elast kt_made kt_turned ktt_taken upd_made state out_made squared summed "
             "hlogged hrstd hy hy2 rounded split")

    def bview(x, s_):
        return x.rearrange("p (n b) -> p n b", b=2 * s_)

    def gla_gate_pe(pe):
        c = st_z.base
        w_h, w_l = chunk_w(c % 2, KD, P)
        pe.wait_ge(w_split, c + 1)
        for k in range(KD):
            wait_for(pe, n_a.s["split"], k + 1)
            last = mm3(pe, ps[:, 0, :], w_h[:, k, :], w_l[:, k, :], xh[:, k, :], xl[:, k, :],
                       k == 0, k == KD - 1)
        last.then_inc(w_used, 1)
        pe.wait_ge(G["z_taken"], 1)
        pe.wait_ge(G["tables"], 48)
        for hd in range(4):
            pe.matmul(ps[:, 4 + hd, :], g_wg[:, hd * P:(hd + 1) * P], g_z[:, :], start=True, stop=True)\
              .then_inc(G["pre_made"], 1)

    def gla_gate_act(act):
        wait_for(act, n_a.s["rstd"], 1)
        act.dma_start(g_wg[:, :], dram["a_gate_up"]).then_inc(G["tables"], 16)
        act.dma_start(g_masks[:, :, :], dram["level_masks"].rearrange("p (a b) -> p a b", a=8))\
           .then_inc(G["tables"], 16)
        act.dma_start(g_reset[:, :], dram["scan_reset"]).then_inc(G["tables"], 16)
        act.wait_ge(w_used, st_z.base + 1)
        act.activation(g_z[:, :], ps[0:16, 0, :], ACT.Copy).then_inc(G["z_taken"], 1)
        for hd in range(4):
            act.wait_ge(G["pre_made"], hd + 1)
            g = GAINS["b_gate"] + hd
            act.activation(sq[:, hd, :], ps[:, 4 + hd, :], ACT.Identity, bias=gains[:, g:g + 1])\
               .then_inc(G["biased"], 1)
        for hd in range(4):
            act.wait_ge(G["biased"], hd + 1)
            wait_past(act, G["combined"], hd)
            act.activation(g_tmp[:, :], sq[:, hd, :], ACT.Abs).then_inc(G["absed"], 1)
            act.wait_ge(G["absed"], hd + 1)
            act.activation(g_tmp[:, :], g_tmp[:, :], ACT.Exp, scale=-1.0).then_inc(G["exped1"], 1)
            act.wait_ge(G["exped1"], hd + 1)
            act.activation(g_tmp[:, :], g_tmp[:, :], ACT.Ln, bias=1.0).then_inc(G["logged"], 1)

    def gla_gate_dve(dve):
        dve.memset(g_at[:, :], 0.0).then_inc(G["zeroed"], 1)
        for buf in (g_ks0, g_ks1, g_qs0, g_qs1):
            dve.memset(buf[:, :], 0.0).then_inc(G["zeroed"], 1)
        dve.wait_ge(G["tables"], 48)
        for hd in range(4):
            dve.wait_ge(G["logged"], hd + 1)
            dve.scalar_tensor_tensor(out=sq[:, hd, :], in0=sq[:, hd, :], scalar=0.0, in1=g_tmp[:, :],
                                     op0=ALU.min, op1=ALU.subtract).then_inc(G["combined"], 1)
            dve.wait_ge(G["combined"], hd + 1)
            dve.tensor_tensor_scan(g_b[:, hd, :], g_reset[:, :], sq[:, hd, :], 0.0, ALU.mult, ALU.add)\
               .then_inc(G["scanned"], 1)

    NL = len(LEVELS) + 1
    KS, QS = (g_ks0, g_ks1), (g_qs0, g_qs1)

    def gla_pe(pe):
        def body(hd):
            c = st_gla.base + 4 * hd
            sl = [(st_gla.base + u) % 2 for u in range(4)]
            w_h, w_l = chunk_w(sl[0], KD, 256)
            pe.wait_ge(w_split, c + 1)
            wait_past(pe, G["g_taken"], 2 * hd)
            for k in range(KD):
                for j in range(2):
                    last = mm3(pe, ps[:, j, :], w_h[:, k, j * P:(j + 1) * P], w_l[:, k, j * P:(j + 1) * P],
                               xh[:, k, :], xl[:, k, :], k == 0, k == KD - 1)
            last.then_inc(w_used, 1)
            w_h, w_l = chunk_w(sl[1], KD, 256)
            pe.wait_ge(w_split, c + 2)
            for t in range(TB):
                if t % 2 == 0:
                    pe.wait_ge(G["k_taken" if t else "q_taken"], hd + 1)
                for k in range(KD):
                    last = mm3(pe, ps[:, t // 2, (t % 2) * 256:(t % 2) * 256 + 256],
                               xh[:, k, t * P:(t + 1) * P], xl[:, k, t * P:(t + 1) * P],
                               w_h[:, k, :], w_l[:, k, :], k == 0, k == KD - 1)
                if t == 1:
                    last.then_inc(G["v0_made"], 1)
            last.then_inc(w_used, 1)
            for j in range(2):
                w_h, w_l = chunk_w(sl[2 + j], KD, P)
                pe.wait_ge(w_split, c + 3 + j)
                pe.wait_ge(G["v_taken"], 2 * hd + j + 1)
                for k in range(KD):
                    last = mm3(pe, ps[:, j, :], w_h[:, k, :], w_l[:, k, :], xh[:, k, :], xl[:, k, :],
                               k == 0, k == KD - 1)
                last.then_inc(w_used, 1)
            for lv in range(NL):
                n = NL * hd + lv
                kk, qq = (KS[lv % 2], QS[lv % 2]) if lv < NL - 1 else (g_k, g_q)
                if lv < NL - 1:
                    pe.wait_ge(G["ks"], (NL - 1) * hd + lv + 1)
                    pe.wait_ge(G["qs"], (NL - 1) * hd + lv + 1)
                wait_past(pe, G["merged"], n - 1)
                for t in range(TB):
                    last = pe.matmul(ps[:, 2 + lv % 2, t * P:(t + 1) * P], kk[:, t * P:(t + 1) * P],
                                     qq[:, t * P:(t + 1) * P], start=True, stop=True)
                last.then_inc(G["products"], 1)
            pe.wait_ge(G["kt_made"], hd + 1)
            wait_past(pe, G["hlogged"], hd)
            for t in range(TB):
                last = pe.transpose(ps[:, 4, t * P:(t + 1) * P], g_kt[:, t * P:(t + 1) * P], ident[:, :])
            last.then_inc(G["kt_turned"], 1)
            pe.wait_ge(G["ktt_taken"], hd + 1)
            pe.wait_ge(G["merged"], NL * (hd + 1))
            pe.wait_ge(G["qe"], hd + 1)
            wait_past(pe, G["hy"], 2 * hd)
            for t in range(TB):
                if t > 0:
                    pe.wait_ge(G["state"], 3 * hd + t)
                for dv in range(2):
                    o = ps[:, 6 + dv, t * P:(t + 1) * P]
                    last = pe.matmul(o, g_v[:, t, dv * P:(dv + 1) * P], g_at[:, t * P:(t + 1) * P],
                                     start=True, stop=(t == 0))
                    if t > 0:
                        last = pe.matmul(o, g_s[:, dv * P:(dv + 1) * P], g_qe[:, t * P:(t + 1) * P],
                                         start=False, stop=True)
                last.then_inc(G["out_made"], 1)
                if t < TB - 1:
                    pe.matmul(ps[:, 5, 0:256], g_ktt[:, t * P:(t + 1) * P], g_v[:, t, :],
                              start=True, stop=True).then_inc(G["upd_made"], 1)
            for dv in range(2):
                pe.wait_ge(G["squared"], 2 * hd + dv + 1)
                pe.matmul(ps[:, 4, :], ones[:, :], g_y[:, dv, :], start=(dv == 0), stop=(dv == 1))\
                  .then_inc(G["summed"], 1)
        turns(pe, 4, body)

    def gla_act(act):
        def body(hd):
            c = st_gla.base + 4 * hd
            act.wait_ge(w_used, c + 1)
            wait_past(act, G["products"], NL * hd)
            wait_past(act, G["qe"], hd)
            act.activation(g_q[:, :], ps[:, 0, :], ACT.Copy, scale=float(P) ** -0.5).then_inc(G["q_taken"], 1)
            for j in range(2):
                if j == 0:
                    act.wait_ge(G["v0_made"], hd + 1)
                else:
                    act.wait_ge(w_used, c + 2)
                wait_past(act, G["out_made"], 4 * hd)
                act.activation(g_v[:, 2 * j:2 * j + 2, :],
                               ps[:, j, :].rearrange("p (a b) -> p a b", a=2), ACT.Copy)\
                   .then_inc(G["v_taken"], 1)
            for j in range(2):
                act.wait_ge(w_used, c + 3 + j)
                wait_past(act, G["hy2"], 2 * hd)
                act.activation(g_g[:, j, :], ps[:, j, :], ACT.Silu).then_inc(G["g_taken"], 1)
            log_exp(act)
            for lv, s_ in enumerate(LEVELS):
                n = (NL - 1) * hd + lv
                act.wait_ge(G["diff"], n + 1)
                wait_past(act, G["qs"], n)
                wait_past(act, G["ks"], n)
                d, e = bview(g_tmp[:, :], s_), bview(g_e[:, :], s_)
                act.activation(e[:, :, 0:s_], d[:, :, 0:s_], ACT.Exp, scale=-1.0 / GLA_TAU).then_inc(G["e"], 1)
                act.activation(e[:, :, s_:2 * s_], d[:, :, s_:2 * s_], ACT.Exp, scale=1.0 / GLA_TAU)\
                   .then_inc(G["e"], 1)
            wait_past(act, G["state"], 3 * hd)
            act.wait_ge(G["cum_taken"], hd + 1)
            act.wait_ge(G["qs"], (NL - 1) * (hd + 1))
            act.activation(g_e[:, :], g_cum[:, :], ACT.Exp, scale=1.0 / GLA_TAU).then_inc(G["eb"], 1)
            act.wait_ge(G["dlast"], hd + 1)
            act.activation(g_tmp[:, :], g_tmp[:, :], ACT.Exp, scale=1.0 / GLA_TAU).then_inc(G["elast"], 1)
            act.wait_ge(G["kt_turned"], hd + 1)
            wait_past(act, G["upd_made"], 3 * hd)
            act.activation(g_ktt[:, :], ps[:, 4, :], ACT.Copy).then_inc(G["ktt_taken"], 1)
            act.wait_ge(G["out_made"], 4 * hd + 4)
            wait_past(act, G["split"], 2 * hd)
            for dv in range(2):
                act.activation(g_y[:, dv, :], ps[:, 6 + dv, :], ACT.Square).then_inc(G["squared"], 1)
            act.wait_ge(G["summed"], 2 * hd + 2)
            act.activation(rstd[:, :], ps[:, 4, :], ACT.Ln, bias=eps[:, 0:1], scale=1.0 / 256)\
               .then_inc(G["hlogged"], 1)
            act.wait_ge(G["hlogged"], hd + 1)
            act.activation(rstd[:, :], rstd[:, :], ACT.Exp, scale=-0.5).then_inc(G["hrstd"], 1)
            for dv in range(2):
                act.wait_ge(G["hy2"], 2 * hd + dv + 1)
                act.activation(at_tile(oh, 2 * hd + dv), g_y[:, dv, :], ACT.Copy).then_inc(G["rounded"], 1)
        turns(act, 4, body)

    def gla_dve(dve):
        def body(hd):
            c = st_gla.base + 4 * hd
            dve.wait_ge(w_used, c + 1)
            wait_past(dve, G["kt_made"], hd)
            wait_past(dve, G["products"], NL * hd)
            dve.tensor_copy(g_k[:, :], ps[:, 1, :]).then_inc(G["k_taken"], 1)
            if isinstance(hd, int):
                dve.wait_ge(G["scanned"], 4)
                dve.wait_ge(G["zeroed"], 5)
            wait_past(dve, G["state"], 3 * hd)
            dve.tensor_copy(g_cum[:, :], at_tile(g_b, hd)).then_inc(G["cum_taken"], 1)
            dve.wait_ge(G["cum_taken"], hd + 1)
            dve.wait_ge(G["q_taken"], hd + 1)
            dve.wait_ge(G["k_taken"], hd + 1)
            wait_past(dve, G["out_made"], 4 * hd)

            def merge(lv):
                n = NL * hd + lv
                dve.wait_ge(G["products"], n + 1)
                wait_past(dve, G["merged"], n)
                stand_alone(dve.copy_predicated(
                    g_at[:, :].rearrange("p (a b) -> p a b", a=TB),
                    g_masks[:, lv:lv + 1, :].broadcast_to([P, TB, P]),
                    ps[:, 2 + lv % 2, :].rearrange("p (a b) -> p a b", a=TB)))\
                   .then_inc(G["merged"], 1)

            for lv, s_ in enumerate(LEVELS):
                n = (NL - 1) * hd + lv
                b = bview(g_cum[:, :], s_)
                ref = b[:, :, s_ - 1:s_].broadcast_to([P, TOK // (2 * s_), 2 * s_])
                wait_past(dve, G["e"], 2 * n)
                dve.tensor_tensor(bview(g_tmp[:, :], s_), b, ref, ALU.subtract).then_inc(G["diff"], 1)
                if lv > 0:
                    merge(lv - 1)
                dve.wait_ge(G["e"], 2 * n + 2)
                if lv >= 2:
                    dve.wait_ge(G["products"], NL * hd + lv - 1)
                e = bview(g_e[:, :], s_)
                dve.tensor_tensor(bview(KS[lv % 2][:, :], s_)[:, :, 0:s_], bview(g_k[:, :], s_)[:, :, 0:s_],
                                  e[:, :, 0:s_], ALU.mult).then_inc(G["ks"], 1)
                dve.tensor_tensor(bview(QS[lv % 2][:, :], s_)[:, :, s_:2 * s_],
                                  bview(g_q[:, :], s_)[:, :, s_:2 * s_], e[:, :, s_:2 * s_],
                                  ALU.mult).then_inc(G["qs"], 1)
            b4 = g_cum[:, :].rearrange("p (a b) -> p a b", a=TB)
            last4 = b4[:, :, P - 1:P].broadcast_to([P, TB, P])
            dve.wait_ge(G["e"], 2 * (NL - 1) * (hd + 1))
            dve.tensor_tensor(g_tmp[:, :].rearrange("p (a b) -> p a b", a=TB), last4, b4, ALU.subtract)\
               .then_inc(G["dlast"], 1)
            merge(NL - 2)
            dve.wait_ge(G["eb"], hd + 1)
            dve.tensor_tensor(g_qe[:, :], g_q[:, :], g_e[:, :], ALU.mult).then_inc(G["qe"], 1)
            merge(NL - 1)
            dve.wait_ge(G["elast"], hd + 1)
            dve.tensor_tensor(g_kt[:, :], g_k[:, :], g_tmp[:, :], ALU.mult).then_inc(G["kt_made"], 1)
            for t in range(TB - 1):
                dve.wait_ge(G["upd_made"], 3 * hd + t + 1)
                if t == 0:
                    dve.tensor_copy(g_s[:, :], ps[:, 5, 0:256]).then_inc(G["state"], 1)
                else:
                    dve.wait_ge(G["out_made"], 4 * hd + t + 1)
                    dve.wait_ge(G["state"], 3 * hd + t)
                    dve.scalar_tensor_tensor(out=g_s[:, :], in0=g_s[:, :],
                                             scalar=g_e[:, t * P + P - 1:t * P + P], in1=ps[:, 5, 0:256],
                                             op0=ALU.mult, op1=ALU.add).then_inc(G["state"], 1)
            dve.wait_ge(G["hrstd"], hd + 1)
            dve.wait_ge(G["g_taken"], 2 * hd + 2)
            for dv in range(2):
                g = GAINS["a_head"] + dv
                dve.scalar_tensor_tensor(out=g_y[:, dv, :], in0=ps[:, 6 + dv, :], scalar=gains[:, g:g + 1],
                                         in1=rstd[:, :], op0=ALU.mult, op1=ALU.mult).then_inc(G["hy"], 1)
            for dv in range(2):
                dve.wait_ge(G["hy"], 2 * hd + dv + 1)
                dve.tensor_tensor(g_y[:, dv, :], g_y[:, dv, :], g_g[:, dv, :], ALU.mult).then_inc(G["hy2"], 1)
            for dv in range(2):
                dve.wait_ge(G["rounded"], 2 * hd + dv + 1)
                to = at_tile(oh, 2 * hd + dv)
                dve.tensor_tensor(at_tile(ol, 2 * hd + dv), g_y[:, dv, :], to.bitcast(F32), ALU.subtract)\
                   .then_inc(G["split"], 1)
        turns(dve, 4, body)

    a_diff = attention("diff", "diff", st_diff, 8, 0.125, (f_q0, f_q1), (f_k0, f_k1), (f_v0, f_v1),
                       f_p, f_t, (f_causal, f_causal), 0)

    L = sems("lam", "loaded dots exped made")
    H = sems("hn", "squared summed logged rooted scaled rounded split")

    def lambda_act(act):
        wait_for(act, n_b.s["rstd"], 1)
        act.dma_start(f_lam[:, 0:256], dram["lambda_rows"]).then_inc(L["loaded"], 16)
        act.dma_start(f_causal[:, :], dram["tab_causal"]).then_inc(L["loaded"], 16)
        act.wait_ge(L["dots"], 2)
        act.activation(lam[:, 2:4], lam[:, 0:2], ACT.Exp).then_inc(L["exped"], 1)

    def lambda_dve(dve):
        dve.wait_ge(L["loaded"], 32)
        for j in range(2):
            dve.tensor_tensor_reduce(f_raw[:, j, 0:64], f_lam[:, 128 * j:128 * j + 64],
                                     f_lam[:, 128 * j + 64:128 * j + 128], 1.0, 0.0, ALU.mult, ALU.add,
                                     lam[:, j:j + 1]).then_inc(L["dots"], 1)
        dve.wait_ge(L["exped"], 1)
        dve.tensor_tensor(lam[:, 4:5], lam[:, 3:4], lam[:, 2:3], ALU.subtract).then_inc(L["made"], 1)
        dve.wait_ge(L["made"], 1)
        dve.tensor_scalar(lam[:, 7:8], lam[:, 4:5], -LAMBDA_INIT, None, ALU.add).then_inc(L["made"], 1)
        dve.tensor_scalar(lam[:, 5:6], gains[:, GAINS["b_head"]:GAINS["b_head"] + 1], 1.0 - LAMBDA_INIT,
                          None, ALU.mult).then_inc(L["made"], 1)
        dve.wait_ge(L["made"], 3)

    def headnorm_act(act):
        def square(t):
            wait_past(act, H["summed"], t - 1)
            act.activation(sq[:, t % 2, :], f_o[:, t, :], ACT.Square).then_inc(H["squared"], 1)

        act.wait_ge(a_diff.s["o_taken"], 8)
        square(0)
        for t in range(8):
            if t < 7:
                square(t + 1)
            act.wait_ge(H["summed"], t + 1)
            wait_past(act, H["scaled"], t - 1)
            act.activation(sq[:, 2 + t % 2, :], ps[:, t % 4, :], ACT.Ln, bias=eps[:, 0:1], scale=1.0 / P)\
               .then_inc(H["logged"], 1)
            act.wait_ge(H["logged"], t + 1)
            act.activation(sq[:, 2 + t % 2, :], sq[:, 2 + t % 2, :], ACT.Exp, scale=-0.5)\
               .then_inc(H["rooted"], 1)
            act.wait_ge(H["scaled"], t + 1)
            act.activation(xh[:, t, :], xf[:, t % 2, :], ACT.Copy).then_inc(H["rounded"], 1)

    def headnorm_pe(pe):
        for t in range(8):
            pe.wait_ge(H["squared"], t + 1)
            wait_past(pe, H["logged"], t - 3)
            pe.matmul(ps[:, t % 4, :], ones[:, :], sq[:, t % 2, :], start=True, stop=True)\
              .then_inc(H["summed"], 1)

    def headnorm_dve(dve):
        for t in range(8):
            dve.wait_ge(H["rooted"], t + 1)
            wait_past(dve, H["split"], t - 1)
            dve.scalar_tensor_tensor(out=xf[:, t % 2, :], in0=f_o[:, t, :], scalar=lam[:, 5:6],
                                     in1=sq[:, 2 + t % 2, :], op0=ALU.mult, op1=ALU.mult)\
               .then_inc(H["scaled"], 1)
            dve.wait_ge(H["rounded"], t + 1)
            dve.tensor_tensor(xl[:, t, :], xf[:, t % 2, :], xh[:, t, :].bitcast(F32), ALU.subtract)\
               .then_inc(H["split"], 1)



    def norm_of(*outs):
        return Norm(KD, hsrc, [(hi, lo, GAINS[g]) for hi, lo, g in outs])

    def halves(stages, ready, swiglu, kt):
        ups, downs = [], []
        for up, down in stages:
            ups.append(Up(up, ready, swiglu, prev=downs[-1] if downs else None))
            downs.append(Resid(down, kt, 1, (hidh, hidl), ups[-1].s["split"], prev=ups[-1]))
        return ups, downs

    n_ffn, n_mlp, u_ffn, r_ffn, u_mlp, r_mlp = [], [], [], [], [], []

    def add_ffn(layer):
        n_ffn.append(norm_of((xh, xl, f"ffn{layer}")))
        ups, downs = halves(st_ffn[2 * layer:2 * layer + 2], n_ffn[-1].s["split"], True, KF)
        u_ffn.extend(ups)
        r_ffn.extend(downs)

    def add_mlp(layer):
        n_mlp.append(norm_of((xh, xl, f"mlp{layer}")))
        ups, downs = halves(st_mlp[2 * layer:2 * layer + 2], n_mlp[-1].s["split"], False, KH)
        u_mlp.extend(ups)
        r_mlp.extend(downs)

    n_attn0 = norm_of((xh, xl, "attn0"))
    n_cq = Norm(2, lambda t: lraw[:, t, :], [(e_cqh, e_cql, GAINS["e_q"])])
    n_ck = Norm(1, lambda t: lraw[:, 2 + t, :], [(e_ckh, e_ckl, GAINS["e_kv"])])
    r_eout = Resid(st_eout, KD, 2, (oh, ol), a_dil.s["o_taken"], before=4)
    add_ffn(0)
    n_attn1 = norm_of((xh, xl, "attn1"))
    r_oout = Resid(st_oout, KD, 2, (oh, ol), a_swa.s["o_taken"])
    add_ffn(1)
    n_fin = Norm(KD, hsrc, [])
    n_a = norm_of((xh, xl, "a"))
    r_aout = Resid(st_aout, KD, 2, (oh, ol), G["split"])
    add_mlp(0)
    n_b = norm_of((xh, xl, "b"), (f_kh, f_kl, "kv"))
    r_bout = Resid(st_bout, KD, 2, (xh, xl), H["split"])
    add_mlp(1)

    CONSTS = 6

    @block.sync
    def _(sp):
        sp.dma_start(h[:, :, :], dram["x_t"].rearrange("p (a b) -> p a b", a=KD)).then_inc(x_loaded, 16)
        sp.dma_start(gains[:, :], dram["gains"]).then_inc(const_loaded, 16)
        sp.dma_start(ident[:, :], dram["ident"]).then_inc(const_loaded, 16)
        sp.dma_start(blockones[:, :], dram["blockones"]).then_inc(const_loaded, 16)
        sp.dma_start(e_causal[:, :], dram["tab_causal"]).then_inc(const_loaded, 16)
        sp.dma_start(e_ropeq[:, :], dram["rope_q"]).then_inc(const_loaded, 16)

        def load(entry, i, c, slot, uses, n):
            array, elems, first, step = entry
            wait_past(sp, w_split, c - 1)
            sp.dma_start(raw[slot][:, 0:elems], array[first + step * i]).then_inc(w_loaded[slot], 16)
        for st in ORDER:
            each_chunk(sp, st, load)
        wait_for(sp, r_mlp[3].added, KD)
        sp.dma_start(dram["out_t"].rearrange("p (a b) -> p a b", a=KD), h[:, :, :]).then_inc(out_stored, 16)
        sp.wait_ge(out_stored, 16)

    @block.gpsimd
    def _(pool):
        def split(entry, i, c, slot, uses, n):
            elems = entry[1]
            pool.wait_ge(w_loaded[slot], 16 * uses)
            wait_past(pool, w_used, c - 1)
            stand_alone(pool.tensor_scalar(wh[slot][:, 0:elems], raw[slot][:, 0:elems], 1.0, 1.0,
                                           ALU.mult, ALU.mult))\
                .then_inc(w_rounded, 1)
            pool.wait_ge(w_rounded, c + 1)
            pool.tensor_tensor(wl[slot][:, 0:elems], raw[slot][:, 0:elems],
                               wh[slot][:, 0:elems].bitcast(F32), ALU.subtract).then_inc(w_split, 1)
        for st in ORDER:
            each_chunk(pool, st, split)

    @block.tensor
    def _(pe):
        pe.wait_ge(consts_made, 2)
        pe.wait_ge(const_loaded, 80)
        norm_pe(pe, n_attn0)
        latents_pe(pe)
        norm_pe(pe, n_cq)
        norm_pe(pe, n_ck)
        att_pe(pe, a_mla, [(n_cq.s["split"], 2), (n_ck.s["split"], 1), (key_placed, 4)])
        att_pe(pe, a_dil, [])
        resid_pe(pe, r_eout)
        for layer in range(2):
            if layer == 1:
                norm_pe(pe, n_attn1)
                swa_kv_pe(pe)
                att_pe(pe, a_swa, [(kv_taken, 2)])
                resid_pe(pe, r_oout)
            norm_pe(pe, n_ffn[layer])
            for half in range(2):
                up_pe(pe, u_ffn[2 * layer + half])
                resid_pe(pe, r_ffn[2 * layer + half])
        norm_pe(pe, n_fin)
        norm_pe(pe, n_a)
        gla_gate_pe(pe)
        gla_pe(pe)
        resid_pe(pe, r_aout)
        for layer in range(2):
            if layer == 1:
                norm_pe(pe, n_b)
                att_pe(pe, a_diff, [(n_b.s["split"], 2 * KD)])
                headnorm_pe(pe)
                resid_pe(pe, r_bout)
            norm_pe(pe, n_mlp[layer])
            for half in range(2):
                up_pe(pe, u_mlp[2 * layer + half])
                resid_pe(pe, r_mlp[2 * layer + half])

    @block.scalar
    def _(act):
        act.wait_ge(consts_made, 2)
        act.wait_ge(const_loaded, 80)
        log_exp(act)
        norm_act(act, n_attn0, [(x_loaded, 16)])
        latents_act(act)
        norm_act(act, n_cq, [(lat["taken"], 3)])
        norm_act(act, n_ck, [])
        att_act(act, a_mla)
        att_act(act, a_dil)
        for layer in range(2):
            if layer == 1:
                norm_act(act, n_attn1, [(r_ffn[1].added, KD)])
                swa_kv_act(act)
                att_act(act, a_swa)
            norm_act(act, n_ffn[layer], [((r_eout, r_oout)[layer].added, 4)])
            for half in range(2):
                up_act(act, u_ffn[2 * layer + half])
            log_exp(act)
        norm_act(act, n_fin, [(r_ffn[3].added, KD)])
        norm_act(act, n_a, [(n_fin.s["scaled"], KD)])
        gla_gate_act(act)
        gla_act(act)
        for layer in range(2):
            if layer == 1:
                norm_act(act, n_b, [(r_mlp[1].added, KD)])
                lambda_act(act)
                att_act(act, a_diff)
                headnorm_act(act)
            norm_act(act, n_mlp[layer], [((r_aout, r_bout)[layer].added, 4)])
            for half in range(2):
                up_act(act, u_mlp[2 * layer + half])

    @block.vector
    def _(dve):
        dve.memset(ones[:, :], 1.0).then_inc(consts_made, 1)
        dve.memset(eps[:, :], EPS).then_inc(consts_made, 1)
        dve.wait_ge(const_loaded, 80)
        norm_dve(dve, n_attn0)
        latents_dve(dve)
        norm_dve(dve, n_cq)
        norm_dve(dve, n_ck)
        att_dve(dve, a_mla)
        att_dve(dve, a_dil)
        resid_dve(dve, r_eout)
        for layer in range(2):
            if layer == 1:
                norm_dve(dve, n_attn1)
                att_dve(dve, a_swa)
                resid_dve(dve, r_oout)
            norm_dve(dve, n_ffn[layer])
            for half in range(2):
                up_dve(dve, u_ffn[2 * layer + half])
                resid_dve(dve, r_ffn[2 * layer + half])
        final_dve(dve)
        norm_dve(dve, n_a)
        gla_gate_dve(dve)
        gla_dve(dve)
        resid_dve(dve, r_aout)
        for layer in range(2):
            if layer == 1:
                norm_dve(dve, n_b)
                lambda_dve(dve)
                att_dve(dve, a_diff)
                headnorm_dve(dve)
                resid_dve(dve, r_bout)
            norm_dve(dve, n_mlp[layer])
            for half in range(2):
                up_dve(dve, u_mlp[2 * layer + half])
                resid_dve(dve, r_mlp[2 * layer + half])


def panels(w, column_lists):
    out = []
    for cols in column_lists:
        part = w[:, cols]
        out.append(part.reshape(part.shape[0] // P, P, -1).transpose(1, 0, 2).reshape(P, -1))
    return np.ascontiguousarray(np.stack(out))


def shape_constants():
    f = np.float32
    pos = np.arange(TOK, dtype=f)
    inv = f(10000.0) ** (-np.arange(0, 32, 2, dtype=f) / f(32))
    ang = (pos[:, None] * inv[None, :]).astype(f)
    cos, sin = np.cos(ang).T.astype(f), np.sin(ang).T.astype(f)
    c32, s32 = np.concatenate([cos, cos]), np.concatenate([-sin, sin])
    rope_q = np.concatenate([np.ones((64, TOK), f), c32, s32])
    pad = np.zeros((64, TOK), f)
    rope_k = np.stack([np.concatenate([pad, c32, c32]), np.concatenate([pad, s32, s32])])
    q = np.arange(P)[:, None]
    off = q + TOK - P - np.arange(TOK)[None, :]
    causal = np.where(off >= 0, 0.0, MASKED).astype(f)
    count = (off <= 128).astype(int) + (off % 4 == 0) + (off % 16 == 0)
    logs = np.where((off >= 0) & (count > 0), np.log(np.maximum(count, 1)), 0.0)
    valid = (off >= 0) & (count > 0)
    dil = []
    for hd in range(8):
        slope = 2.0 ** (-(hd + 1))
        dil.append(np.where(valid, (logs - slope * off) * 8.0, MASKED))
    dil = np.stack(dil).reshape(4, 2, P, TOK).transpose(0, 2, 1, 3).reshape(4, P, 2 * TOK).astype(f)
    dist = q + P - np.arange(2 * P)[None, :]
    ok = (dist >= 0) & (dist < 128)
    swa = []
    for pair in range(8):
        for hd in (pair, pair + 8):
            swa.append(np.where(ok, -(2.0 ** (-8.0 * (hd + 1) / 16)) * dist * 8.0, MASKED))
    swa = np.stack(swa).reshape(8, 2, P, 2 * P).transpose(0, 2, 1, 3).reshape(8, P, 4 * P).astype(f)
    j, i = np.arange(P)[:, None], np.arange(P)[None, :]
    masks = [(j // (2 * s) == i // (2 * s)) & (j % (2 * s) < s) & (i % (2 * s) >= s) for s in LEVELS]
    masks.append(j == i)
    masks = np.stack(masks, 1).reshape(P, -1).astype(np.uint32)
    reset = np.ones((P, TOK), f)
    reset[:, ::P] = 0.0
    blocks = np.zeros((P, P), f)
    blocks[:64, :64] = 1.0
    blocks[64:, 64:] = 1.0
    return {"rope_q": rope_q, "rope_k": rope_k, "tab_causal": causal, "tab_dil": dil, "tab_swa": swa,
            "level_masks": masks, "scan_reset": reset, "ident": np.eye(P, dtype=f), "blockones": blocks}


def lay_out(v):
    a = {k: np.asarray(x) for k, x in v.items()}
    r = np.arange
    arrays = dict(shape_constants())
    arrays["x_t"] = np.ascontiguousarray(a["x"][0].T.reshape(KD, P, TOK).transpose(1, 0, 2).reshape(P, -1))

    w = a["e_w_in"][0]
    kr = r(384, 416)
    krs = np.concatenate([r(400, 416), r(384, 400)])
    arrays["w_e_in"] = panels(w, [r(256), np.concatenate([r(256, 384), kr, kr, krs, krs])])
    cols = []
    for pr in range(4):
        for hd in (2 * pr, 2 * pr + 1):
            b = hd * 96
            cols.append(np.concatenate([r(b, b + 96), r(b + 80, b + 96), r(b + 64, b + 80)]))
    arrays["w_e_uq"] = panels(a["e_w_uq"][0], [np.concatenate(cols[2 * i:2 * i + 2]) for i in range(4)])
    arrays["w_e_ukv"] = panels(a["e_w_ukv"][0], [r(256 * i, 256 * i + 256) for i in range(4)])
    q0, k0, v0 = 416, 416 + 512, 416 + 1024
    arrays["w_e_qk"] = panels(w, [np.concatenate([r(q0 + P * i, q0 + P * i + P), r(k0 + P * i, k0 + P * i + P)])
                                  for i in range(4)])
    arrays["w_e_v"] = panels(w, [r(v0 + P * i, v0 + P * i + P) for i in range(4)])

    def wide(m):
        return panels(m, [r(256 * i, 256 * i + 256) for i in range(m.shape[1] // 256)])
    arrays["w_e_out"] = wide(a["e_w_out"][0])
    gu, dn = [], []
    for layer in range(2):
        for half in range(2):
            s = half * HALF_FF
            gu.append(panels(a["f_w_gate_up"][layer],
                             [np.concatenate([r(s + P * i, s + P * i + P), r(FF + s + P * i, FF + s + P * i + P)])
                              for i in range(KF)]))
            dn.append(panels(a["f_w_down"][layer][s:s + HALF_FF], [r(P * i, P * i + P) for i in range(KD)]))
    arrays["w_f_gu"], arrays["w_f_dn"] = np.concatenate(gu), np.concatenate(dn)
    wo = a["o_w_qkv"][0]
    arrays["w_o_kv"] = panels(wo, [r(1024, 1280)])
    pair_cols = [np.concatenate([r(64 * i, 64 * i + 64), r(64 * (i + 8), 64 * (i + 8) + 64)]) for i in range(8)]
    arrays["w_o_q"] = panels(wo, pair_cols)
    arrays["w_o_out"] = wide(a["o_w_out"][0][np.concatenate(pair_cols)])
    wa = a["a_w_in_2"][0]
    z = np.zeros((D, P), np.float32)
    z[:, 0:16] = wa[:, 3072:3088]
    arrays["w_a_z"] = panels(z, [r(P)])
    arrays["w_a_qk"] = panels(wa, [np.concatenate([r(P * i, P * i + P), r(512 + P * i, 512 + P * i + P)])
                                   for i in range(4)])
    arrays["w_a_v"] = panels(wa, [r(1024 + 256 * i, 1280 + 256 * i) for i in range(4)])
    arrays["w_a_g"] = panels(wa, [r(2048 + P * i, 2048 + P * i + P) for i in range(8)])
    arrays["a_gate_up"] = np.ascontiguousarray(a["a_w_gate_up_2"][0])
    arrays["w_a_out"] = wide(a["a_w_out_2"][0])
    up, dn = [], []
    for layer in range(2):
        for half in range(2):
            s = half * HALF_HID
            up.append(wide(a["mlp_w1_2"][layer][:, s:s + HALF_HID]))
            dn.append(panels(a["mlp_w2_2"][layer][s:s + HALF_HID], [r(P * i, P * i + P) for i in range(KD)]))
    arrays["w_m_up"], arrays["w_m_dn"] = np.concatenate(up), np.concatenate(dn)
    both = np.concatenate([a["b_w_q_2"][0], a["w_kv_2"]], axis=1)
    arrays["w_b_qk"] = panels(both, [np.concatenate([r(P * i, P * i + P), r(1024 + P * i, 1024 + P * i + P)])
                                     for i in range(8)])
    arrays["w_b_v"] = panels(both, [r(2048 + P * i, 2048 + P * i + P) for i in range(8)])
    arrays["w_b_out"] = wide(a["b_w_out_2"][0])

    def tiles(vec):
        return vec.reshape(-1, P).T

    def twice(vec):
        return np.concatenate([vec, vec])[:, None]
    sinks = a["o_sinks"][0][np.stack([r(8), r(8) + 8], 1).reshape(-1)]
    parts = {
        "attn0": tiles(a["attn_norm"][0]), "attn1": tiles(a["attn_norm"][1]),
        "ffn0": tiles(a["ffn_norm"][0]), "ffn1": tiles(a["ffn_norm"][1]), "final": tiles(a["final_norm"]),
        "e_q": tiles(a["e_q_norm"][0]), "e_kv": tiles(a["e_kv_norm"][0]), "a": tiles(a["a_norm_2"][0]),
        "a_head": tiles(a["a_head_norm_2"][0]), "kv": tiles(a["kv_norm_2"]), "k": twice(a["k_norm_2"]),
        "b": tiles(a["b_norm_2"][0]), "q": twice(a["b_q_norm_2"][0]), "b_head": tiles(a["b_head_norm_2"][0]),
        "mlp0": tiles(a["mlp_norm_2"][0]), "mlp1": tiles(a["mlp_norm_2"][1]), "b_gate": tiles(a["a_b_gate_2"][0]),
        "sinks": np.broadcast_to(sinks[None, :], (P, 16)),
    }
    arrays["gains"] = np.ascontiguousarray(np.concatenate([parts[n] for n in GAINS], axis=1))
    arrays["lambda_rows"] = np.ascontiguousarray(np.broadcast_to(a["b_lambda_2"][0].reshape(1, -1), (P, 256)))
    return arrays


def kernel(**inputs):
    import concourse.bacc as bacc
    from concourse.bass_utils import run_bass_kernel_spmd

    arrays = lay_out(inputs)
    nc = bacc.Bacc("TRN2", target_bir_lowering=False, num_devices=1)
    dram = {n: nc.dram_tensor("in_" + n, list(x.shape), mybir.dt.from_np(x.dtype), kind="ExternalInput").ap()
            for n, x in arrays.items()}
    dram["out_t"] = nc.dram_tensor("out_t", [P, KD * TOK], F32, kind="ExternalOutput").ap()
    build(nc, dram)
    got = run_bass_kernel_spmd(nc, [{"in_" + n: x for n, x in arrays.items()}], core_ids=[0]).results[0]["out_t"]
    return np.ascontiguousarray(got.reshape(P, KD, TOK).transpose(1, 0, 2).reshape(D, TOK).T)[None]
```

```python
from contextlib import ExitStack

import numpy as np

import concourse.bass as bass
from concourse import mybir

F32 = mybir.dt.float32
F32R = mybir.dt.float32r
U32 = mybir.dt.uint32
ACT = mybir.ActivationFunctionType
ALU = mybir.AluOpType

P = 128
TOK = 512
TB = TOK // P
D = 1024
KD = D // P
EPS = 1e-6
FF = 2816
HALF_FF = FF // 2
KF = HALF_FF // P
HID = 4096
HALF_HID = HID // 2
KH = HALF_HID // P
MASKED = -1e30
LAMBDA_INIT = 0.8 - 0.6 * float(np.exp(-0.3))
GLA_TAU = 16.0
SLOT = KD * 256
LEVELS = (64, 32, 16, 8, 4, 2, 1)

GAINS = {}
_at = 0
for _name, _n in (("attn0", 8), ("attn1", 8), ("ffn0", 8), ("ffn1", 8), ("final", 8), ("e_q", 2),
                  ("e_kv", 1), ("a", 8), ("a_head", 2), ("kv", 8), ("k", 1), ("b", 8), ("q", 1),
                  ("b_head", 1), ("mlp0", 8), ("mlp1", 8), ("b_gate", 4), ("sinks", 16)):
    GAINS[_name] = _at
    _at += _n
NGAINS = _at


CAUSAL_AT = [P * i * (i + 1) // 2 for i in range(TB + 1)]


class Stage:

    def __init__(self, base, iters, body, tail=()):
        self.base, self.iters, self.body, self.tail = base, iters, body, tail
        self.step = len(body)
        self.count = iters * len(body) + len(tail)
        assert iters == 1 or self.step % 2 == 0


def same(base, array, elems, n, first=0):
    if n == 1:
        return Stage(base, 1, [(array, elems, first, 0)])
    tail = [(array, elems, first + n - 1, 0)] if n % 2 else []
    return Stage(base, n // 2, [(array, elems, first, 2), (array, elems, first + 1, 2)], tail)


def turns(eng, iters, body):
    body(0)
    if iters > 1:
        with eng.Fori(1, iters) as i:
            body(i)


def each_chunk(eng, st, fn):
    def body(i):
        for u, entry in enumerate(st.body):
            fn(entry, i, st.base + st.step * i + u, (st.base + u) % 2,
               (st.base + u) // 2 + (st.step // 2) * i + 1 if st.iters > 1 else (st.base + u) // 2 + 1,
               st.step * i + u)
    turns(eng, st.iters, body)
    for u, entry in enumerate(st.tail):
        c = st.base + st.iters * st.step + u
        fn(entry, 0, c, c % 2, c // 2 + 1, c - st.base)


class Mark:

    def __init__(self, sem, base):
        self.sem, self.base = sem, base


def wait_for(eng, mark, value):
    if isinstance(mark, Mark):
        eng.wait_ge(mark.sem, value + mark.base)
    else:
        eng.wait_ge(mark, value)


def wait_past(eng, mark, value):
    if not isinstance(value, int) or value > 0:
        wait_for(eng, mark, value)


def build(nc, dram):
    with ExitStack() as ctx:
        _build(nc, dram, ctx)


def _build(nc, dram, ctx):
    chunks = 0
    ORDER = []

    def stage(make, *args):
        nonlocal chunks
        st = make(chunks, *args)
        ORDER.append(st)
        chunks += st.count
        return st

    W = dram
    st_ein = stage(same, W["w_e_in"], KD * 256, 2)
    st_dilv = stage(same, W["w_e_v"], KD * 256, 2)
    st_mla = stage(Stage, 4, [(W["w_e_uq"], 512, 0, 1), (W["w_e_ukv"], 256, 0, 1)])
    st_dil = stage(same, W["w_e_qk"], KD * 256, 4)
    st_eout = stage(same, W["w_e_out"], KD * 256, 4)
    st_ffn = []
    for layer in range(2):
        if layer == 1:
            st_okv = stage(same, W["w_o_kv"], KD * 256, 1)
            st_swa = stage(same, W["w_o_q"], KD * P, 8)
            st_oout = stage(same, W["w_o_out"], KD * 256, 4)
        for half in range(2):
            up = stage(same, W["w_f_gu"], KD * 256, KF, (2 * layer + half) * KF)
            down = stage(same, W["w_f_dn"], KF * P, KD, (2 * layer + half) * KD)
            st_ffn.append((up, down))
    st_z = stage(same, W["w_a_z"], KD * P, 1)
    st_gla = stage(Stage, 4, [(W["w_a_qk"], KD * 256, 0, 1), (W["w_a_v"], KD * 256, 0, 1),
                              (W["w_a_g"], KD * P, 0, 2), (W["w_a_g"], KD * P, 1, 2)])
    st_aout = stage(same, W["w_a_out"], KD * 256, 4)
    st_mlp = []
    for layer in range(2):
        if layer == 1:
            st_dv = stage(same, W["w_b_v"], KD * 256, 4)
            st_diff = stage(same, W["w_b_qk"], KD * 256, 8)
            st_bout = stage(same, W["w_b_out"], KD * 256, 4)
        for half in range(2):
            up = stage(same, W["w_m_up"], KD * 256, KH // 2, (2 * layer + half) * KH // 2)
            down = stage(same, W["w_m_dn"], KH * P, KD, (2 * layer + half) * KD)
            st_mlp.append((up, down))

    def sb(name, shape, dt=F32):
        return ctx.enter_context(nc.sbuf_tensor(name, shape, dt))

    def sem(name):
        return ctx.enter_context(nc.semaphore(name))

    h = sb("h", [P, KD, TOK])
    xh = sb("xh", [P, KD, TOK], F32R)
    xl = sb("xl", [P, KD, TOK], F32R)
    raw = [sb(f"raw{i}", [P, SLOT]) for i in range(2)]
    wh = [sb(f"wh{i}", [P, SLOT], F32R) for i in range(2)]
    wl = [sb(f"wl{i}", [P, SLOT], F32R) for i in range(2)]
    sq = sb("sq", [P, 4, TOK])
    rstd = sb("rstd", [P, TOK])
    xf = sb("xf", [P, 2, TOK])
    gains = sb("gains", [P, NGAINS])
    ident = sb("ident", [P, P])
    ones = sb("ones", [P, P])
    blockones = sb("blockones", [P, P])
    eps = sb("eps", [P, 1])
    small = sb("small", [P, 64])

    arena_base = (nc.sbuf_base + 63) // 64 * 64

    def area(name, specs, start=arena_base):
        at, out = start, []
        for n, shape, dt in specs:
            size = int(np.prod(shape[1:])) * 4
            out.append(nc.alloc_sbuf_tensor_at(f"{name}_{n}", list(shape), dt, offset=at))
            at += (size + 63) // 64 * 64
        assert at <= nc.sbuf_usable_end, (name, at, nc.sbuf_usable_end)
        return out, at

    (oh, ol), arena_rest = area("mix", [("oh", (P, KD, TOK), F32R), ("ol", (P, KD, TOK), F32R)])
    (d_v,), arena_heads = area("dilv", [("v", (P, 4, TOK), F32)], arena_rest)
    (e_cqh, e_cql, e_ckh, e_ckl, e_q0, e_q1, e_k0, e_k1, e_v0, e_v1, e_p, e_t0, e_causal, e_ropeq), _ = area("mla", [
         ("cqh", (P, 2, TOK), F32R), ("cql", (P, 2, TOK), F32R),
         ("ckh", (P, 1, TOK), F32R), ("ckl", (P, 1, TOK), F32R),
         ("q0", (P, 2, TOK), F32), ("q1", (P, 2, TOK), F32),
         ("k0", (P, 2, TOK), F32), ("k1", (P, 2, TOK), F32),
         ("v0", (P, TB, P), F32), ("v1", (P, TB, P), F32),
         ("p", (P, 2, CAUSAL_AT[-1]), F32), ("t0", (P, TB, TOK), F32),
         ("causal", (P, TOK), F32), ("ropeq", (P, TOK), F32)], arena_heads)
    (d_q0, d_q1, d_k0, d_k1, d_p, d_t0, d_b0, d_b1), _ = area("dil", [
        ("q0", (P, TOK), F32), ("q1", (P, TOK), F32), ("k0", (P, TOK), F32), ("k1", (P, TOK), F32),
        ("p", (P, 2, CAUSAL_AT[-1]), F32), ("t0", (P, TB, TOK), F32),
        ("b0", (P, 2, TOK), F32), ("b1", (P, 2, TOK), F32)], arena_heads)
    (s_q0, s_q1, s_k, s_v, s_p, s_t0, s_b0, s_b1, s_neg0, s_neg1, s_es), _ = area("swa", [
        ("q0", (P, TOK), F32), ("q1", (P, TOK), F32), ("k", (P, TOK), F32), ("v", (P, TB, P), F32),
        ("p", (P, 2, CAUSAL_AT[-1]), F32), ("t0", (P, TB, TOK), F32),
        ("b0", (P, 2, 256), F32), ("b1", (P, 2, 256), F32), ("neg0", (P, 2), F32),
        ("neg1", (P, 2), F32), ("es", (P, 8), F32)], arena_rest)
    (hidh, hidl), _ = area("ffn", [("hidh", (P, KH, TOK), F32R), ("hidl", (P, KH, TOK), F32R)])
    (g_b, g_q0, g_q1, g_k0, g_k1, g_v0, g_v1, g_g0, g_g1, g_tmp0, g_tmp1, g_e0, g_e1,
     g_ks0, g_ks1, g_qs0, g_qs1, g_at, g_masks, g_cum0, g_cum1), _ = area("gla", [
         ("b", (P, 4, TOK), F32),
         ("q0", (P, TOK), F32), ("q1", (P, TOK), F32), ("k0", (P, TOK), F32), ("k1", (P, TOK), F32),
         ("v0", (P, TB, 256), F32), ("v1", (P, TB, 256), F32),
         ("g0", (P, 2, TOK), F32), ("g1", (P, 2, TOK), F32), ("tmp0", (P, TOK), F32),
         ("tmp1", (P, TOK), F32), ("e0", (P, TOK), F32), ("e1", (P, TOK), F32),
         ("ks0", (P, TOK), F32), ("ks1", (P, TOK), F32), ("qs0", (P, TOK), F32),
         ("qs1", (P, TOK), F32), ("at", (P, TOK), F32), ("masks", (P, 8, P), U32),
         ("cum0", (P, TOK), F32), ("cum1", (P, TOK), F32)], arena_rest)
    g_qe, g_kt, g_ktt, g_s, g_y = sq[:, 0, :], sq[:, 1, :], sq[:, 2, :], sq[:, 3, 0:256], xf
    g_z, g_wg, g_reset = g_e0[0:16, :], g_tmp0[0:16, :], g_e1
    (f_kh, f_kl, f_vo, f_q0, f_q1, f_k0, f_k1, f_v, f_p, f_pt), _ = area("diff", [
        ("kh", (P, KD, TOK), F32R), ("kl", (P, KD, TOK), F32R), ("vo", (P, KD, TOK), F32),
        ("q0", (P, TOK), F32), ("q1", (P, TOK), F32), ("k0", (P, TOK), F32), ("k1", (P, TOK), F32),
        ("v", (P, TOK), F32), ("p", (P, 3, CAUSAL_AT[-1]), F32), ("pt", (P, TB, TOK), F32)])
    f_causal, f_raw, f_lam = rstd, xf, f_p[:, 2, 0:256]

    rsum, rinv, nmax, lamr = small[:, 0:8], small[:, 8:16], small[:, 16:24], small[:, 24:28]
    lam = small[:, 32:40]
    kc_tab, ks_tab = xf[:, 0, :], xf[:, 1, :]

    ps = ctx.enter_context(nc.psum_tensor("ps", [P, 8, TOK], F32))
    A0, A1, T_BANK, O_BANK = 0, 1, 5, 7
    S_BANK = ((2, 3, 4, 2), (3, 4, 2, 3))

    w_loaded = [sem("w_loaded0"), sem("w_loaded1")]
    w_rounded = sem("w_rounded")
    w_split = sem("w_split")
    w_used = sem("w_used")
    x_loaded = [sem(f"x_loaded{i}") for i in range(4)]
    const_loaded = sem("const_loaded")
    consts_made = sem("consts_made")
    out_stored = sem("out_stored")

    def sems(tag, names):
        return {n: sem(f"{tag}_{n}") for n in names.split()}

    block = ctx.enter_context(nc.Block())

    def log_exp(act):
        act.preload_act_table_set("natural_log_exp_and_others")

    def stand_alone(ins):
        return ins.wait_op(consts_made, 2, "sem-ge")

    def mm3(pe, out, sh, sl, mh, ml, start, stop):
        pe.matmul(out, sh, mh, start=start, stop=False)
        pe.matmul(out, sh, ml, start=False, stop=False)
        return pe.matmul(out, sl, mh, start=False, stop=stop)

    def chunk_w(slot, kt, cols):
        n = kt * cols
        return (wh[slot][:, 0:n].rearrange("p (k n) -> p k n", k=kt),
                wl[slot][:, 0:n].rearrange("p (k n) -> p k n", k=kt))

    norm_sems = sems("norm", "squared summed totaled logged rstd scaled rounded split")
    resid_sems = sems("resid", "added")
    up_sems = sems("up", "acted made rounded split")
    counted = {}

    def marks(group, adds):
        out = {}
        for name, n in adds.items():
            key = (id(group), name)
            out[name] = Mark(group[name], counted.get(key, 0))
            counted[key] = counted.get(key, 0) + n
        return out

    class Norm:
        def __init__(self, nt, src, outs, after=None):
            n = nt * max(1, len(outs))
            steps = (after.st.count, after.st.count - 2, 2 * after.nt) if after else (nt, nt, 0)
            self.s = marks(norm_sems, dict(squared=steps[0], summed=steps[1], totaled=steps[2], logged=1,
                                           rstd=1, scaled=n, rounded=nt * len(outs), split=nt * len(outs)))
            self.after, self.pieces, self.made = after, None, None
            if after:
                after.norm = self
            self.nt, self.src = nt, src
            self.outs, self.bank = outs, T_BANK

    def norm_act(act, N, ready):
        s = N.s
        for sm, v in ready:
            wait_for(act, sm, v)
        if N.after:
            R = N.after

            def square(entry, i, c, slot, uses, n):
                first = isinstance(n, int) and n == 0
                wait_for(act, R.added, n + 1)
                if not first:
                    wait_past(act, s["summed"], n - 1)
                x = h[:, 0:R.nt, :] if first else h[:, bass.ds(n * R.nt, R.nt), :]
                act.activation(sq[:, 2:2 + R.nt, :] if first else sq[:, 0:R.nt, :], x, ACT.Square)\
                   .then_inc(s["squared"].sem, 1)
            each_chunk(act, R.st, square)
            wait_for(act, s["totaled"], 2 * R.nt)
        else:
            for t in range(N.nt):
                if N.pieces and t % 2 == 0:
                    act.wait_ge(N.pieces[t // 2], 16)
                if N.made:
                    wait_for(act, N.made, t + 1)
                if t >= 4:
                    wait_for(act, s["summed"], t - 3)
                act.activation(sq[:, t % 4, :], N.src(t), ACT.Square).then_inc(s["squared"].sem, 1)
            wait_for(act, s["summed"], N.nt)
        act.activation(rstd[:, :], ps[:, N.bank, :], ACT.Ln, bias=eps[:, 0:1],
                       scale=1.0 / (N.nt * P)).then_inc(s["logged"].sem, 1)
        wait_for(act, s["logged"], 1)
        act.activation(rstd[:, :], rstd[:, :], ACT.Exp, scale=-0.5).then_inc(s["rstd"].sem, 1)
        m = 0
        for high, _, _ in N.outs:
            for t in range(N.nt):
                m += 1
                wait_for(act, s["scaled"], m)
                act.activation(high[:, t, :], xf[:, (m - 1) % 2, :], ACT.Copy).then_inc(s["rounded"].sem, 1)

    def norm_dve(dve, N, ready=()):
        s = N.s
        for sm, v in ready:
            wait_for(dve, sm, v)
        wait_for(dve, s["rstd"], 1)
        if s["split"].base:
            wait_for(dve, s["split"], 0)
        todo = [(hi, lo, g, t) for hi, lo, g in N.outs for t in range(N.nt)]

        def scale(m):
            _, _, g, t = todo[m]
            if m >= 2:
                wait_for(dve, s["split"], m - 1)
            dve.scalar_tensor_tensor(out=xf[:, m % 2, :], in0=N.src(t), scalar=gains[:, g + t:g + t + 1],
                                     in1=rstd[:, :], op0=ALU.mult, op1=ALU.mult).then_inc(s["scaled"].sem, 1)

        scale(0)
        for m, (hi, lo, g, t) in enumerate(todo):
            if m + 1 < len(todo):
                scale(m + 1)
            wait_for(dve, s["rounded"], m + 1)
            dve.tensor_tensor(lo[:, t, :], xf[:, m % 2, :], hi[:, t, :].bitcast(F32),
                              ALU.subtract).then_inc(s["split"].sem, 1)

    def norm_pe(pe, N):
        s = N.s
        if N.after:
            R = N.after
            wait_for(pe, s["summed"], R.st.count - 2)
            for j in range(R.nt):
                pe.matmul(ps[:, N.bank, :], ones[:, :], sq[:, 2 + j, :], start=(j == 0),
                          stop=False).then_inc(s["totaled"].sem, 1)
            wait_for(pe, s["squared"], R.st.count)
            for j in range(R.nt):
                pe.matmul(ps[:, N.bank, :], ones[:, :], sq[:, j, :], start=False,
                          stop=(j == R.nt - 1)).then_inc(s["totaled"].sem, 1)
            return
        for t in range(N.nt):
            wait_for(pe, s["squared"], t + 1)
            pe.matmul(ps[:, N.bank, :], ones[:, :], sq[:, t % 4, :], start=(t == 0),
                      stop=(t == N.nt - 1)).then_inc(s["summed"].sem, 1)

    class Resid:
        def __init__(self, st, kt, nt, xs, ready, before=0, prev=None):
            self.st, self.kt, self.nt, self.xs, self.ready = st, kt, nt, xs, ready
            self.added = marks(resid_sems, dict(added=st.count))["added"]
            self.before, self.prev, self.read, self.per = before, prev, self.added, 1
            self.norm = None

        def pair(self, slot):
            return (slot + self.st.base) % 2 if self.nt == 2 else slot

    def banks_read(pe, X, n):
        if isinstance(n, int) and n < 2:
            if X.prev:
                wait_for(pe, X.prev.read, X.prev.per * (X.prev.st.count + n - 1))
        else:
            wait_for(pe, X.read, X.per * (n - 1))

    def resid_tile(pe, R, slot, k):
        w_h, w_l = chunk_w(slot, R.kt, R.nt * P)
        for j in range(R.nt):
            last = mm3(pe, ps[:, 2 * R.pair(slot) + j, :], w_h[:, k, j * P:(j + 1) * P],
                       w_l[:, k, j * P:(j + 1) * P], R.xs[0][:, k, :], R.xs[1][:, k, :],
                       k == 0, k == R.kt - 1)
        return last

    def resid_first(pe, R, k):
        c = R.st.base
        if k == 0:
            pe.wait_ge(w_split, c + 1)
            banks_read(pe, R, 0)
        wait_for(pe, R.ready, max(1, k + 1 - R.before))
        return resid_tile(pe, R, c % 2, k)

    def resid_pe(pe, R, done=0, between={}):
        def one(entry, i, c, slot, uses, n):
            if isinstance(n, int) and n == 0:
                for k in range(done, R.kt):
                    between.get(k, lambda: None)()
                    last = resid_first(pe, R, k)
            else:
                pe.wait_ge(w_split, c + 1)
                banks_read(pe, R, n)
                for k in range(R.kt):
                    last = resid_tile(pe, R, slot, k)
            last.then_inc(w_used, 1)
        each_chunk(pe, R.st, one)

    def resid_dve(dve, R):
        def one(entry, i, c, slot, uses, n):
            par = R.pair(slot)
            if R.norm and not (isinstance(n, int) and n < 2):
                s = R.norm.s
                wait_for(dve, s["squared"], n)
                wait_past(dve, s["summed"], n - 2)
                dve.tensor_tensor(sq[:, 2:2 + R.nt, :], sq[:, 2:2 + R.nt, :], sq[:, 0:R.nt, :],
                                  ALU.add).then_inc(s["summed"].sem, 1)
            dve.wait_ge(w_used, c + 1)
            to = h[:, bass.ds(n * R.nt, R.nt), :] if not isinstance(n, int) else h[:, n * R.nt:(n + 1) * R.nt, :]
            dve.tensor_tensor(to, to, ps[:, 2 * par:2 * par + R.nt, :], ALU.add).then_inc(R.added.sem, 1)
        each_chunk(dve, R.st, one)

    class Up:
        def __init__(self, st, ready, swiglu, prev=None):
            self.st, self.ready, self.swiglu, self.prev = st, ready, swiglu, prev
            n = st.count * (1 if swiglu else 2)
            self.s = marks(up_sems, dict(acted=n, made=n, rounded=n, split=n))
            self.read, self.per = (self.s["made"], 1) if swiglu else (self.s["acted"], 2)

    def at_tile(buf, n):
        return buf[:, n, :] if isinstance(n, int) else buf[:, bass.ds(n, 1), :].rearrange("p a t -> p (a t)")

    def up_pe(pe, U):
        def one(entry, i, c, slot, uses, n):
            w_h, w_l = chunk_w(slot, KD, 256)
            par = slot
            pe.wait_ge(w_split, c + 1)
            banks_read(pe, U, n)
            for k in range(KD):
                if isinstance(n, int) and n == 0:
                    wait_for(pe, U.ready, k + 1)
                for j in range(2):
                    last = mm3(pe, ps[:, 2 * par + j, :], w_h[:, k, j * P:(j + 1) * P],
                               w_l[:, k, j * P:(j + 1) * P], xh[:, k, :], xl[:, k, :], k == 0, k == KD - 1)
            last.then_inc(w_used, 1)
        each_chunk(pe, U.st, one)

    def up_act(act, U):
        s = U.s

        def one(entry, i, c, slot, uses, n):
            par = slot
            act.wait_ge(w_used, c + 1)
            if U.swiglu:
                wait_past(act, s["made"], n - 1)
                act.activation(sq[:, par, :], ps[:, 2 * par, :], ACT.Silu).then_inc(s["acted"].sem, 1)
                wait_for(act, s["made"], n + 1)
                act.activation(at_tile(hidh, n), sq[:, 2 + par, :], ACT.Copy).then_inc(s["rounded"].sem, 1)
            else:
                for j in range(2):
                    wait_past(act, s["made"], 2 * n + j - 1)
                    act.activation(sq[:, j, :], ps[:, 2 * par + j, :], ACT.Relu).then_inc(s["acted"].sem, 1)
                for j in range(2):
                    wait_for(act, s["made"], 2 * n + j + 1)
                    act.activation(at_tile(hidh, 2 * n + j), sq[:, 2 + j, :], ACT.Copy).then_inc(s["rounded"].sem, 1)
        each_chunk(act, U.st, one)

    def up_dve(dve, U):
        s = U.s

        def one(entry, i, c, slot, uses, n):
            par = slot
            if U.swiglu:
                wait_for(dve, s["acted"], n + 1)
                wait_past(dve, s["split"], n - 1)
                dve.tensor_tensor(sq[:, 2 + par, :], sq[:, par, :], ps[:, 2 * par + 1, :],
                                  ALU.mult).then_inc(s["made"].sem, 1)
                wait_for(dve, s["rounded"], n + 1)
                dve.tensor_tensor(at_tile(hidl, n), sq[:, 2 + par, :], at_tile(hidh, n).bitcast(F32),
                                  ALU.subtract).then_inc(s["split"].sem, 1)
            else:
                for j in range(2):
                    wait_for(dve, s["acted"], 2 * n + j + 1)
                    wait_past(dve, s["split"], 2 * n + j - 1)
                    dve.tensor_tensor(sq[:, 2 + j, :], sq[:, j, :], sq[:, j, :], ALU.mult).then_inc(s["made"].sem, 1)
                for j in range(2):
                    wait_for(dve, s["rounded"], 2 * n + j + 1)
                    dve.tensor_tensor(at_tile(hidl, 2 * n + j), sq[:, 2 + j, :],
                                      at_tile(hidh, 2 * n + j).bitcast(F32), ALU.subtract).then_inc(s["split"].sem, 1)
        each_chunk(dve, U.st, one)

    hsrc = lambda t: h[:, t, :]

    lat = sems("lat", "taken roped")
    lraw = e_t0
    k_rot = e_p[:, :, :].rearrange("p a b -> p (a b)")[:, 0:3 * TOK].rearrange("p (a b) -> p a b", a=3)

    def latents_pe(pe):
        for n in range(2):
            c = st_ein.base + n
            w_h, w_l = chunk_w(c % 2, KD, 256)
            pe.wait_ge(w_split, c + 1)
            for k in range(KD):
                if n == 0:
                    wait_for(pe, n_attn0.s["split"], k + 1)
                for bank, col in ((0, 0), (1, P)) if n == 0 else ((2, 0), (3, 64), (4, P)):
                    last = mm3(pe, ps[:, bank, :], w_h[:, k, col:col + P], w_l[:, k, col:col + P],
                               xh[:, k, :], xl[:, k, :], k == 0, k == KD - 1)
            last.then_inc(w_used, 1)

    def dil_values_pe(pe, n, middle=lambda: None):
        c = st_dilv.base + n
        w_h, w_l = chunk_w(c % 2, KD, 256)
        pe.wait_ge(w_split, c + 1)
        if n == 1:
            pe.wait_ge(lat["taken"], 2)
        for t in range(TB):
            if t == 2:
                middle()
            for k in range(KD):
                last = mm3(pe, ps[:, (6, 0)[n] + t // 2, (t % 2) * 256:(t % 2) * 256 + 256],
                           xh[:, k, t * P:(t + 1) * P], xl[:, k, t * P:(t + 1) * P],
                           w_h[:, k, :], w_l[:, k, :], k == 0, k == KD - 1)
        last.then_inc(w_used, 1)

    def dil_values_act(act, n):
        act.wait_ge(w_used, st_dilv.base + n + 1)
        b = (6, 0)[n]
        for j in range(2):
            act.activation(d_v[:, 2 * n + j, :].rearrange("p (a b) -> p a b", a=TB),
                           ps[:, b:b + 2, :].rearrange("p c (t d) -> p (c t) d", t=2)[:, :, j * P:(j + 1) * P],
                           ACT.Copy).then_inc(dil_values, 1)

    dil_values = sem("dil_values")

    def latents_act(act):
        act.wait_ge(w_used, st_ein.base + 1)
        for t in range(2):
            act.activation(lraw[:, t, :], ps[:, t, :], ACT.Copy).then_inc(lat["taken"], 1)
        act.wait_ge(w_used, st_ein.base + 2)
        act.activation(lraw[:, 2, :], ps[:, 2, :], ACT.Copy).then_inc(lat["taken"], 1)
        wait_for(act, n_attn0.s["split"], KD)
        act.dma_start(kc_tab, dram["rope_k"][0]).then_inc(rope_loaded, 16)
        act.dma_start(ks_tab, dram["rope_k"][1]).then_inc(rope_loaded, 16)
        act.wait_ge(lat["roped"], 3)
        for kbuf in (e_k0, e_k1):
            for hh in range(2):
                act.activation(kbuf[64:P, hh, :], k_rot[64:P, 2, :], ACT.Copy).then_inc(key_placed, 1)

    def latents_dve(dve):
        dve.wait_ge(w_used, st_ein.base + 2)
        dve.wait_ge(rope_loaded, 32)
        for t, tab in enumerate((kc_tab, ks_tab)):
            dve.tensor_tensor(k_rot[64:P, t, :], ps[64:P, 3 + t, :], tab[64:P, :],
                              ALU.mult).then_inc(lat["roped"], 1)
        dve.wait_ge(lat["roped"], 2)
        dve.tensor_tensor(k_rot[64:P, 2, :], k_rot[64:P, 0, :], k_rot[64:P, 1, :],
                          ALU.add).then_inc(lat["roped"], 1)

    rope_loaded = sem("rope_loaded")
    key_placed = sem("key_placed")

    ATT_ALL = ("q_made q_staged k_staged v_staged scored masked exped inverted normed turned pt_copied pv_done "
           "o_rounded o_taken")
    ATT_MORE = {"mla": "", "dil": " tab_loaded0 tab_loaded1", "swa": " tab_loaded0 tab_loaded1 es"}

    class Att:
        pass

    def attention(tag, kind, st, pairs, scale, q, k, v, p, pt, tab, first_out):
        A = Att()
        A.kind, A.st, A.pairs, A.scale, A.first_out = kind, st, pairs, scale, first_out
        A.q, A.k, A.v, A.p, A.pt, A.tab = q, k, v, p, pt, tab
        A.s = sems(tag, ATT_ALL + ATT_MORE[kind])
        return A

    CAUSAL = [(0, (i + 1) * P) for i in range(TB)]
    BAND = [(max(i - 1, 0) * P, (i + 1) * P) for i in range(TB)]

    def span(A, i):
        return BAND[i] if A.kind == "swa" else CAUSAL[i]

    def probs(A, hh, i):
        a, b = span(A, i)
        return A.p[:, hh, CAUSAL_AT[i]:CAUSAL_AT[i] + b - a]

    def heads_v(A, p, st, j):
        if A.kind == "dil":
            return A.v[:, p, j * P:(j + 1) * P]
        return A.v[st][:, j, :]

    def heads_q(A, st, hh, i):
        if A.kind == "mla":
            return A.q[st][:, hh, i * P:(i + 1) * P]
        return A.q[st][64 * hh:64 * hh + 64, i * P:(i + 1) * P]

    def heads_k(A, st, hh, i):
        a, b = span(A, i)
        if A.kind == "mla":
            return A.k[st][:, hh, a:b]
        return A.k[st][64 * hh:64 * hh + 64, a:b]

    def table(A, st, hh, i):
        a, b = span(A, i)
        if A.kind == "mla":
            return A.tab[st][:, TOK - (b - a):TOK]
        full = 256 if A.kind == "swa" else TOK
        return A.tab[st][:, hh, full - (b - a):full]

    def attention_steps(eng, n, project, step, tail):
        project(0, 0, 0)

        def body(i):
            for u in range(2):
                prev = None if isinstance(i, int) and i == 0 and u == 0 else (2 * i + u - 1, 1 - u)
                step(2 * i + u, u, i, (2 * i + u + 1, 1 - u, i + u), prev)
        turns(eng, n // 2 - 1, body)
        i = n // 2 - 1
        step(n - 2, 0, i, (n - 1, 1, i), (n - 3, 1))
        step(n - 1, 1, i, None, (n - 2, 0))
        tail(n - 1, 1)

    def att_pe(pe, A, ready, R=None):
        s, kind = A.s, A.kind
        after = [lambda k=k: resid_first(pe, R, k) for k in range(KD - 1)] if R else []
        for sm, v in ready:
            wait_for(pe, sm, v)

        def tile(bank, w_h, w_l, col, x, ks, n=KD):
            for k in ks:
                last = mm3(pe, ps[:, bank, :], w_h[:, k, col:col + P], w_l[:, k, col:col + P],
                           x[0][:, k, :], x[1][:, k, :], k == 0, k == n - 1)
            return last

        def pieces(p, st, turn):
            if kind == "swa":
                c = A.st.base + p
                w_h, w_l = chunk_w((A.st.base + st) % 2, KD, P)

                def quarter(n):
                    if n == 0:
                        pe.wait_ge(w_split, c + 1)
                        wait_past(pe, s["q_staged"], p)
                    last = tile(A0, w_h, w_l, 0, (xh, xl), (2 * n, 2 * n + 1))
                    if n == 3:
                        last.then_inc(w_used, 1)
                return [lambda n=n: quarter(n) for n in range(4)]

            if kind == "dil":
                c = A.st.base + p

                def half(which, n):
                    w_h, w_l = chunk_w((A.st.base + st) % 2, KD, 256)
                    if n == 0:
                        if which == 0:
                            pe.wait_ge(w_split, c + 1)
                        wait_past(pe, s["k_staged" if which else "q_staged"], p)
                    last = tile(A0 + which, w_h, w_l, which * P, (xh, xl), range(4 * n, 4 * n + 4))
                    if n == 1:
                        last.then_inc(w_used if which else s["q_made"], 1)
                return [lambda a=a, n=n: half(a, n) for a in range(2) for n in range(2)]

            c = A.st.base + 2 * p
            slots = (A.st.base % 2, (A.st.base + 1) % 2)
            def queries():
                w_h, w_l = chunk_w(slots[0], 2, 256)
                pe.wait_ge(w_split, c + 1)
                if isinstance(p, int) and p == 0:
                    pe.wait_ge(dil_values, 4)
                wait_past(pe, s["v_staged"], p)
                wait_past(pe, s["k_staged"], 2 * p)
                for hh in range(2):
                    last = tile(A0 + hh, w_h, w_l, hh * P, (e_cqh, e_cql), range(2), 2)
                last.then_inc(w_used, 1)

            def keys():
                w_h, w_l = chunk_w(slots[1], 1, 256)
                pe.wait_ge(w_split, c + 2)
                for hh in range(2):
                    pe.wait_ge(s["q_staged"], 2 * p + hh + 1)
                    tile(A0 + hh, w_h, w_l, hh * P, (e_ckh, e_ckl), range(1), 1)\
                        .then_inc(keys_made, 1)

            def values():
                w_h, w_l = chunk_w(slots[1], 1, 256)
                vh = w_h[:, 0, :].rearrange("p (a b) -> p a b", a=2)[:, :, 64:P]
                vl = w_l[:, 0, :].rearrange("p (a b) -> p a b", a=2)[:, :, 64:P]
                pe.wait_ge(s["k_staged"], 2 * p + 1)
                for t in range(TB):
                    last = mm3(pe, ps[:, A0, t * P:(t + 1) * P], e_ckh[:, 0, t * P:(t + 1) * P],
                               e_ckl[:, 0, t * P:(t + 1) * P], vh, vl, True, True)
                last.then_inc(w_used, 1)
            return [queries, keys, values]

        def scores(p, st, hh):
            if hh == 0:
                pe.wait_ge(s["q_staged"], 2 * (p + 1) if kind == "mla" else p + 1)
                if kind != "swa":
                    pe.wait_ge(s["k_staged"], 2 * (p + 1) if kind == "mla" else p + 1)
                    if kind == "mla":
                        pe.wait_ge(s["v_staged"], p + 1)
                    elif isinstance(p, int) and p == 0:
                        pe.wait_ge(dil_values, 4)
            for i in range(TB):
                a, b = span(A, i)
                u = 8 * p + 4 * hh + i
                wait_past(pe, s["masked"], u - 1 if hh == 0 and i < 2 else u - 2)
                pe.matmul(ps[:, S_BANK[hh][i], 0:b - a], heads_q(A, st, hh, i), heads_k(A, st, hh, i),
                          start=True, stop=True).then_inc(s["scored"], 1)

        def turn_band(p, hh, g):
            u = 8 * p + 4 * hh + 2 * g
            pe.wait_ge(s["normed"], u + 2)
            wait_past(pe, s["pt_copied"], u - 2)
            for i in (2 * g, 2 * g + 1):
                for j in range(2 if i else 1):
                    at = 256 * j + P * (i - 2 * g)
                    last = pe.transpose(ps[:, T_BANK + g, at:at + P], probs(A, hh, i)[:, j * P:(j + 1) * P],
                                        ident[:, :])
            last.then_inc(s["turned"], 2)

        def turn_p(p, hh, blocks):
            if kind == "swa":
                return turn_band(p, hh, blocks[0] // 2)
            for i in blocks:
                a, b = span(A, i)
                u = 8 * p + 4 * hh + i
                pe.wait_ge(s["normed"], u + 1)
                wait_past(pe, s["pt_copied"], u - 1)
                for j in range((b - a) // P):
                    last = pe.transpose(ps[:, T_BANK + i % 2, j * P:(j + 1) * P],
                                        probs(A, hh, i)[:, j * P:(j + 1) * P], ident[:, :])
                last.then_inc(s["turned"], 1)

        def pv(p, st, hh):
            pe.wait_ge(s["pt_copied"], 8 * p + 4 * hh + 4)
            if hh == 0:
                wait_past(pe, s["o_taken"], p)
            pt = A.pt
            o = ps[64 * hh:64 * hh + 64, O_BANK, :]
            cols = slice(64 * hh, 64 * hh + 64)
            if kind == "swa":
                for i in range(TB):
                    a, b = span(A, i)
                    n = (b - a) // P
                    for j in range(n):
                        last = pe.matmul(o[:, i * P:(i + 1) * P], heads_v(A, p, st, a // P + j)[:, cols],
                                         pt[:, j, i * P:(i + 1) * P], start=(j == 0), stop=(j == n - 1))
            else:
                for j in range(TB):
                    last = pe.matmul(o[:, j * P:TOK], heads_v(A, p, st, j)[:, cols], pt[:, j, j * P:TOK],
                                     start=(j == 0), stop=(j == TB - 1))
            last.then_inc(s["pv_done"], 1)

        SHARE = {"mla": (0, 1, 0, 1, 0, 1, 0, 0, 0), "dil": (0, 1, 0, 1, 0, 1, 0, 1, 0),
                 "swa": (0, 1, 1, 0, 1, 0, 1, 0, 0)}

        def step(p, st, turn, nx, prev):
            if nx:
                todo, share = pieces(*nx), iter(SHARE[kind])
            else:
                todo, share = list(after), iter((0, 1, 1, 1, 1, 1, 1, 1, 0))

            def some():
                for _ in range(next(share)):
                    if todo:
                        todo.pop(0)()

            some()
            scores(p, st, 0)
            some()
            if prev:
                tail(*prev)
            some()
            scores(p, st, 1)
            some()
            turn_p(p, 0, (0, 1))
            some()
            turn_p(p, 0, (2, 3))
            some()
            pv(p, st, 0)
            some()
            turn_p(p, 1, (0, 1))
            some()
            turn_p(p, 1, (2, 3))
            some()
            assert not todo

        def tail(p, st):
            pv(p, st, 1)

        def project(p, st, turn):
            for piece in pieces(p, st, turn):
                piece()

        attention_steps(pe, A.pairs, project, step, tail)

    keys_made = sem("mla_keys_made")

    def att_act(act, A, ready=()):
        s, kind = A.s, A.kind
        for sm, v in ready:
            wait_for(act, sm, v)

        def load_table(p, st):
            wait_past(act, s["masked"], 8 * (p - 1))
            src = dram["tab_dil"] if kind == "dil" else dram["tab_swa"]
            act.dma_start(A.tab[st][:, :, :], src[p].rearrange("p (a b) -> p a b", a=2))\
               .then_inc(s[f"tab_loaded{st}"], 16)

        def queries(p, st):
            if kind == "swa":
                act.wait_ge(w_used, A.st.base + p + 1)
            else:
                act.wait_ge(s["q_made"], p + 1)
            act.activation(A.q[st][:, :], ps[:, A0, :], ACT.Copy).then_inc(s["q_staged"], 1)

        def keys(p, st):
            for hh in range(2):
                act.wait_ge(keys_made, 2 * p + hh + 1)
                act.activation(A.k[st][0:64, hh, :], ps[0:64, A0 + hh, :], ACT.Copy)\
                   .then_inc(s["k_staged"], 1)

        def values(p, st):
            act.wait_ge(w_used, A.st.base + 2 * p + 2)
            act.activation(A.v[st][:, :, :], ps[:, A0, :].rearrange("p (a b) -> p a b", a=TB),
                           ACT.Copy).then_inc(s["v_staged"], 1)

        def project(p, st, turn):
            if kind in ("dil", "swa"):
                load_table(p, st)
                queries(p, st)
            if kind == "mla":
                keys(p, st)
            if kind == "mla":
                values(p, st)

        def exps(p, hh):
            for i in range(TB):
                a, b = span(A, i)
                u = 8 * p + 4 * hh + i
                row = 4 * hh + i
                act.wait_ge(s["masked"], u + 1)
                act.activation(probs(A, hh, i), probs(A, hh, i), ACT.Exp, scale=-1.0,
                               bias=nmax[:, row:row + 1], accum_out=rsum[:, row:row + 1])\
                   .then_inc(s["exped"], 1)
            if kind == "swa":
                act.wait_ge(s["es"], 2 * (2 * p + hh) + 1)
                act.activation(s_es[:, 4 * hh:4 * hh + 4], s_es[:, 4 * hh:4 * hh + 4], ACT.Exp)\
                   .then_inc(s["exped"], 1)

        def copy_band(p, hh):
            u = 8 * p + 4 * hh
            wait_past(act, s["pv_done"], 2 * p + hh)
            act.wait_ge(s["turned"], u + 2)
            act.activation(A.pt[:, 0, 0:256], ps[:, T_BANK, 0:256], ACT.Copy).then_inc(s["pt_copied"], 1)
            act.activation(A.pt[:, 1, P:256], ps[:, T_BANK, 256 + P:512], ACT.Copy).then_inc(s["pt_copied"], 1)
            act.wait_ge(s["turned"], u + 4)
            act.activation(A.pt[:, 0:2, 256:512], ps[:, T_BANK + 1, :].rearrange("p (a b) -> p a b", a=2),
                           ACT.Copy).then_inc(s["pt_copied"], 2)

        def copy_pt(p, hh):
            if kind == "swa":
                return copy_band(p, hh)
            for i in range(TB):
                a, b = span(A, i)
                n = (b - a) // P
                u = 8 * p + 4 * hh + i
                act.wait_ge(s["turned"], u + 1)
                wait_past(act, s["pv_done"], 2 * p + hh)
                act.activation(A.pt[:, 0:n, i * P:(i + 1) * P],
                               ps[:, T_BANK + i % 2, 0:n * P].rearrange("p (a b) -> p a b", a=n),
                               ACT.Copy).then_inc(s["pt_copied"], 1)

        def tail(p, st):
            act.wait_ge(s["pv_done"], 2 * p + 2)
            act.activation(at_tile(oh, A.first_out + p), ps[:, O_BANK, :], ACT.Copy)\
               .then_inc(s["o_rounded"], 1)

        def step(p, st, turn, nx, prev):
            if nx and kind in ("dil", "swa"):
                load_table(nx[0], nx[1])
            exps(p, 0)
            if prev:
                tail(*prev)
            exps(p, 1)
            if nx and kind == "dil":
                queries(nx[0], nx[1])
            if nx and kind == "mla":
                keys(nx[0], nx[1])
            copy_pt(p, 0)
            if nx and kind == "mla":
                values(nx[0], nx[1])
            if nx and kind == "swa":
                queries(nx[0], nx[1])
            copy_pt(p, 1)

        attention_steps(act, A.pairs, project, step, tail)

    def att_dve(dve, A, ready=()):
        s, kind = A.s, A.kind
        for sm, v in ready:
            wait_for(dve, sm, v)

        def neg_sinks(p, st):
            wait_past(dve, s["masked"], 8 * (p - 1))
            g = GAINS["sinks"] + 2 * p
            src = gains[:, g:g + 2] if isinstance(p, int) else gains[:, bass.ds(g, 2)]
            dve.tensor_scalar(A.neg[st][:, :], src, -1.0, None, ALU.mult).then_inc(sinks_ready, 1)

        def rotate(p, st):
            dve.wait_ge(w_used, A.st.base + 2 * p + 1)
            for hh in range(2):
                dve.tensor_tensor(A.q[st][:, hh, :], ps[:, A0 + hh, :], e_ropeq[:, :], ALU.mult)\
                   .then_inc(s["q_staged"], 1)

        def keys(p, st):
            dve.wait_ge(w_used, A.st.base + p + 1)
            dve.tensor_copy(A.k[st][:, :], ps[:, A1, :]).then_inc(s["k_staged"], 1)

        def project(p, st, turn):
            if kind == "swa":
                neg_sinks(p, st)
            elif kind == "mla":
                rotate(p, st)
            else:
                keys(p, st)

        def mask(p, st, turn, hh):
            for i in range(TB):
                a, b = span(A, i)
                u = 8 * p + 4 * hh + i
                row = 4 * hh + i
                dve.wait_ge(s["scored"], u + 1)
                if kind in ("dil", "swa") and hh == 0 and i == 0:
                    dve.wait_ge(s[f"tab_loaded{st}"], 16 * (turn + 1))
                    if kind == "swa":
                        dve.wait_ge(sinks_ready, p + 1)
                wait_past(dve, s["turned"], u - 7)
                if u_is_late(p, hh):
                    dve.wait_ge(s["exped"], exped_before(A, p, hh))
                start = A.neg[st][:, hh:hh + 1] if kind == "swa" else 3e38
                stand_alone(dve.tensor_tensor_reduce(
                    probs(A, hh, i), ps[:, S_BANK[hh][i], 0:b - a], table(A, st, hh, i), -A.scale,
                    start, ALU.add, ALU.min, nmax[:, row:row + 1])).then_inc(s["masked"], 1)
            if kind == "swa":
                dve.wait_ge(s["masked"], 8 * p + 4 * hh + 4)
                dve.tensor_scalar(s_es[:, 4 * hh:4 * hh + 4], nmax[:, 4 * hh:4 * hh + 4],
                                  A.neg[st][:, hh:hh + 1], None, ALU.subtract).then_inc(s["es"], 1)

        def u_is_late(p, hh):
            return not (isinstance(p, int) and p == 0)

        def exped_before(A, p, hh):
            per = 10 if A.kind == "swa" else 8
            return per * p + (per // 2) * hh - per // 2

        def norm(p, hh):
            per = 10 if kind == "swa" else 8
            dve.wait_ge(s["exped"], per * p + (per // 2) * (hh + 1))
            r = slice(4 * hh, 4 * hh + 4)
            if kind == "swa":
                dve.tensor_tensor(rsum[:, r], rsum[:, r], s_es[:, r], ALU.add).then_inc(s["es"], 1)
                dve.wait_ge(s["es"], 2 * (2 * p + hh) + 2)
            dve.reciprocal(rinv[:, r], rsum[:, r]).then_inc(s["inverted"], 1)
            dve.wait_ge(s["inverted"], 2 * p + hh + 1)
            for i in range(TB):
                a, b = span(A, i)
                dve.tensor_scalar(probs(A, hh, i), probs(A, hh, i),
                                  rinv[:, 4 * hh + i:4 * hh + i + 1],
                                  None, ALU.mult).then_inc(s["normed"], 1)

        def tail(p, st):
            dve.wait_ge(s["o_rounded"], p + 1)
            o = A.first_out + p
            dve.tensor_tensor(at_tile(ol, o), ps[:, O_BANK, :], at_tile(oh, o).bitcast(F32),
                              ALU.subtract).then_inc(s["o_taken"], 1)

        def step(p, st, turn, nx, prev):
            mask(p, st, turn, 0)
            norm(p, 0)
            if prev:
                tail(*prev)
            mask(p, st, turn, 1)
            if nx and kind == "mla":
                rotate(nx[0], nx[1])
            norm(p, 1)
            if nx and kind == "dil":
                keys(nx[0], nx[1])
            if nx and kind == "swa":
                neg_sinks(nx[0], nx[1])

        attention_steps(dve, A.pairs, project, step, tail)

    sinks_ready = sem("swa_sinks_ready")

    a_mla = attention("mla", "mla", st_mla, 4, 96.0 ** -0.5, (e_q0, e_q1), (e_k0, e_k1), (e_v0, e_v1),
                      e_p, e_t0, (e_causal, e_causal), 0)
    a_dil = attention("dil", "dil", st_dil, 4, 0.125, (d_q0, d_q1), (d_k0, d_k1), d_v,
                      d_p, d_t0, (d_b0, d_b1), 4)
    a_swa = attention("swa", "swa", st_swa, 8, 0.125, (s_q0, s_q1), (s_k, s_k), (s_v, s_v),
                      s_p, s_t0, (s_b0, s_b1), 0)
    a_swa.neg = (s_neg0, s_neg1)
    kv_taken = sem("swa_kv_taken")
    kv_keys = sem("swa_kv_keys")

    def swa_kv_pe(pe):
        c = st_okv.base
        w_h, w_l = chunk_w(c % 2, KD, 256)
        pe.wait_ge(w_split, c + 1)
        for k in range(KD):
            wait_for(pe, n_attn1.s["split"], k + 1)
            last = mm3(pe, ps[:, A1, :], w_h[:, k, 0:P], w_l[:, k, 0:P], xh[:, k, :], xl[:, k, :],
                       k == 0, k == KD - 1)
        last.then_inc(kv_keys, 1)
        for t in range(TB):
            for k in range(KD):
                last = mm3(pe, ps[:, O_BANK, t * P:(t + 1) * P], xh[:, k, t * P:(t + 1) * P],
                           xl[:, k, t * P:(t + 1) * P], w_h[:, k, P:2 * P], w_l[:, k, P:2 * P],
                           k == 0, k == KD - 1)
        last.then_inc(w_used, 1)

    def swa_kv_act(act):
        act.wait_ge(kv_keys, 1)
        act.activation(s_k[:, :], ps[:, A1, :], ACT.Copy).then_inc(kv_taken, 1)
        act.wait_ge(w_used, st_okv.base + 1)
        act.activation(s_v[:, :, :], ps[:, O_BANK, :].rearrange("p (a b) -> p a b", a=TB), ACT.Copy)\
           .then_inc(kv_taken, 1)

    def final_dve(dve):
        wait_for(dve, n_fin.s["rstd"], 1)
        for t in range(KD):
            g = GAINS["final"] + t
            dve.scalar_tensor_tensor(out=h[:, t, :], in0=h[:, t, :], scalar=gains[:, g:g + 1],
                                     in1=rstd[:, :], op0=ALU.mult, op1=ALU.mult)\
               .then_inc(n_fin.s["scaled"].sem, 1)

    G = sems("gla", "tables z_taken pre_made biased absed exped1 logged combined scanned q_made "
             "q_taken k_taken v0_made v_taken g_taken cum_taken diff e ks qs products merged zeroed "
             "eb qe dlast elast kt_made kt_turned ktt_taken upd_made state out_made squared summed "
             "gated hlogged hrstd hy hy2 rounded split")
    NL = len(LEVELS)
    NP = NL + 1
    Q2, K2, V2, G2, CUM2 = (g_q0, g_q1), (g_k0, g_k1), (g_v0, g_v1), (g_g0, g_g1), (g_cum0, g_cum1)
    KS, QS, TMP, E = (g_ks0, g_ks1), (g_qs0, g_qs1), (g_tmp0, g_tmp1), (g_e0, g_e1)

    def bview(x, s_):
        return x.rearrange("p (n b) -> p n b", b=2 * s_)

    def gla_pieces(pe, hd):
        c = st_gla.base + 4 * hd
        sl = [(st_gla.base + u) % 2 for u in range(4)]

        def half(which, n):
            w_h, w_l = chunk_w(sl[0], KD, 256)
            if n == 0:
                if which == 0:
                    pe.wait_ge(w_split, c + 1)
                wait_past(pe, G["g_taken"], 2 * (hd - 1) + which + 1)
            for k in range(4 * n, 4 * n + 4):
                last = mm3(pe, ps[:, which, :], w_h[:, k, which * P:(which + 1) * P],
                           w_l[:, k, which * P:(which + 1) * P], xh[:, k, :], xl[:, k, :],
                           k == 0, k == KD - 1)
            if n == 1:
                last.then_inc(w_used if which else G["q_made"], 1)

        def value(t):
            w_h, w_l = chunk_w(sl[1], KD, 256)
            if t == 0:
                pe.wait_ge(w_split, c + 2)
                pe.wait_ge(G["q_taken"], hd + 1)
            elif t == 2:
                pe.wait_ge(G["k_taken"], hd + 1)
            for k in range(KD):
                last = mm3(pe, ps[:, t // 2, (t % 2) * 256:(t % 2) * 256 + 256],
                           xh[:, k, t * P:(t + 1) * P], xl[:, k, t * P:(t + 1) * P],
                           w_h[:, k, :], w_l[:, k, :], k == 0, k == KD - 1)
            if t == 1:
                last.then_inc(G["v0_made"], 1)
            elif t == 3:
                last.then_inc(w_used, 1)

        def gate(j, n):
            w_h, w_l = chunk_w(sl[2 + j], KD, P)
            if n == 0:
                pe.wait_ge(w_split, c + 3 + j)
                pe.wait_ge(G["v_taken"], 2 * hd + j + 1)
            for k in range(4 * n, 4 * n + 4):
                last = mm3(pe, ps[:, j, :], w_h[:, k, :], w_l[:, k, :], xh[:, k, :], xl[:, k, :],
                           k == 0, k == KD - 1)
            if n == 1:
                last.then_inc(w_used, 1)

        return ([lambda a=a, n=n: half(a, n) for a in range(2) for n in range(2)]
                + [lambda t=t: value(t) for t in range(TB)]
                + [lambda a=a, n=n: gate(a, n) for a in range(2) for n in range(2)])

    def gla_gate_pe(pe):
        c = st_z.base
        w_h, w_l = chunk_w(c % 2, KD, P)
        pe.wait_ge(w_split, c + 1)
        for k in range(KD):
            wait_for(pe, n_a.s["split"], k + 1)
            last = mm3(pe, ps[:, 2, :], w_h[:, k, :], w_l[:, k, :], xh[:, k, :], xl[:, k, :],
                       k == 0, k == KD - 1)
        last.then_inc(w_used, 1)
        todo = gla_pieces(pe, 0)
        for piece in todo[:4]:
            piece()
        pe.wait_ge(G["z_taken"], 1)
        pe.wait_ge(G["tables"], 48)
        for hd in range(4):
            pe.matmul(ps[:, 4 + hd, :], g_wg[:, hd * P:(hd + 1) * P], g_z[:, :], start=True, stop=True)\
              .then_inc(G["pre_made"], 1)
        for piece in todo[4:]:
            piece()

    def gla_gate_act(act):
        wait_for(act, n_a.s["rstd"], 1)
        act.dma_start(g_wg[:, :], dram["a_gate_up"]).then_inc(G["tables"], 16)
        act.dma_start(g_masks[:, :, :], dram["level_masks"].rearrange("p (a b) -> p a b", a=NP))\
           .then_inc(G["tables"], 16)
        act.dma_start(g_reset[:, :], dram["scan_reset"]).then_inc(G["tables"], 16)
        act.wait_ge(w_used, st_z.base + 1)
        act.activation(g_z[:, :], ps[0:16, 2, :], ACT.Copy).then_inc(G["z_taken"], 1)
        gla_query(act, 0)
        for hd in range(4):
            act.wait_ge(G["pre_made"], hd + 1)
            g = GAINS["b_gate"] + hd
            act.activation(sq[:, hd, :], ps[:, 4 + hd, :], ACT.Identity, bias=gains[:, g:g + 1])\
               .then_inc(G["biased"], 1)
        act.wait_ge(G["biased"], 4)
        act.activation(g_b[:, :, :], sq[:, :, :], ACT.Abs).then_inc(G["absed"], 1)
        act.wait_ge(G["absed"], 1)
        act.activation(g_b[:, :, :], g_b[:, :, :], ACT.Exp, scale=-1.0).then_inc(G["exped1"], 1)
        act.wait_ge(G["exped1"], 1)
        act.activation(g_b[:, :, :], g_b[:, :, :], ACT.Ln, bias=1.0).then_inc(G["logged"], 1)
        gla_values(act, 0, 0)
        gla_values(act, 0, 1)
        gla_gates(act, 0)

    def gla_gate_dve(dve):
        dve.memset(g_at[:, :], 0.0).then_inc(G["zeroed"], 1)
        for buf in (g_ks0, g_ks1, g_qs0, g_qs1):
            dve.memset(buf[:, :], 0.0).then_inc(G["zeroed"], 1)
        gla_key(dve, 0)
        dve.wait_ge(G["logged"], 1)
        dve.scalar_tensor_tensor(out=sq[:, :, :], in0=sq[:, :, :], scalar=0.0, in1=g_b[:, :, :],
                                 op0=ALU.min, op1=ALU.subtract).then_inc(G["combined"], 1)
        dve.wait_ge(G["tables"], 48)
        dve.wait_ge(G["combined"], 1)
        for hd in range(4):
            dve.tensor_tensor_scan(g_b[:, hd, :], g_reset[:, :], sq[:, hd, :], 0.0, ALU.mult, ALU.add)\
               .then_inc(G["scanned"], 1)
        gla_begin(dve, 0)

    def gla_query(act, hd):
        act.wait_ge(G["q_made"], hd + 1)
        wait_past(act, G["products"], NP * (hd - 1))
        wait_past(act, G["qe"], hd - 1)
        act.activation(Q2[hd % 2][:, :], ps[:, 0, :], ACT.Copy, scale=float(P) ** -0.5)\
           .then_inc(G["q_taken"], 1)

    def gla_key(dve, hd):
        dve.wait_ge(w_used, st_gla.base + 4 * hd + 1)
        wait_past(dve, G["products"], NP * (hd - 1))
        wait_past(dve, G["kt_made"], hd - 1)
        dve.tensor_copy(K2[hd % 2][:, :], ps[:, 1, :]).then_inc(G["k_taken"], 1)

    def gla_values(act, hd, j):
        if j == 0:
            act.wait_ge(G["v0_made"], hd + 1)
        else:
            act.wait_ge(w_used, st_gla.base + 4 * hd + 2)
        wait_past(act, G["out_made"], 4 * (hd - 1))
        act.activation(V2[hd % 2][:, 2 * j:2 * j + 2, :],
                       ps[:, j, :].rearrange("p (a b) -> p a b", a=2), ACT.Copy).then_inc(G["v_taken"], 1)

    def gla_gates(act, hd):
        for j in range(2):
            act.wait_ge(w_used, st_gla.base + 4 * hd + 3 + j)
            wait_past(act, G["hy2"], 2 * (hd - 1))
            act.activation(G2[hd % 2][:, j, :], ps[:, j, :], ACT.Copy).then_inc(G["g_taken"], 1)

    def gla_diff(dve, hd, lv):
        s_ = LEVELS[lv]
        b = bview(CUM2[hd % 2][:, :], s_)
        ref = b[:, :, s_ - 1:s_].broadcast_to([P, TOK // (2 * s_), 2 * s_])
        dve.tensor_tensor(bview(TMP[lv % 2][:, :], s_), b, ref, ALU.subtract).then_inc(G["diff"], 1)

    def gla_begin(dve, hd):
        if hd == 0:
            dve.wait_ge(G["scanned"], 4)
            dve.wait_ge(G["zeroed"], 5)
        wait_past(dve, G["eb"], hd - 1)
        dve.tensor_copy(CUM2[hd % 2][:, :], g_b[:, hd, :]).then_inc(G["cum_taken"], 1)
        dve.wait_ge(G["cum_taken"], hd + 1)
        wait_past(dve, G["e"], 2 * NL * hd)
        gla_diff(dve, hd, 0)
        wait_past(dve, G["kt_made"], hd)
        gla_diff(dve, hd, 1)

    def gla_pe(pe):
        def step(hd, st, turn, nx, prev):
            todo = gla_pieces(pe, nx[0]) if nx else [lambda k=k: out_tile(k) for k in range(6)]

            def some():
                if todo:
                    todo.pop(0)()

            def scores(n):
                kk, qq = (KS[(n - 1) % 2], QS[(n - 1) % 2]) if n else (K2[st], Q2[st])
                if n:
                    pe.wait_ge(G["ks"], NL * hd + n)
                    pe.wait_ge(G["qs"], NL * hd + n)
                else:
                    pe.wait_ge(G["q_taken"], hd + 1)
                    pe.wait_ge(G["k_taken"], hd + 1)
                wait_past(pe, G["merged"], NP * hd + n - 1)
                for t in range(TB):
                    last = pe.matmul(ps[:, 2 + n % 2, t * P:(t + 1) * P], kk[:, t * P:(t + 1) * P],
                                     qq[:, t * P:(t + 1) * P], start=True, stop=True)
                last.then_inc(G["products"], 1)

            for n in range(NP):
                scores(n)
                some()
                if n == 1 and prev:
                    sums(prev[0])
            pe.wait_ge(G["kt_made"], hd + 1)
            wait_past(pe, G["hlogged"], hd)
            for t in range(TB):
                last = pe.transpose(ps[:, 4, t * P:(t + 1) * P], g_kt[:, t * P:(t + 1) * P], ident[:, :])
            last.then_inc(G["kt_turned"], 1)
            some()
            pe.wait_ge(G["merged"], NP * (hd + 1))
            pe.wait_ge(G["qe"], hd + 1)
            pe.wait_ge(G["v_taken"], 2 * hd + 2)
            wait_past(pe, G["hy"], 2 * hd)
            for t in range(TB):
                if t > 0:
                    pe.wait_ge(G["state"], 3 * hd + t)
                for dv in range(2):
                    o = ps[:, 6 + dv, t * P:(t + 1) * P]
                    last = pe.matmul(o, V2[st][:, t, dv * P:(dv + 1) * P], g_at[:, t * P:(t + 1) * P],
                                     start=True, stop=(t == 0))
                    if t > 0:
                        last = pe.matmul(o, g_s[:, dv * P:(dv + 1) * P], g_qe[:, t * P:(t + 1) * P],
                                         start=False, stop=True)
                last.then_inc(G["out_made"], 1)
                if t < TB - 1:
                    if t == 0:
                        pe.wait_ge(G["ktt_taken"], hd + 1)
                    pe.matmul(ps[:, 5, 0:256], g_ktt[:, t * P:(t + 1) * P], V2[st][:, t, :],
                              start=True, stop=True).then_inc(G["upd_made"], 1)
                    some()
            assert not todo

        def out_tile(k):
            if k == 0:
                pe.wait_ge(G["g_taken"], 8)
            resid_first(pe, r_aout, k)

        def sums(hd):
            for dv in range(2):
                pe.wait_ge(G["squared"], 2 * hd + dv + 1)
                pe.matmul(ps[:, 4, :], ones[:, :], g_y[:, dv, :], start=(dv == 0), stop=(dv == 1))\
                  .then_inc(G["summed"], 1)
        attention_steps(pe, 4, lambda *a: None, step, lambda hd, st: sums(hd))

    def gla_act(act):
        def square(hd):
            act.wait_ge(G["out_made"], 4 * hd + 4)
            wait_past(act, G["split"], 2 * hd)
            for dv in range(2):
                act.activation(g_y[:, dv, :], ps[:, 6 + dv, :], ACT.Square).then_inc(G["squared"], 1)

        def root(hd):
            act.wait_ge(G["summed"], 2 * hd + 2)
            act.activation(rstd[:, :], ps[:, 4, :], ACT.Ln, bias=eps[:, 0:1], scale=1.0 / 256)\
               .then_inc(G["hlogged"], 1)
            act.wait_ge(G["hlogged"], hd + 1)
            act.activation(rstd[:, :], rstd[:, :], ACT.Exp, scale=-0.5).then_inc(G["hrstd"], 1)

        def rounded(hd):
            for dv in range(2):
                act.wait_ge(G["hy2"], 2 * hd + dv + 1)
                act.activation(oh[:, 2 * hd + dv, :], g_y[:, dv, :], ACT.Copy).then_inc(G["rounded"], 1)

        def tail(hd, st):
            square(hd)
            root(hd)
            rounded(hd)

        def step(hd, st, turn, nx, prev):
            for lv, s_ in enumerate(LEVELS):
                n = NL * hd + lv
                act.wait_ge(G["diff"], n + 1)
                wait_past(act, G["qs"], n - 1)
                wait_past(act, G["ks"], n - 1)
                if lv == 1:
                    wait_past(act, G["state"], 3 * hd)
                d, e = bview(TMP[lv % 2][:, :], s_), bview(E[lv % 2][:, :], s_)
                act.activation(e[:, :, 0:s_], d[:, :, 0:s_], ACT.Exp, scale=-1.0 / GLA_TAU).then_inc(G["e"], 1)
                act.activation(e[:, :, s_:2 * s_], d[:, :, s_:2 * s_], ACT.Exp, scale=1.0 / GLA_TAU)\
                   .then_inc(G["e"], 1)
                if prev:
                    if lv == 0:
                        square(prev[0])
                    elif lv == 2:
                        root(prev[0])
                    elif lv == 3:
                        rounded(prev[0])
                if nx:
                    if lv == 1:
                        gla_query(act, nx[0])
                    elif lv == 5:
                        gla_values(act, nx[0], 0)
            act.wait_ge(G["ks"], NL * (hd + 1) - 1)
            act.wait_ge(G["qs"], NL * (hd + 1) - 1)
            act.activation(E[1][:, :], CUM2[st][:, :], ACT.Exp, scale=1.0 / GLA_TAU).then_inc(G["eb"], 1)
            act.wait_ge(G["dlast"], hd + 1)
            act.activation(TMP[1][:, :], TMP[1][:, :], ACT.Exp, scale=1.0 / GLA_TAU).then_inc(G["elast"], 1)
            if nx:
                gla_values(act, nx[0], 1)
            act.wait_ge(G["kt_turned"], hd + 1)
            wait_past(act, G["upd_made"], 3 * hd)
            act.activation(g_ktt[:, :], ps[:, 4, :], ACT.Copy).then_inc(G["ktt_taken"], 1)
            act.wait_ge(G["g_taken"], 2 * hd + 2)
            act.activation(G2[st][:, :, :], G2[st][:, :, :], ACT.Silu).then_inc(G["gated"], 1)
            log_exp(act)
            if nx:
                gla_gates(act, nx[0])
        attention_steps(act, 4, lambda *a: None, step, tail)

    def gla_dve(dve):
        def merge(hd, n):
            dve.wait_ge(G["products"], NP * hd + n + 1)
            wait_past(dve, G["merged"], NP * hd + n)
            if n == 0:
                wait_past(dve, G["out_made"], 4 * hd)
            m = n - 1 if n else NL
            stand_alone(dve.copy_predicated(
                g_at[:, :].rearrange("p (a b) -> p a b", a=TB),
                g_masks[:, m:m + 1, :].broadcast_to([P, TB, P]),
                ps[:, 2 + n % 2, :].rearrange("p (a b) -> p a b", a=TB))).then_inc(G["merged"], 1)

        def scale(hd):
            dve.wait_ge(G["hrstd"], hd + 1)
            for dv in range(2):
                g = GAINS["a_head"] + dv
                dve.scalar_tensor_tensor(out=g_y[:, dv, :], in0=ps[:, 6 + dv, :], scalar=gains[:, g:g + 1],
                                         in1=rstd[:, :], op0=ALU.mult, op1=ALU.mult).then_inc(G["hy"], 1)
            dve.wait_ge(G["gated"], hd + 1)
            for dv in range(2):
                dve.wait_ge(G["hy"], 2 * hd + dv + 1)
                dve.tensor_tensor(g_y[:, dv, :], g_y[:, dv, :], G2[hd % 2][:, dv, :], ALU.mult)\
                   .then_inc(G["hy2"], 1)

        def split(hd):
            for dv in range(2):
                dve.wait_ge(G["rounded"], 2 * hd + dv + 1)
                to = oh[:, 2 * hd + dv, :]
                dve.tensor_tensor(ol[:, 2 * hd + dv, :], g_y[:, dv, :], to.bitcast(F32), ALU.subtract)\
                   .then_inc(G["split"], 1)

        def tail(hd, st):
            scale(hd)
            split(hd)

        def step(hd, st, turn, nx, prev):
            if hd == 0:
                dve.wait_ge(G["q_taken"], 1)
            dve.wait_ge(G["k_taken"], hd + 1)
            for lv, s_ in enumerate(LEVELS):
                n = NL * hd + lv
                dve.wait_ge(G["e"], 2 * n + 2)
                dve.wait_ge(G["q_taken"], hd + 1)
                if lv >= 2:
                    dve.wait_ge(G["products"], NP * hd + lv)
                e = bview(E[lv % 2][:, :], s_)
                dve.tensor_tensor(bview(KS[lv % 2][:, :], s_)[:, :, 0:s_], bview(K2[st][:, :], s_)[:, :, 0:s_],
                                  e[:, :, 0:s_], ALU.mult).then_inc(G["ks"], 1)
                dve.tensor_tensor(bview(QS[lv % 2][:, :], s_)[:, :, s_:2 * s_],
                                  bview(Q2[st][:, :], s_)[:, :, s_:2 * s_], e[:, :, s_:2 * s_],
                                  ALU.mult).then_inc(G["qs"], 1)
                if lv + 2 < NL:
                    gla_diff(dve, hd, lv + 2)
                elif lv + 2 == NL:
                    b4 = CUM2[st][:, :].rearrange("p (a b) -> p a b", a=TB)
                    last4 = b4[:, :, P - 1:P].broadcast_to([P, TB, P])
                    dve.tensor_tensor(TMP[1][:, :].rearrange("p (a b) -> p a b", a=TB), last4, b4,
                                      ALU.subtract).then_inc(G["dlast"], 1)
                merge(hd, lv)
                if prev:
                    if lv == 2:
                        scale(prev[0])
                    elif lv == 3:
                        split(prev[0])
                if nx and lv == 3:
                    gla_key(dve, nx[0])
            dve.wait_ge(G["elast"], hd + 1)
            dve.tensor_tensor(g_kt[:, :], K2[st][:, :], TMP[1][:, :], ALU.mult).then_inc(G["kt_made"], 1)
            dve.wait_ge(G["eb"], hd + 1)
            dve.tensor_tensor(g_qe[:, :], Q2[st][:, :], E[1][:, :], ALU.mult).then_inc(G["qe"], 1)
            merge(hd, NL)
            if nx:
                gla_begin(dve, nx[0])
            for t in range(TB - 1):
                dve.wait_ge(G["upd_made"], 3 * hd + t + 1)
                dve.wait_ge(G["out_made"], 4 * hd + t + 1)
                if t == 0:
                    dve.tensor_copy(g_s[:, :], ps[:, 5, 0:256]).then_inc(G["state"], 1)
                else:
                    dve.wait_ge(G["state"], 3 * hd + t)
                    dve.scalar_tensor_tensor(out=g_s[:, :], in0=g_s[:, :],
                                             scalar=E[1][:, t * P + P - 1:t * P + P], in1=ps[:, 5, 0:256],
                                             op0=ALU.mult, op1=ALU.add).then_inc(G["state"], 1)
        attention_steps(dve, 4, lambda *a: None, step, tail)

    L = sems("lam", "loaded dots exped made")
    F = sems("diff", "v_staged v_placed q_made raw_staged squared sums_made logged rooted q_staged k_staged "
             "scored masked exped inverted p_scaled normed turned pt_copied pv_done o_taken")
    H = sems("hn", "squared summed logged rooted scaled rounded split")
    NHD = 8
    FQ, FK = (f_q0, f_q1), (f_k0, f_k1)

    def f_probs(buf, i):
        return f_p[:, buf, CAUSAL_AT[i]:CAUSAL_AT[i + 1]]

    def lambda_act(act):
        wait_for(act, n_b.s["rstd"], 1)
        act.dma_start(f_lam, dram["lambda_rows"]).then_inc(L["loaded"], 16)
        act.wait_ge(L["dots"], 2)
        act.activation(lam[:, 2:4], lam[:, 0:2], ACT.Exp).then_inc(L["exped"], 1)
        wait_for(act, n_b.s["split"], 2 * KD)
        act.dma_start(f_causal[:, :], dram["tab_causal"]).then_inc(L["loaded"], 16)

    def lambda_dve(dve):
        dve.wait_ge(L["loaded"], 16)
        for j in range(2):
            dve.tensor_tensor_reduce(f_q1[:, 64 * j:64 * j + 64], f_lam[:, 128 * j:128 * j + 64],
                                     f_lam[:, 128 * j + 64:128 * j + 128], 1.0, 0.0, ALU.mult, ALU.add,
                                     lam[:, j:j + 1]).then_inc(L["dots"], 1)
        dve.wait_ge(L["exped"], 1)
        dve.tensor_tensor(lam[:, 4:5], lam[:, 3:4], lam[:, 2:3], ALU.subtract).then_inc(L["made"], 1)
        dve.wait_ge(L["made"], 1)
        dve.tensor_scalar(lam[:, 7:8], lam[:, 4:5], -LAMBDA_INIT, None, ALU.add).then_inc(L["made"], 1)
        dve.tensor_scalar(lam[:, 5:6], gains[:, GAINS["b_head"]:GAINS["b_head"] + 1], 1.0 - LAMBDA_INIT,
                          None, ALU.mult).then_inc(L["made"], 1)
        dve.wait_ge(L["made"], 3)

    def diff_values_pe(pe):
        for n in range(4):
            c = st_dv.base + n
            w_h, w_l = chunk_w(c % 2, KD, 256)
            pe.wait_ge(w_split, c + 1)
            wait_past(pe, F["v_staged"], 2 * (n - 1))
            for k in range(KD):
                if n == 0:
                    wait_for(pe, n_b.s["split"], k + 1)
                for t in range(TB):
                    last = mm3(pe, ps[:, 4 * (n % 2) + t, 0:256], f_kh[:, k, t * P:(t + 1) * P],
                               f_kl[:, k, t * P:(t + 1) * P], w_h[:, k, :], w_l[:, k, :],
                               k == 0, k == KD - 1)
            last.then_inc(w_used, 1)

    def diff_values_act(act, n):
        act.wait_ge(w_used, st_dv.base + n + 1)
        for j in range(2):
            act.activation(f_vo[:, 2 * n + j, :].rearrange("p (a b) -> p a b", a=TB),
                           ps[:, 4 * (n % 2):4 * (n % 2) + 4, j * P:(j + 1) * P],
                           ACT.Copy).then_inc(F["v_staged"], 1)

    def diff_pe(pe):
        def half(p, st, which, n):
            c = st_diff.base + p
            w_h, w_l = chunk_w((st_diff.base + st) % 2, KD, 256)
            if n == 0 and which == 0:
                pe.wait_ge(w_split, c + 1)
                if isinstance(p, int) and p == 0:
                    pe.wait_ge(F["v_staged"], 6)
                    wait_for(pe, n_b.s["split"], 2 * KD)
            if n == 0:
                wait_past(pe, F["logged"], 2 * p - 1 + which)
            x = (f_kh, f_kl) if which else (xh, xl)
            for k in range(4 * n, 4 * n + 4):
                last = mm3(pe, ps[:, which, :], w_h[:, k, which * P:(which + 1) * P],
                           w_l[:, k, which * P:(which + 1) * P], x[0][:, k, :], x[1][:, k, :],
                           k == 0, k == KD - 1)
            if n == 1:
                last.then_inc(w_used if which else F["q_made"], 1)

        def sums(p, which):
            pe.wait_ge(F["squared"], 2 * p + which + 1)
            pe.wait_ge(F["raw_staged"], 2 * p + which + 1)
            pe.matmul(ps[:, which, :], blockones[:, :], sq[:, which, :], start=True, stop=True)\
              .then_inc(F["sums_made"], 1)

        def scores(p, st, hh):
            if hh == 0:
                pe.wait_ge(F["q_staged"], p + 1)
                pe.wait_ge(F["k_staged"], p + 1)
                if isinstance(p, int) and p == 0:
                    pe.wait_ge(F["v_staged"], 8)
            for i in range(TB):
                u = 8 * p + 4 * hh + i
                wait_past(pe, F["masked"], u - 1 if hh == 0 and i < 2 else u - 2)
                rows = slice(64 * hh, 64 * hh + 64)
                pe.matmul(ps[:, S_BANK[hh][i], 0:(i + 1) * P], FQ[st][rows, i * P:(i + 1) * P],
                          FK[st][rows, 0:(i + 1) * P], start=True, stop=True).then_inc(F["scored"], 1)

        def turn_p(p, st, blocks):
            for i in blocks:
                u = TB * p + i
                pe.wait_ge(F["normed"], u + 1)
                wait_past(pe, F["pt_copied"], u - 1)
                for j in range(i + 1):
                    last = pe.transpose(ps[:, T_BANK + i % 2, j * P:(j + 1) * P],
                                        f_probs(st, i)[:, j * P:(j + 1) * P], ident[:, :])
                last.then_inc(F["turned"], 1)

        def pv(p):
            pe.wait_ge(F["pt_copied"], TB * (p + 1))
            wait_past(pe, H["logged"], p)
            pe.wait_ge(F["v_placed"], p + 1)
            for j in range(TB):
                last = pe.matmul(ps[:, O_BANK, j * P:TOK], f_v[:, j * P:(j + 1) * P], f_pt[:, j, j * P:TOK],
                                 start=(j == 0), stop=(j == TB - 1))
            last.then_inc(F["pv_done"], 1)

        def head_sum(p):
            pe.wait_ge(F["o_taken"], p + 1)
            pe.wait_ge(H["squared"], p + 1)
            pe.matmul(ps[:, O_BANK, :], ones[:, :], sq[:, 0, :], start=True, stop=True)\
              .then_inc(H["summed"], 1)

        def step(p, st, turn, nx, prev):
            if nx:
                half(*nx[:2], 0, 0)
            scores(p, st, 0)
            if nx:
                half(*nx[:2], 0, 1)
            if past_two(p):
                head_sum(p - 2)
            scores(p, st, 1)
            if nx:
                half(*nx[:2], 1, 0)
            if prev:
                turn_p(*prev, (0, 1))
            if nx:
                half(*nx[:2], 1, 1)
            if prev:
                turn_p(*prev, (2, 3))
            if nx:
                sums(nx[0], 0)
                sums(nx[0], 1)
            if prev:
                pv(prev[0])

        def tail(p, st):
            resid_pe(pe, r_bout, 0, {0: lambda: head_sum(p - 1), 2: lambda: turn_p(p, st, (0, 1)),
                                  3: lambda: turn_p(p, st, (2, 3)), 5: lambda: pv(p),
                                  7: lambda: head_sum(p)})

        def project(p, st, turn):
            for which in range(2):
                half(p, st, which, 0)
                half(p, st, which, 1)
            sums(p, 0)
            sums(p, 1)

        attention_steps(pe, NHD, project, step, tail)

    def past_two(p):
        return not isinstance(p, int) or p >= 2

    def clip(v, top):
        return min(v, top) if isinstance(v, int) else v

    def diff_act(act):
        def square(p, which):
            act.wait_ge(F["raw_staged"], 2 * p + which + 1)
            wait_past(act, F["sums_made"], 2 * p - 1 + which)
            if which == 0:
                wait_past(act, H["summed"], p - 2)
            act.activation(sq[:, which, :], f_raw[:, which, :], ACT.Square).then_inc(F["squared"], 1)

        def root(p, which):
            act.wait_ge(F["sums_made"], 2 * p + which + 1)
            wait_past(act, F["k_staged" if which else "q_staged"], p)
            if which == 0:
                wait_past(act, H["scaled"], p - 2)
            act.activation(sq[:, 2 + which, :], ps[:, which, :], ACT.Ln, bias=eps[:, 0:1],
                           scale=1.0 / 64).then_inc(F["logged"], 1)
            act.wait_ge(F["logged"], 2 * p + which + 1)
            act.activation(sq[:, 2 + which, :], sq[:, 2 + which, :], ACT.Exp, scale=-0.5)\
               .then_inc(F["rooted"], 1)

        def exps(p, st, hh):
            for i in range(TB):
                row = 4 * hh + i
                act.wait_ge(F["masked"], 8 * p + row + 1)
                x = f_probs(2 if hh else st, i)
                act.activation(x, x, ACT.Exp, scale=-1.0, bias=nmax[:, row:row + 1],
                               accum_out=rsum[:, row:row + 1]).then_inc(F["exped"], 1)

        def copy_pt(p, blocks):
            for i in blocks:
                act.wait_ge(F["turned"], TB * p + i + 1)
                wait_past(act, F["pv_done"], p)
                act.activation(f_pt[:, 0:i + 1, i * P:(i + 1) * P],
                               ps[:, T_BANK + i % 2, 0:(i + 1) * P].rearrange("p (a b) -> p a b", a=i + 1),
                               ACT.Copy).then_inc(F["pt_copied"], 1)

        def place_values(p):
            act.wait_ge(F["v_staged"], clip(p + 1, NHD))
            wait_past(act, F["pv_done"], p)
            stand_alone(act.activation(f_v[:, :], at_tile(f_vo, p), ACT.Copy)).then_inc(F["v_placed"], 1)

        def output(p):
            act.wait_ge(F["pv_done"], p + 1)
            act.wait_ge(F["v_placed"], p + 1)
            stand_alone(act.activation(at_tile(f_vo, p), ps[:, O_BANK, :], ACT.Copy)).then_inc(F["o_taken"], 1)
            act.wait_ge(F["sums_made"], clip(2 * p + 5, 2 * NHD))
            wait_past(act, H["summed"], p)
            act.activation(sq[:, 0, :], ps[:, O_BANK, :], ACT.Square).then_inc(H["squared"], 1)

        def head_root(p):
            act.wait_ge(H["summed"], p + 1)
            act.wait_ge(F["q_staged"], clip(p + 3, NHD))
            wait_past(act, H["scaled"], p)
            act.activation(sq[:, 2, :], ps[:, O_BANK, :], ACT.Ln, bias=eps[:, 0:1], scale=1.0 / P)\
               .then_inc(H["logged"], 1)
            act.wait_ge(H["logged"], p + 1)
            act.activation(sq[:, 2, :], sq[:, 2, :], ACT.Exp, scale=-0.5).then_inc(H["rooted"], 1)

        def step(p, st, turn, nx, prev):
            exps(p, st, 0)
            if past_two(p):
                head_root(p - 2)
            exps(p, st, 1)
            if nx:
                square(nx[0], 0)
            if prev:
                place_values(prev[0])
                copy_pt(prev[0], range(TB))
            if nx:
                square(nx[0], 1)
                root(nx[0], 0)
                root(nx[0], 1)
            if prev:
                output(prev[0])

        def rounded(t):
            act.wait_ge(w_used, st_diff.base + NHD)
            act.wait_ge(H["scaled"], t + 1)
            act.activation(xh[:, t, :], f_vo[:, t, :], ACT.Copy).then_inc(H["rounded"], 1)

        def tail(p, st):
            place_values(p)
            for t in range(0, 3):
                rounded(t)
            head_root(p - 1)
            copy_pt(p, (0, 1))
            for t in range(3, 5):
                rounded(t)
            copy_pt(p, (2, 3))
            rounded(5)
            rounded(6)
            output(p)
            head_root(p)
            rounded(7)

        def project(p, st, turn):
            for which in range(2):
                square(p, which)
            for which in range(2):
                root(p, which)

        for n in range(4):
            diff_values_act(act, n)
        attention_steps(act, NHD, project, step, tail)

    def diff_dve(dve):
        def raw(p, which):
            if which == 0:
                dve.wait_ge(F["q_made"], p + 1)
            else:
                dve.wait_ge(w_used, st_diff.base + p + 1)
            wait_past(dve, F["k_staged" if which else "q_staged"], p)
            wait_past(dve, F["squared"], 2 * p - 1 + which)
            dve.tensor_copy(f_raw[:, which, :], ps[:, which, :]).then_inc(F["raw_staged"], 1)

        def normed(p, st, which):
            to, g, nm = ((FQ[st], "q", "q_staged"), (FK[st], "k", "k_staged"))[which]
            dve.wait_ge(F["rooted"], 2 * p + which + 1)
            dve.scalar_tensor_tensor(out=to[:, :], in0=f_raw[:, which, :],
                                     scalar=gains[:, GAINS[g]:GAINS[g] + 1],
                                     in1=sq[:, 2 + which, :], op0=ALU.mult, op1=ALU.mult)\
               .then_inc(F[nm], 1)

        def mask(p, st, hh):
            for i in range(TB):
                u = 8 * p + 4 * hh + i
                row = 4 * hh + i
                dve.wait_ge(F["scored"], u + 1)
                if hh == 0:
                    wait_past(dve, F["turned"], TB * (p - 2) + i + 1)
                else:
                    wait_past(dve, F["normed"], TB * p)
                wait_past(dve, F["exped"], 8 * p + 4 * hh - 4)
                stand_alone(dve.tensor_tensor_reduce(
                    f_probs(2 if hh else st, i), ps[:, S_BANK[hh][i], 0:(i + 1) * P],
                    f_causal[:, TOK - (i + 1) * P:TOK], -0.125, 3e38, ALU.add, ALU.min,
                    nmax[:, row:row + 1])).then_inc(F["masked"], 1)

        def norm(p, st):
            dve.wait_ge(F["exped"], 8 * p + 8)
            dve.reciprocal(rinv[:, 0:8], rsum[:, 0:8]).then_inc(F["inverted"], 1)
            dve.wait_ge(F["inverted"], 2 * p + 1)
            dve.tensor_scalar(lamr, rinv[:, 4:8], lam[:, 7:8], None, ALU.mult).then_inc(F["inverted"], 1)
            for i in range(TB):
                dve.tensor_scalar(f_probs(st, i), f_probs(st, i), rinv[:, i:i + 1], None,
                                  ALU.mult).then_inc(F["p_scaled"], 1)
            dve.wait_ge(F["inverted"], 2 * p + 2)
            for i in range(TB):
                dve.wait_ge(F["p_scaled"], TB * p + i + 1)
                dve.scalar_tensor_tensor(out=f_probs(st, i), in0=f_probs(2, i), scalar=lamr[:, i:i + 1],
                                         in1=f_probs(st, i), op0=ALU.mult, op1=ALU.add)\
                   .then_inc(F["normed"], 1)

        def head_scale(p):
            dve.wait_ge(H["rooted"], p + 1)
            dve.wait_ge(H["squared"], p + 1)
            dve.scalar_tensor_tensor(out=at_tile(f_vo, p), in0=at_tile(f_vo, p), scalar=lam[:, 5:6],
                                     in1=sq[:, 2, :], op0=ALU.mult, op1=ALU.mult).then_inc(H["scaled"], 1)

        def step(p, st, turn, nx, prev):
            mask(p, st, 0)
            mask(p, st, 1)
            if nx:
                raw(nx[0], 0)
            if past_two(p):
                head_scale(p - 2)
            norm(p, st)
            if nx:
                raw(nx[0], 1)
                normed(nx[0], nx[1], 0)
                normed(nx[0], nx[1], 1)

        def split(t):
            dve.wait_ge(H["rounded"], t + 1)
            dve.tensor_tensor(xl[:, t, :], f_vo[:, t, :], xh[:, t, :].bitcast(F32), ALU.subtract)\
               .then_inc(H["split"], 1)

        def tail(p, st):
            for t in range(0, 3):
                split(t)
            head_scale(p - 1)
            for t in range(3, 7):
                split(t)
            head_scale(p)
            split(7)

        def project(p, st, turn):
            for which in range(2):
                raw(p, which)
            for which in range(2):
                normed(p, st, which)

        dve.wait_ge(L["loaded"], 32)
        wait_for(dve, n_b.s["split"], 2 * KD)
        attention_steps(dve, NHD, project, step, tail)

    def norm_of(*outs, after=None):
        return Norm(KD, hsrc, [(hi, lo, GAINS[g]) for hi, lo, g in outs], after)

    def halves(stages, ready, swiglu, kt):
        ups, downs = [], []
        for up, down in stages:
            ups.append(Up(up, ready, swiglu, prev=downs[-1] if downs else None))
            downs.append(Resid(down, kt, 1, (hidh, hidl), ups[-1].s["split"], prev=ups[-1]))
        return ups, downs

    n_ffn, n_mlp, u_ffn, r_ffn, u_mlp, r_mlp = [], [], [], [], [], []

    def add_ffn(layer, after):
        n_ffn.append(norm_of((xh, xl, f"ffn{layer}"), after=after))
        ups, downs = halves(st_ffn[2 * layer:2 * layer + 2], n_ffn[-1].s["split"], True, KF)
        u_ffn.extend(ups)
        r_ffn.extend(downs)

    def add_mlp(layer, after):
        n_mlp.append(norm_of((xh, xl, f"mlp{layer}"), after=after))
        ups, downs = halves(st_mlp[2 * layer:2 * layer + 2], n_mlp[-1].s["split"], False, KH)
        u_mlp.extend(ups)
        r_mlp.extend(downs)

    n_attn0 = norm_of((xh, xl, "attn0"))
    n_attn0.pieces = x_loaded
    n_cq = Norm(2, lambda t: lraw[:, t, :], [(e_cqh, e_cql, GAINS["e_q"])])
    n_ck = Norm(1, lambda t: lraw[:, 2 + t, :], [(e_ckh, e_ckl, GAINS["e_kv"])])
    r_eout = Resid(st_eout, KD, 2, (oh, ol), a_dil.s["o_taken"], before=4)
    add_ffn(0, r_eout)
    n_attn1 = norm_of((xh, xl, "attn1"), after=r_ffn[1])
    r_oout = Resid(st_oout, KD, 2, (oh, ol), a_swa.s["o_taken"])
    add_ffn(1, r_oout)
    n_fin = norm_of(after=r_ffn[3])
    n_a = norm_of((xh, xl, "a"))
    n_a.made = n_fin.s["scaled"]
    r_aout = Resid(st_aout, KD, 2, (oh, ol), G["split"])
    add_mlp(0, r_aout)
    n_b = norm_of((f_kh, f_kl, "kv"), (xh, xl, "b"), after=r_mlp[1])
    r_bout = Resid(st_bout, KD, 2, (xh, xl), H["split"])
    add_mlp(1, r_bout)

    CONSTS = 6

    @block.sync
    def _(sp):
        x_t = dram["x_t"].rearrange("p (a b) -> p a b", a=KD)
        for j in range(4):
            sp.dma_start(h[:, 2 * j:2 * j + 2, :], x_t[:, 2 * j:2 * j + 2, :]).then_inc(x_loaded[j], 16)
        sp.dma_start(gains[:, :], dram["gains"]).then_inc(const_loaded, 16)
        sp.dma_start(ident[:, :], dram["ident"]).then_inc(const_loaded, 16)
        sp.dma_start(blockones[:, :], dram["blockones"]).then_inc(const_loaded, 16)
        sp.dma_start(e_causal[:, :], dram["tab_causal"]).then_inc(const_loaded, 16)
        sp.dma_start(e_ropeq[:, :], dram["rope_q"]).then_inc(const_loaded, 16)

        def load(entry, i, c, slot, uses, n):
            array, elems, first, step = entry
            wait_past(sp, w_split, c - 1)
            sp.dma_start(raw[slot][:, 0:elems], array[first + step * i]).then_inc(w_loaded[slot], 16)
        for st in ORDER:
            each_chunk(sp, st, load)
        wait_for(sp, r_mlp[3].added, KD)
        sp.dma_start(dram["out_t"].rearrange("p (a b) -> p a b", a=KD), h[:, :, :]).then_inc(out_stored, 16)
        sp.wait_ge(out_stored, 16)

    @block.gpsimd
    def _(pool):
        def split(entry, i, c, slot, uses, n):
            elems = entry[1]
            pool.wait_ge(w_loaded[slot], 16 * uses)
            wait_past(pool, w_used, c - 1)
            stand_alone(pool.tensor_scalar(wh[slot][:, 0:elems], raw[slot][:, 0:elems], 1.0, 1.0,
                                           ALU.mult, ALU.mult))\
                .then_inc(w_rounded, 1)
            pool.wait_ge(w_rounded, c + 1)
            pool.tensor_tensor(wl[slot][:, 0:elems], raw[slot][:, 0:elems],
                               wh[slot][:, 0:elems].bitcast(F32), ALU.subtract).then_inc(w_split, 1)
        for st in ORDER:
            each_chunk(pool, st, split)

    @block.tensor
    def _(pe):
        pe.wait_ge(consts_made, 2)
        norm_pe(pe, n_attn0)
        pe.wait_ge(const_loaded, 80)
        latents_pe(pe)
        dil_values_pe(pe, 0)
        norm_pe(pe, n_cq)
        dil_values_pe(pe, 1, lambda: norm_pe(pe, n_ck))
        att_pe(pe, a_mla, [(n_cq.s["split"], 2), (n_ck.s["split"], 1), (key_placed, 4)])
        att_pe(pe, a_dil, [], r_eout)
        resid_pe(pe, r_eout, KD - 1)
        for layer in range(2):
            if layer == 1:
                norm_pe(pe, n_attn1)
                swa_kv_pe(pe)
                att_pe(pe, a_swa, [(kv_taken, 2)], r_oout)
                resid_pe(pe, r_oout, KD - 1)
            norm_pe(pe, n_ffn[layer])
            for half in range(2):
                up_pe(pe, u_ffn[2 * layer + half])
                resid_pe(pe, r_ffn[2 * layer + half])
        norm_pe(pe, n_fin)
        norm_pe(pe, n_a)
        gla_gate_pe(pe)
        gla_pe(pe)
        resid_pe(pe, r_aout, 6)
        for layer in range(2):
            if layer == 1:
                norm_pe(pe, n_b)
                diff_values_pe(pe)
                diff_pe(pe)
            norm_pe(pe, n_mlp[layer])
            for half in range(2):
                up_pe(pe, u_mlp[2 * layer + half])
                resid_pe(pe, r_mlp[2 * layer + half])

    @block.scalar
    def _(act):
        act.wait_ge(consts_made, 2)
        log_exp(act)
        norm_act(act, n_attn0, [])
        act.wait_ge(const_loaded, 80)
        latents_act(act)
        norm_act(act, n_cq, [(lat["taken"], 3)])
        norm_act(act, n_ck, [])
        for n in range(2):
            dil_values_act(act, n)
        att_act(act, a_mla)
        att_act(act, a_dil)
        for layer in range(2):
            if layer == 1:
                norm_act(act, n_attn1, [])
                swa_kv_act(act)
                att_act(act, a_swa)
            norm_act(act, n_ffn[layer], [])
            for half in range(2):
                up_act(act, u_ffn[2 * layer + half])
            log_exp(act)
        norm_act(act, n_fin, [])
        norm_act(act, n_a, [])
        gla_gate_act(act)
        gla_act(act)
        for layer in range(2):
            if layer == 1:
                norm_act(act, n_b, [])
                lambda_act(act)
                diff_act(act)
            norm_act(act, n_mlp[layer], [])
            for half in range(2):
                up_act(act, u_mlp[2 * layer + half])

    @block.vector
    def _(dve):
        dve.memset(ones[:, :], 1.0).then_inc(consts_made, 1)
        dve.memset(eps[:, :], EPS).then_inc(consts_made, 1)
        dve.wait_ge(const_loaded, 80)
        norm_dve(dve, n_attn0)
        latents_dve(dve)
        norm_dve(dve, n_cq)
        norm_dve(dve, n_ck)
        att_dve(dve, a_mla)
        att_dve(dve, a_dil)
        resid_dve(dve, r_eout)
        for layer in range(2):
            if layer == 1:
                norm_dve(dve, n_attn1)
                att_dve(dve, a_swa)
                resid_dve(dve, r_oout)
            norm_dve(dve, n_ffn[layer])
            for half in range(2):
                up_dve(dve, u_ffn[2 * layer + half])
                resid_dve(dve, r_ffn[2 * layer + half])
        final_dve(dve)
        norm_dve(dve, n_a)
        gla_gate_dve(dve)
        gla_dve(dve)
        resid_dve(dve, r_aout)
        for layer in range(2):
            if layer == 1:
                norm_dve(dve, n_b)
                lambda_dve(dve)
                diff_dve(dve)
                resid_dve(dve, r_bout)
            norm_dve(dve, n_mlp[layer])
            for half in range(2):
                up_dve(dve, u_mlp[2 * layer + half])
                resid_dve(dve, r_mlp[2 * layer + half])


def panels(w, column_lists):
    out = []
    for cols in column_lists:
        part = w[:, cols]
        out.append(part.reshape(part.shape[0] // P, P, -1).transpose(1, 0, 2).reshape(P, -1))
    return np.ascontiguousarray(np.stack(out))


def shape_constants():
    f = np.float32
    pos = np.arange(TOK, dtype=f)
    inv = f(10000.0) ** (-np.arange(0, 32, 2, dtype=f) / f(32))
    ang = (pos[:, None] * inv[None, :]).astype(f)
    cos, sin = np.cos(ang).T.astype(f), np.sin(ang).T.astype(f)
    c32, s32 = np.concatenate([cos, cos]), np.concatenate([-sin, sin])
    rope_q = np.concatenate([np.ones((64, TOK), f), c32, s32])
    pad = np.zeros((64, TOK), f)
    rope_k = np.stack([np.concatenate([pad, c32, c32]), np.concatenate([pad, s32, s32])])
    q = np.arange(P)[:, None]
    off = q + TOK - P - np.arange(TOK)[None, :]
    causal = np.where(off >= 0, 0.0, MASKED).astype(f)
    count = (off <= 128).astype(int) + (off % 4 == 0) + (off % 16 == 0)
    logs = np.where((off >= 0) & (count > 0), np.log(np.maximum(count, 1)), 0.0)
    valid = (off >= 0) & (count > 0)
    dil = []
    for hd in range(8):
        slope = 2.0 ** (-(hd + 1))
        dil.append(np.where(valid, (logs - slope * off) * 8.0, MASKED))
    dil = np.stack(dil).reshape(4, 2, P, TOK).transpose(0, 2, 1, 3).reshape(4, P, 2 * TOK).astype(f)
    dist = q + P - np.arange(2 * P)[None, :]
    ok = (dist >= 0) & (dist < 128)
    swa = []
    for pair in range(8):
        for hd in (pair, pair + 8):
            swa.append(np.where(ok, -(2.0 ** (-8.0 * (hd + 1) / 16)) * dist * 8.0, MASKED))
    swa = np.stack(swa).reshape(8, 2, P, 2 * P).transpose(0, 2, 1, 3).reshape(8, P, 4 * P).astype(f)
    j, i = np.arange(P)[:, None], np.arange(P)[None, :]
    masks = [(j // (2 * s) == i // (2 * s)) & (j % (2 * s) < s) & (i % (2 * s) >= s) for s in LEVELS]
    masks.append(j == i)
    masks = np.stack(masks, 1).reshape(P, -1).astype(np.uint32)
    reset = np.ones((P, TOK), f)
    reset[:, ::P] = 0.0
    blocks = np.zeros((P, P), f)
    blocks[:64, :64] = 1.0
    blocks[64:, 64:] = 1.0
    return {"rope_q": rope_q, "rope_k": rope_k, "tab_causal": causal, "tab_dil": dil, "tab_swa": swa,
            "level_masks": masks, "scan_reset": reset, "ident": np.eye(P, dtype=f), "blockones": blocks}


def lay_out(v):
    a = {k: np.asarray(x) for k, x in v.items()}
    r = np.arange
    arrays = dict(shape_constants())
    arrays["x_t"] = np.ascontiguousarray(a["x"][0].T.reshape(KD, P, TOK).transpose(1, 0, 2).reshape(P, -1))

    w = a["e_w_in"][0]
    kr = r(384, 416)
    krs = np.concatenate([r(400, 416), r(384, 400)])
    arrays["w_e_in"] = panels(w, [r(256), np.concatenate([r(256, 384), kr, kr, krs, krs])])
    cols = []
    for pr in range(4):
        for hd in (2 * pr, 2 * pr + 1):
            b = hd * 96
            cols.append(np.concatenate([r(b, b + 96), r(b + 80, b + 96), r(b + 64, b + 80)]))
    arrays["w_e_uq"] = panels(a["e_w_uq"][0], [np.concatenate(cols[2 * i:2 * i + 2]) for i in range(4)])
    arrays["w_e_ukv"] = panels(a["e_w_ukv"][0], [r(256 * i, 256 * i + 256) for i in range(4)])
    q0, k0, v0 = 416, 416 + 512, 416 + 1024
    arrays["w_e_qk"] = panels(w, [np.concatenate([r(q0 + P * i, q0 + P * i + P), r(k0 + P * i, k0 + P * i + P)])
                                  for i in range(4)])
    arrays["w_e_v"] = panels(w, [r(v0 + 256 * i, v0 + 256 * i + 256) for i in range(2)])

    def wide(m):
        return panels(m, [r(256 * i, 256 * i + 256) for i in range(m.shape[1] // 256)])
    arrays["w_e_out"] = wide(a["e_w_out"][0])
    gu, dn = [], []
    for layer in range(2):
        for half in range(2):
            s = half * HALF_FF
            gu.append(panels(a["f_w_gate_up"][layer],
                             [np.concatenate([r(s + P * i, s + P * i + P), r(FF + s + P * i, FF + s + P * i + P)])
                              for i in range(KF)]))
            dn.append(panels(a["f_w_down"][layer][s:s + HALF_FF], [r(P * i, P * i + P) for i in range(KD)]))
    arrays["w_f_gu"], arrays["w_f_dn"] = np.concatenate(gu), np.concatenate(dn)
    wo = a["o_w_qkv"][0]
    arrays["w_o_kv"] = panels(wo, [r(1024, 1280)])
    pair_cols = [np.concatenate([r(64 * i, 64 * i + 64), r(64 * (i + 8), 64 * (i + 8) + 64)]) for i in range(8)]
    arrays["w_o_q"] = panels(wo, pair_cols)
    arrays["w_o_out"] = wide(a["o_w_out"][0][np.concatenate(pair_cols)])
    wa = a["a_w_in_2"][0]
    z = np.zeros((D, P), np.float32)
    z[:, 0:16] = wa[:, 3072:3088]
    arrays["w_a_z"] = panels(z, [r(P)])
    arrays["w_a_qk"] = panels(wa, [np.concatenate([r(P * i, P * i + P), r(512 + P * i, 512 + P * i + P)])
                                   for i in range(4)])
    arrays["w_a_v"] = panels(wa, [r(1024 + 256 * i, 1280 + 256 * i) for i in range(4)])
    arrays["w_a_g"] = panels(wa, [r(2048 + P * i, 2048 + P * i + P) for i in range(8)])
    arrays["a_gate_up"] = np.ascontiguousarray(a["a_w_gate_up_2"][0])
    arrays["w_a_out"] = wide(a["a_w_out_2"][0])
    up, dn = [], []
    for layer in range(2):
        for half in range(2):
            s = half * HALF_HID
            up.append(wide(a["mlp_w1_2"][layer][:, s:s + HALF_HID]))
            dn.append(panels(a["mlp_w2_2"][layer][s:s + HALF_HID], [r(P * i, P * i + P) for i in range(KD)]))
    arrays["w_m_up"], arrays["w_m_dn"] = np.concatenate(up), np.concatenate(dn)
    both = np.concatenate([a["b_w_q_2"][0], a["w_kv_2"]], axis=1)
    arrays["w_b_qk"] = panels(both, [np.concatenate([r(P * i, P * i + P), r(1024 + P * i, 1024 + P * i + P)])
                                     for i in range(8)])
    arrays["w_b_v"] = panels(both, [r(2048 + 256 * i, 2304 + 256 * i) for i in range(4)])
    arrays["w_b_out"] = wide(a["b_w_out_2"][0])

    def tiles(vec):
        return vec.reshape(-1, P).T

    def twice(vec):
        return np.concatenate([vec, vec])[:, None]
    sinks = a["o_sinks"][0][np.stack([r(8), r(8) + 8], 1).reshape(-1)]
    parts = {
        "attn0": tiles(a["attn_norm"][0]), "attn1": tiles(a["attn_norm"][1]),
        "ffn0": tiles(a["ffn_norm"][0]), "ffn1": tiles(a["ffn_norm"][1]), "final": tiles(a["final_norm"]),
        "e_q": tiles(a["e_q_norm"][0]), "e_kv": tiles(a["e_kv_norm"][0]), "a": tiles(a["a_norm_2"][0]),
        "a_head": tiles(a["a_head_norm_2"][0]), "kv": tiles(a["kv_norm_2"]), "k": twice(a["k_norm_2"]),
        "b": tiles(a["b_norm_2"][0]), "q": twice(a["b_q_norm_2"][0]), "b_head": tiles(a["b_head_norm_2"][0]),
        "mlp0": tiles(a["mlp_norm_2"][0]), "mlp1": tiles(a["mlp_norm_2"][1]), "b_gate": tiles(a["a_b_gate_2"][0]),
        "sinks": np.broadcast_to(sinks[None, :], (P, 16)),
    }
    arrays["gains"] = np.ascontiguousarray(np.concatenate([parts[n] for n in GAINS], axis=1))
    arrays["lambda_rows"] = np.ascontiguousarray(np.broadcast_to(a["b_lambda_2"][0].reshape(1, -1), (P, 256)))
    return arrays


def kernel(**inputs):
    import concourse.bacc as bacc
    from concourse.bass_utils import run_bass_kernel_spmd

    arrays = lay_out(inputs)
    nc = bacc.Bacc("TRN2", target_bir_lowering=False, num_devices=1)
    dram = {n: nc.dram_tensor("in_" + n, list(x.shape), mybir.dt.from_np(x.dtype), kind="ExternalInput").ap()
            for n, x in arrays.items()}
    dram["out_t"] = nc.dram_tensor("out_t", [P, KD * TOK], F32, kind="ExternalOutput").ap()
    build(nc, dram)
    got = run_bass_kernel_spmd(nc, [{"in_" + n: x for n, x in arrays.items()}], core_ids=[0]).results[0]["out_t"]
    return np.ascontiguousarray(got.reshape(P, KD, TOK).transpose(1, 0, 2).reshape(D, TOK).T)[None]
```
